# Optimizing a Trainium2 kernel written in Bass

```python
import jax, jax.numpy as jnp
from jax import lax
import numpy as np

D_MODEL = 1024
BATCH = 1
SEQ = 512
DEPTH = 1
DEC_BATCH = 8
DEC_SEQ = 1
PAST_LEN = 2048
PAGE_SIZE = 128

N_BRANCH = 4
BRANCH_WIDTH = D_MODEL // 2
H_A = 4
DV_A = BRANCH_WIDTH // H_A
DK_A = DV_A // 2
GLA_RANK = 16
GLA_TAU = 16.0
H_B = 4
DV_B = BRANCH_WIDTH // H_B
DF_B = D_MODEL // 16
POOL_WIDTH = BRANCH_WIDTH
POOL_WINDOWS = (2, 4, 8, 16)
POOL_GROUP = POOL_WIDTH // len(POOL_WINDOWS)
POOL_HIST = max(POOL_WINDOWS) - 1
H_D = 8
HD_D = BRANCH_WIDTH // H_D
KVH_D = 2
G_D = H_D // KVH_D
CMP_STRIDE = 16
CMP_BLOCK = 2 * CMP_STRIDE
SEL_BLOCK = 4 * CMP_STRIDE
TOPK = 16
WINDOW = 512
Q_BLOCK = 32
FORCE_BONUS = 1000.0
CHUNK = 16
D_FF = 4 * D_MODEL
EPS = 1e-6
NEG = -1e30
IN_SIZES = (H_A * DK_A, H_A * DK_A, H_A * DV_A, H_A * DV_A, GLA_RANK,
            H_B * DF_B, H_B * DF_B, H_B * DV_B, H_B * DV_B,
            POOL_WIDTH,
            H_D * HD_D, KVH_D * HD_D, KVH_D * HD_D, KVH_D * HD_D, KVH_D * HD_D, KVH_D * HD_D, KVH_D * HD_D, H_D * 3)
IN_WIDTH = sum(IN_SIZES)

kernel_name = 'hybrid_gla_hgrn2_pool_nsa_step'

def rms_norm(x, g):
    xf = x.astype(jnp.float32)
    y = xf * lax.rsqrt(jnp.mean(xf * xf, axis=-1, keepdims=True) + EPS)
    return (y * g.astype(jnp.float32)).astype(x.dtype)

def masked_softmax(s, mask):
    p = jax.nn.softmax(jnp.where(mask, s, NEG), axis=-1)
    return jnp.where(mask, p, 0.0)

def split_cols(z):
    offs, c = [], 0
    for s in IN_SIZES[:-1]:
        c += s
        offs.append(c)
    return jnp.split(z, offs, axis=-1)

def chunked_gla(q, k, v, log_f, s0):
    f32 = jnp.float32
    B, L, H, K = q.shape
    pad = (-L) % CHUNK
    n = (L + pad) // CHUNK
    pw = ((0, 0), (0, pad), (0, 0), (0, 0))

    def blocks(a):
        return jnp.pad(a.astype(f32), pw).reshape(B, n, CHUNK, H, a.shape[-1])

    q, k, v, g = blocks(q), blocks(k), blocks(v), blocks(log_f)
    b = jnp.cumsum(g, axis=2)
    causal = jnp.tril(jnp.ones((CHUNK, CHUNK), dtype=bool))[None, None, :, :, None, None]
    decay = jnp.exp(jnp.where(causal, b[:, :, :, None] - b[:, :, None, :], -jnp.inf))
    attn = jnp.einsum('bnthk,bnshk,bntshk->bnhts', q, k, decay)
    o_intra = jnp.einsum('bnhts,bnshv->bnthv', attn, v)
    b_last = b[:, :, -1]
    q_dec = q * jnp.exp(b)
    d_state = jnp.einsum('bnshk,bnshv->bnhkv', k * jnp.exp(b_last[:, :, None] - b), v)

    def step(S, inp):
        qd, ds, bl = inp
        o = jnp.einsum('bthk,bhkv->bthv', qd, S)
        return S * jnp.exp(bl)[..., None] + ds, o

    s_fin, o_inter = lax.scan(step, s0.astype(f32),
                              (jnp.moveaxis(q_dec, 1, 0), jnp.moveaxis(d_state, 1, 0), jnp.moveaxis(b_last, 1, 0)))
    o = o_intra + jnp.moveaxis(o_inter, 0, 1)
    return o.reshape(B, n * CHUNK, H, -1)[:, :L], s_fin

def pool_mixer(u, prev, pos0, w_grp, scale):
    f32 = jnp.float32
    B, L, C = u.shape
    ext = jnp.concatenate([prev.astype(f32), u.astype(f32)], axis=1)
    cs = jnp.pad(jnp.cumsum(ext, axis=1), ((0, 0), (1, 0), (0, 0)))
    n_avail = pos0 + jnp.arange(L) + 1
    means = []
    for gi, w in enumerate(POOL_WINDOWS):
        c0 = gi * POOL_GROUP
        lo = POOL_HIST + 1 - w
        win_sum = cs[:, POOL_HIST + 1:POOL_HIST + 1 + L, c0:c0 + POOL_GROUP] - cs[:, lo:lo + L, c0:c0 + POOL_GROUP]
        means.append(win_sum / jnp.minimum(w, n_avail).astype(f32)[None, :, None])
    d = jnp.stack(means, axis=2) - u.astype(f32).reshape(B, L, len(POOL_WINDOWS), POOL_GROUP)
    y = jnp.einsum('blgc,gcd->blgd', d, w_grp.astype(f32)).reshape(B, L, C) * scale.astype(f32)
    return y, ext[:, ext.shape[1] - POOL_HIST:]

def nsa_attend(q, gates, kv_cmp, kv_slc, kv_win, pos0, kc_gain):
    f32 = jnp.float32
    B, Lq = q.shape[0], q.shape[1]
    Lk = kv_cmp.shape[1]
    pad = (-Lk) % SEL_BLOCK
    pk = ((0, 0), (0, pad), (0, 0), (0, 0), (0, 0))
    kv_cmp = jnp.pad(kv_cmp.astype(f32), pk)
    kv_slc = jnp.pad(kv_slc.astype(f32), pk)
    lp = Lk + pad
    n16 = lp // CMP_STRIDE
    s16 = kv_cmp.reshape(B, n16, CMP_STRIDE, 2, KVH_D, HD_D).sum(axis=2)
    cmp = (s16[:, :-1] + s16[:, 1:]) / CMP_BLOCK
    kc = rms_norm(cmp[:, :, 0], kc_gain)
    vc = cmp[:, :, 1]
    n_cmp = n16 - 1
    c_end = jnp.arange(n_cmp) * CMP_STRIDE + (CMP_BLOCK - 1)
    n_sel = lp // SEL_BLOCK
    per = SEL_BLOCK // CMP_STRIDE
    ci = jnp.arange(n_cmp)[:, None]
    sj = jnp.arange(n_sel)[None, :]
    overlap = ((ci // per == sj) | ((ci + 1) // per == sj)).astype(f32)
    kb = kv_slc[:, :, 0].reshape(B, n_sel, SEL_BLOCK, KVH_D, HD_D).transpose(0, 3, 1, 2, 4)
    vb = kv_slc[:, :, 1].reshape(B, n_sel, SEL_BLOCK, KVH_D, HD_D).transpose(0, 3, 1, 2, 4)
    k_sel = min(TOPK, n_sel)
    qb_len = Q_BLOCK if Lq % Q_BLOCK == 0 else Lq
    qf = q.astype(f32) * (HD_D ** -0.5)
    gf = gates.astype(f32)
    kvw = kv_win.astype(f32)
    gather = jax.vmap(jax.vmap(lambda blk, ix: blk[ix]))
    blk_ids = jnp.arange(n_sel)[None, :]

    def one_block(i):
        s = i * qb_len
        qb = lax.dynamic_slice_in_dim(qf, s, qb_len, axis=1)
        gb = lax.dynamic_slice_in_dim(gf, s, qb_len, axis=1)
        t = pos0 + s + jnp.arange(qb_len)
        sc = jnp.einsum('bqhgd,bchd->bqhgc', qb, kc)
        pc = masked_softmax(sc, (c_end[None, :] <= t[:, None])[None, :, None, None, :])
        o_cmp = jnp.einsum('bqhgc,bchd->bqhgd', pc, vc)
        imp = jnp.einsum('bqhgc,cn->bqhn', pc, overlap)
        cur = (t // SEL_BLOCK)[:, None]
        forced = (blk_ids == 0) | (blk_ids == cur) | (blk_ids == cur - 1)
        bonus = jnp.where(forced, FORCE_BONUS, 0.0)[None, :, None, :]
        score = jnp.where((blk_ids <= cur)[None, :, None, :], imp + bonus, -jnp.inf)
        _, idx = lax.top_k(score, k_sel)
        idx_h = idx.transpose(0, 2, 1, 3)
        ks = gather(kb, idx_h)
        vs = gather(vb, idx_h)
        ss = jnp.einsum('bqhgd,bhqkpd->bqhgkp', qb, ks)
        kpos = idx[..., None] * SEL_BLOCK + jnp.arange(SEL_BLOCK)
        smask = (kpos <= t[None, :, None, None, None])[:, :, :, None]
        shp = ss.shape
        ps = masked_softmax(ss.reshape(shp[:4] + (-1,)), smask.reshape(smask.shape[:4] + (-1,))).reshape(shp)
        o_slc = jnp.einsum('bqhgkp,bhqkpd->bqhgd', ps, vs)
        wb = lax.dynamic_slice_in_dim(kvw, s, qb_len + WINDOW, axis=1)
        wpos = pos0 - WINDOW + s + jnp.arange(qb_len + WINDOW)
        dist = t[:, None] - wpos[None, :]
        wmask = ((dist >= 0) & (dist <= WINDOW) & (wpos >= 0)[None, :])[None, :, None, None, :]
        sw = jnp.einsum('bqhgd,bkhd->bqhgk', qb, wb[:, :, 0])
        o_win = jnp.einsum('bqhgk,bkhd->bqhgd', masked_softmax(sw, wmask), wb[:, :, 1])
        return gb[..., 0:1] * o_cmp + gb[..., 1:2] * o_slc + gb[..., 2:3] * o_win

    o = lax.map(one_block, jnp.arange(Lq // qb_len))
    return jnp.moveaxis(o, 0, 1).reshape(B, Lq, H_D * HD_D)

def trunk_layer(x, pos0, gla_s0, hgrn_s0, pool_prev, cmp_past, slc_past, win_prior, lw):
    (n1, w_in, gla_wa2, gla_ba, gla_ng, lb, hgrn_ng, pool_w, pool_sc, q_ng, k_ng,
     w_branch, w_gate, b_gate, w_out, n2, w1, w2) = lw
    f32 = jnp.float32
    dt = x.dtype
    B, L = x.shape[0], x.shape[1]
    heads = lambda a, n: a.reshape(B, L, n, -1)
    h = rms_norm(x, n1)
    z = jnp.einsum('bld,de->ble', h, w_in)
    (gq, gk, gv, gr, ga, hq, hf, hi, hg, pu, nq, ck, cv, sk, sv, wk, wv, ng) = split_cols(z)
    log_a = jax.nn.log_sigmoid(jnp.einsum('blr,re->ble', ga, gla_wa2).astype(f32) + gla_ba.astype(f32)) / GLA_TAU
    o, gla_state = chunked_gla(heads(gq, H_A) * (DK_A ** -0.5), heads(gk, H_A), heads(gv, H_A), heads(log_a, H_A), gla_s0)
    o_gla = (rms_norm(o, gla_ng) * jax.nn.silu(heads(gr, H_A).astype(f32))).reshape(B, L, -1)
    fgate = lb + (1.0 - lb) * jax.nn.sigmoid(hf.astype(f32))
    o, hgrn_state = chunked_gla(heads(jax.nn.silu(hq.astype(f32)), H_B) * (DF_B ** -0.5), heads(1.0 - fgate, H_B),
                                heads(hi, H_B), heads(jnp.log(fgate), H_B), hgrn_s0)
    o_hgrn = (rms_norm(o, hgrn_ng) * jax.nn.silu(heads(hg, H_B).astype(f32))).reshape(B, L, -1)
    o_pool, pool_state = pool_mixer(pu, pool_prev, pos0, pool_w, pool_sc)
    q = rms_norm(heads(nq, H_D), q_ng).reshape(B, L, KVH_D, G_D, HD_D)
    kv_cmp_new = jnp.stack([heads(ck, KVH_D), heads(cv, KVH_D)], axis=2)
    kv_slc_new = jnp.stack([rms_norm(heads(sk, KVH_D), k_ng[1]), heads(sv, KVH_D)], axis=2)
    kv_win_new = jnp.stack([rms_norm(heads(wk, KVH_D), k_ng[2]), heads(wv, KVH_D)], axis=2)
    nsa_gates = jax.nn.sigmoid(ng.astype(f32)).reshape(B, L, KVH_D, G_D, 3)
    pad_w = WINDOW - win_prior.shape[1]
    win_all = jnp.concatenate([jnp.pad(win_prior.astype(dt), ((0, 0), (pad_w, 0), (0, 0), (0, 0), (0, 0))), kv_win_new], axis=1)
    o_nsa = nsa_attend(q, nsa_gates,
                       jnp.concatenate([cmp_past.astype(dt), kv_cmp_new], axis=1),
                       jnp.concatenate([slc_past.astype(dt), kv_slc_new], axis=1),
                       win_all, pos0, k_ng[0])
    branches = jnp.stack([o_gla, o_hgrn, o_pool, o_nsa], axis=2).astype(dt)
    proj = jnp.einsum('blnc,ncd->blnd', branches, w_branch)
    gate = jax.nn.sigmoid(jnp.einsum('bld,de->ble', h, w_gate) + b_gate).reshape(B, L, N_BRANCH, -1)
    x = x + jnp.einsum('bld,de->ble', jnp.sum(gate * proj, axis=2), w_out)
    u = jax.nn.relu(jnp.einsum('bld,df->blf', rms_norm(x, n2), w1))
    x = x + jnp.einsum('blf,fd->bld', u * u, w2)
    return x, gla_state, hgrn_state, pool_state.astype(dt), kv_cmp_new, kv_slc_new, kv_win_new

def setup_inputs(seed: int = 0) -> dict:
    key = jax.random.key(seed)
    ks = jax.random.split(key, 32)
    f32 = jnp.float32
    n_pages = PAST_LEN // PAGE_SIZE
    n_phys = (DEC_BATCH * n_pages * 5) // 4
    win_buf = min(WINDOW, PAST_LEN)
    kv_row = (2, KVH_D, HD_D)

    def nrm(i, shape, scale=1.0):
        return jax.random.normal(ks[i], shape, f32) * scale

    def gain(i, shape):
        return 1.0 + nrm(i, shape, 0.02)

    page_table = jax.random.permutation(ks[9], n_phys)[:DEC_BATCH * n_pages].reshape(DEC_BATCH, n_pages).astype(jnp.int32)
    return {
        'x_prompt': nrm(0, (BATCH, SEQ, D_MODEL)),
        'x_sample': nrm(1, (DEC_BATCH, DEC_SEQ, D_MODEL)),
        'state_gla': nrm(2, (DEPTH, DEC_BATCH, H_A, DK_A, DV_A)),
        'state_hgrn': nrm(3, (DEPTH, DEC_BATCH, H_B, DF_B, DV_B)),
        'state_pool': nrm(4, (DEPTH, DEC_BATCH, POOL_HIST, POOL_WIDTH)),
        'cache_cmp_kv': nrm(5, (DEPTH, n_phys, PAGE_SIZE) + kv_row),
        'cache_slc_kv': nrm(6, (DEPTH, n_phys, PAGE_SIZE) + kv_row),
        'cache_win_kv': nrm(7, (DEPTH, DEC_BATCH, win_buf) + kv_row),
        'page_table': page_table,
        'norm1_g': gain(10, (DEPTH, D_MODEL)),
        'w_in': nrm(11, (DEPTH, D_MODEL, IN_WIDTH), D_MODEL ** -0.5),
        'gla_wa2': nrm(12, (DEPTH, GLA_RANK, H_A * DK_A), GLA_RANK ** -0.5),
        'gla_ba': nrm(13, (DEPTH, H_A * DK_A), 0.1),
        'gla_norm_g': gain(14, (DEPTH, DV_A)),
        'hgrn_lb_param': nrm(15, (DEPTH, H_B * DF_B), 0.1),
        'hgrn_norm_g': gain(16, (DEPTH, DV_B)),
        'pool_w': nrm(17, (DEPTH, len(POOL_WINDOWS), POOL_GROUP, POOL_GROUP), POOL_GROUP ** -0.5),
        'pool_scale': gain(18, (DEPTH, POOL_WIDTH)),
        'nsa_q_norm_g': gain(19, (DEPTH, HD_D)),
        'nsa_k_norm_g': gain(20, (DEPTH, 3, HD_D)),
        'w_branch': nrm(21, (DEPTH, N_BRANCH, BRANCH_WIDTH, D_MODEL), BRANCH_WIDTH ** -0.5),
        'w_gate': nrm(22, (DEPTH, D_MODEL, N_BRANCH * D_MODEL), D_MODEL ** -0.5),
        'b_gate': nrm(23, (DEPTH, N_BRANCH * D_MODEL), 0.02),
        'w_out': nrm(24, (DEPTH, D_MODEL, D_MODEL), D_MODEL ** -0.5),
        'norm2_g': gain(25, (DEPTH, D_MODEL)),
        'mlp_w1': nrm(26, (DEPTH, D_MODEL, D_FF), D_MODEL ** -0.5),
        'mlp_w2': nrm(27, (DEPTH, D_FF, D_MODEL), D_FF ** -0.5),
    }

def reference(x_prompt, x_sample, state_gla, state_hgrn, state_pool, cache_cmp_kv, cache_slc_kv, cache_win_kv,
              page_table, norm1_g, w_in, gla_wa2, gla_ba, gla_norm_g, hgrn_lb_param, hgrn_norm_g, pool_w,
              pool_scale, nsa_q_norm_g, nsa_k_norm_g, w_branch, w_gate, b_gate, w_out, norm2_g, mlp_w1, mlp_w2):
    f32 = jnp.float32
    B, L = x_prompt.shape[0], x_prompt.shape[1]
    Bd = x_sample.shape[0]
    dt = x_prompt.dtype
    lb_soft = jax.nn.softmax(hgrn_lb_param.astype(f32), axis=0)
    lb_all = jnp.cumsum(lb_soft, axis=0) - lb_soft[0]
    keep_p = min(WINDOW, L)
    xp, xs = x_prompt, x_sample
    gla_p, gla_s, hgrn_p, hgrn_s, pool_p, pool_s = [], [], [], [], [], []
    cmp_p, cmp_s, slc_p, slc_s, win_p, win_s = [], [], [], [], [], []
    for l in range(DEPTH):
        lw = (norm1_g[l], w_in[l], gla_wa2[l], gla_ba[l], gla_norm_g[l], lb_all[l], hgrn_norm_g[l], pool_w[l],
              pool_scale[l], nsa_q_norm_g[l], nsa_k_norm_g[l], w_branch[l], w_gate[l], b_gate[l], w_out[l],
              norm2_g[l], mlp_w1[l], mlp_w2[l])
        xp, g_p, h_p, p_p, c_p, s_p, w_p = trunk_layer(
            xp, 0, jnp.zeros((B, H_A, DK_A, DV_A), f32), jnp.zeros((B, H_B, DF_B, DV_B), f32),
            jnp.zeros((B, POOL_HIST, POOL_WIDTH), dt), jnp.zeros((B, 0, 2, KVH_D, HD_D), dt),
            jnp.zeros((B, 0, 2, KVH_D, HD_D), dt), jnp.zeros((B, WINDOW, 2, KVH_D, HD_D), dt), lw)
        cmp_past = cache_cmp_kv[l][page_table].reshape(Bd, -1, 2, KVH_D, HD_D)
        slc_past = cache_slc_kv[l][page_table].reshape(Bd, -1, 2, KVH_D, HD_D)
        xs, g_s, h_s, p_s, c_s, s_s, w_s = trunk_layer(
            xs, PAST_LEN, state_gla[l], state_hgrn[l], state_pool[l], cmp_past, slc_past, cache_win_kv[l], lw)
        gla_p.append(g_p); gla_s.append(g_s); hgrn_p.append(h_p); hgrn_s.append(h_s)
        pool_p.append(p_p); pool_s.append(p_s); cmp_p.append(c_p); cmp_s.append(c_s)
        slc_p.append(s_p); slc_s.append(s_s); win_p.append(w_p[:, L - keep_p:]); win_s.append(w_s)
    return (xp, xs,
            jnp.stack(gla_p), jnp.stack(gla_s), jnp.stack(hgrn_p), jnp.stack(hgrn_s),
            jnp.stack(pool_p), jnp.stack(pool_s), jnp.stack(cmp_p), jnp.stack(cmp_s),
            jnp.stack(slc_p), jnp.stack(slc_s), jnp.stack(win_p), jnp.stack(win_s))


_drawn_inputs = setup_inputs


def setup_inputs(seed=0):
    import zlib

    import numpy as np

    out = dict(_drawn_inputs(seed))
    spreads = {}
    factors = {'cache_cmp_kv': 3.844,
     'cache_slc_kv': 3.599,
     'cache_win_kv': 3.201,
     'gla_norm_g': 8.0,
     'hgrn_norm_g': 8.0,
     'pool_scale': 7.022,
     'nsa_q_norm_g': 8.0,
     'nsa_k_norm_g': 3.746,
     'b_gate': 8.0,
     'norm2_g': 3.384}
    for name, (base, spread) in spreads.items():
        noise = np.random.default_rng([zlib.crc32(name.encode()), seed]).standard_normal(out[name].shape)
        drawn = base * np.exp(spread * noise) if base else spread * noise
        out[name] = __import__('jax').numpy.asarray(drawn.astype(out[name].dtype))
    for name, factor in factors.items():
        out[name] = (out[name] * factor).astype(out[name].dtype)
    return out
```

```python
import concourse.bass as bass
from concourse import mybir
from contextlib import ExitStack
import numpy as np

D, L, NS, T = 1024, 512, 8, 520
HALF = T // 2
KT = D // 128
TT = 4
FM, TM, GA = 2560, 2328, 16
HKV, HD, G = 2, 64, 4
PAGES, PAGE = 16, 128
NCMP, NSEL, TOPK = 127, 33, 16
NEG = -1e30
EPS = 1e-6
LEVELS = 7
WINDOWS = (2, 4, 8, 16)
HIST = 15

CV, CQ, CK, CS, CW, CG = 0, 1024, 1536, 1792, 2048, 2304
ZG, ZU, ZQ, ZK = 0, 8, 12, 16


def constants():
    p = np.arange(128)
    parts = {}

    def put(name, a):
        full = np.zeros((128, a.shape[1]), np.float32)
        full[:a.shape[0]] = a
        parts[name] = full

    put("ident", np.eye(128))
    put("ones", np.ones((128, 128)))
    put("causal", np.where(p[None, :] <= p[:, None], 0.0, NEG))
    masks = []
    for lev in range(LEVELS):
        half = 1 << lev
        same = (p[:, None] // (2 * half)) == (p[None, :] // (2 * half))
        masks.append(same & (p[:, None] % (2 * half) < half) & (p[None, :] % (2 * half) >= half))
    masks.append(np.eye(128, dtype=bool))
    put("masks", np.concatenate(masks, 1).astype(np.float32))
    tok = np.arange(L)[:, None]
    c32 = np.arange(32)[None, :]
    pm = ((tok >= 16 * c32) & (tok < 16 * c32 + 32) & (c32 < 31)) / 32.0
    put("pool", pm.reshape(TT, 128, 32).transpose(1, 0, 2).reshape(128, TT * 32))
    c = np.arange(128)[None, :]
    put("shift", np.where((p[:, None] == c) | (p[:, None] == c + 1), 1 / 32.0, 0.0))
    n = np.arange(NSEL)[None, :]
    put("overlap", ((p[:NCMP, None] // 4 == n) | ((p[:NCMP, None] + 1) // 4 == n)).astype(np.float32))
    put("expand", (np.arange(NSEL)[:, None] == p[None, :] // 4).astype(np.float32))
    seen = ((16 * c32 + 31 <= tok) & (c32 < 31)).astype(np.float32)
    seen = seen.reshape(TT, 128, 32).transpose(1, 0, 2).reshape(128, TT * 32)
    put("cmp01", seen)
    put("cmpneg", np.where(seen > 0, 0.0, NEG))
    t16 = np.arange(16)
    put("corr", np.tile(np.concatenate([w / np.minimum(w, t16 + 1.0) for w in WINDOWS]), (128, 1)))
    put("newmask", np.where(np.arange(NS)[:, None] == np.arange(64)[None, :] // 8, 0.0, NEG))
    put("onehot", np.repeat(np.eye(NS), 64, 1))
    bonus = np.zeros((16, NSEL))
    bonus[:, [0, NSEL - 2, NSEL - 1]] = 1000.0
    put("bonus", bonus)
    put("number", np.tile(np.arange(NSEL, dtype=np.float32), (16, 1)))
    put("reset", np.tile((np.arange(L) % 128 != 0).astype(np.float32), (128, 1)))
    off, at = {}, 0
    for k, a in parts.items():
        off[k] = (at, at + a.shape[1])
        at += a.shape[1]
    return np.concatenate(list(parts.values()), 1), off


EVENTS = {
    "pe_event": """la_mm os_mm hist_mm tail_mm ckv_mm kct_mm cxs_mm cxt_mm cxp_mm cxo_mm gb_mm imp_mm sel_mm
           bs_mm""".split(),
    "act_event": """lsp lb_e lf_h decs decc ng rq kst_rs cm_e kst_xr cxe""".split(),
    "dve_event": """eps idx ga_ev q_act lb_d fg lf_g qk kdec qdec tail k_norm q_norm kst ckv kct cm cp q_saved
           gd kst_x cx cxs cxm cxp pct pcg gb rank selt bs nsa_done mix_zero""".split(),
}


SMALL = {}
for _n, _k in (("n1", 8), ("n2", 8), ("bg", 32), ("psc", 4), ("ba", 2), ("lb", 2), ("gn", 1), ("hn", 1),
               ("qg", 64), ("kg", 192), ("r8", 1)):
    SMALL[_n] = (sum(b - a for a, b in SMALL.values()), sum(b - a for a, b in SMALL.values()) + _k)
NSMALL = SMALL["r8"][1]
NCON = constants()[0].shape[1]


def build(nc, A):
    f32, i32 = mybir.dt.float32, mybir.dt.int32
    ACT, ALU, AX = mybir.ActivationFunctionType, mybir.AluOpType, mybir.AxisListType.X
    _, COFF = constants()
    ctx = ExitStack()
    with ctx:
        def sb(name, n, dt=f32):
            return ctx.enter_context(nc.sbuf_tensor(name, [128, n], dt))

        con = sb("con", NCON)
        small = sb("small", NSMALL)
        xT = sb("xT", KT * T)[:].rearrange("p (k t) -> p k t", t=T)
        hT = sb("hT", KT * T)[:].rearrange("p (k t) -> p k t", t=T)
        Z = sb("Z", 20 * T + 5 * TM)
        zf = Z[:, 0:20 * T].rearrange("p (k t) -> p k t", t=T)
        zt = Z[:, 20 * T:].rearrange("p (i c) -> p i c", c=TM)
        R = sb("R", 16704)
        stat = sb("stat", 400)
        eps = stat[:, 396:397]
        idx = sb("idx", 2 * NS, i32)
        gaT = sb("gaT", T)
        wa2 = sb("wa2", 256)
        PS = ctx.enter_context(nc.psum_tensor("PS", [128, 8, 512], f32))
        WA = [R[:, 4096 * s:4096 * (s + 1)] for s in range(2)]
        WB = [R[:, 8192 + 2048 * s:8192 + 2048 * (s + 1)] for s in range(2)]

        def C(name, a=0, b=None, p=128):
            lo, hi = COFF[name]
            return con[0:p, lo + a:(hi if b is None else lo + b)]

        def V(name, a=0, b=None, p=128):
            lo, hi = SMALL[name]
            return small[0:p, lo + a:(hi if b is None else lo + b)]

        ident, ones = C("ident"), C("ones")
        S = {}

        def sem(name):
            if name not in S:
                S[name] = ctx.enter_context(nc.semaphore(name))
            return S[name]

        signalled = {e: 0 for e in EVENTS}

        def once(name):
            e = [e for e in EVENTS if name in EVENTS[e]][0]
            assert EVENTS[e][signalled[e]] == name, name
            signalled[e] += 1
            return sem(e)

        def done(name):
            e = [e for e in EVENTS if name in EVENTS[e]][0]
            return sem(e), EVENTS[e].index(name) + 1

        def steps(eng, name):
            own, n = sem(name), [0]

            def step(ins):
                n[0] += 1
                ins.then_inc(own, 1)
                eng.wait_ge(own, n[0])
            return step

        def pair(bank):
            return PS[:, bank:bank + 2, 0:HALF]

        def halves(ap):
            return ap.rearrange("p (h n) -> p h n", h=2)

        def bc(ap, n):
            return ap.unsqueeze(len(ap.shape)).to_broadcast(list(ap.shape) + [n])


        LF = R[:, 0:4 * T].rearrange("p (k t) -> p k t", t=T)
        KD = R[:, 0:2048].rearrange("p (c k f) -> p c k f", c=4, k=4)
        B = R[:, 2080:4128]
        E0 = R[:, 4160:6208]
        A0 = R[:, 6240:8288]
        A1 = R[:, 12416:14464]
        E1 = R[:, 14464:16512]
        AL, EL = [A0, A1], [E0, E1]
        SIGQ = R[:, 4160:5200].rearrange("p (k t) -> p k t", t=T)
        SIGF = R[:, 5200:6240].rearrange("p (k t) -> p k t", t=T)
        TMPA = R[:, 6240:7280].rearrange("p (k t) -> p k t", t=T)
        SIGG = R[:, 8320:8320 + 8 * T].rearrange("p (k t) -> p k t", t=T)
        SC = R[:, 8320:12416].rearrange("p (g k t) -> p g k t", g=8, k=4)
        ST = R[:, 12416:14464].rearrange("p (c k v) -> p c k v", c=4, k=4)
        OB = R[:, 4160:4160 + 8 * T].rearrange("p (k t) -> p k t", t=T)
        SS = R[:, 8320:12416].rearrange("p (m s k v) -> p m s k v", m=2, s=NS, k=2)
        VB = [R[:, 14464 + 512 * i:14464 + 512 * (i + 1)].rearrange("p (s k v) -> p s k v", s=2, k=2)
              for i in range(2)]
        SQ = [zf[:, ZK + i] for i in range(2)]
        RN = [zf[:, ZK + 2 + i] for i in range(2)]
        decS = stat[:, 0:32].rearrange("p (k s) -> p k s", k=4)
        decC = stat[:, 32:48].rearrange("p (k c) -> p k c", k=4)
        lbv = stat[:, 48:60].rearrange("p (k a) -> p k a", k=2)
        gq8 = stat[:, 60:124]

        def flat(ap):
            return ap.rearrange("p a b -> p (a b)")

        def chunks(buf):
            return buf.rearrange("p (k t) -> p k t", k=4)

        def head_cols(k, par):
            h = (k // 2) * 4 + (k % 2) * 2 + par
            return slice(CV + 128 * h, CV + 128 * (h + 1)), h

        w_in = A["w_in"].rearrange("(k p) n -> p k n", p=128)
        w_gate = A["w_gate"].rearrange("o (k p) n -> p (o k) n", p=128)
        w_branch = A["w_branch"].rearrange("o b (c p) n -> p (o b) c n", p=128)
        w_out = A["w_out"].rearrange("o (k p) n -> p (o k) n", p=128)
        w1 = A["mlp_w1"].rearrange("o (k p) n -> p (o k) n", p=128)
        w2 = A["mlp_w2"].rearrange("o (k p) n -> p (o k) n", p=128)
        mixT = Z[:, 20 * T:28 * T].rearrange("p (k t) -> p k t", t=T)
        uT = Z[:, 0:32 * T].rearrange("p (k t) -> p k t", t=T)
        YT = Z[:, 32 * T:32 * T + 5120].rearrange("p (i d) -> p i d", i=5)
        XI = Z[:, 0:5120].rearrange("p (i d) -> p i d", i=5)


        WP = [R[:, 12416 + 2112 * i:12416 + 2112 * i + 4 * 527].rearrange("p (g t) -> p g t", g=4)
              for i in range(2)]
        poolw = zt[:, 0:4, 0:128]
        hist = zt[0:NS * HIST, 0:4, 128:256]
        tail = zt[0:23, 0:4, 256:384]
        PD = zt[:, 0:4, 504:1024]

        TQ = R[:, 0:2560].rearrange("p (i c) -> p i c", i=5)
        QN = R[:, 2560:5120].rearrange("p (i g k d) -> p i g k d", i=5, g=G, k=HKV)
        TK = R[:, 2560:3840].rearrange("p (i c) -> p i c", i=5)
        QT = R[:, 5120:7200].rearrange("p (g t) -> p g t", t=T)
        KTS, KTW = R[:, 7200:7720], R[:, 7720:8240]
        P = [R[:, 8240 + 512 * i:8752 + 512 * i] for i in range(3)]
        PT = [R[:, 9776 + 512 * i:10288 + 512 * i].rearrange("p (k t) -> p k t", k=4) for i in range(3)]
        PTC = R[:, 8240:9264].rearrange("p (i k t) -> p i k t", i=4, k=2)
        CM = R[:, 11312:12336].rearrange("p (i h c) -> p i h c", i=4, h=8)
        CKV = gaT[0:32, 0:256]
        VBK = zf[:, ZK, 0:512].rearrange("p (k c) -> p k c", k=2)
        ON = zt[:, :, 1024:1536]
        ONT = zf[:, ZQ:ZQ + 4]
        rq = stat[:, 128:188].rearrange("p (i h) -> p i h", i=5)
        kcT = stat[:, 188:220]
        nmc = stat[:, 220:252]
        rsc = stat[:, 252:284].rearrange("p (i h) -> p i h", i=4)
        nm = [stat[:, 284 + i:285 + i] for i in range(3)]
        rs = stat[:, 288:352].rearrange("p (i b h) -> p i b h", i=4, b=2)
        kst = stat[0:32, 352:360]

        X = [R[:, 4096 * i:4096 * (i + 1)] for i in range(4)]
        KTX = zf[:, ZK:ZK + 4].rearrange("p a b -> p (a b)")[:, 0:2048].rearrange("p (i t) -> p i t", i=16)
        KCT = zt[:, 0, 0:8 * NCMP].rearrange("p (s c) -> p s c", s=NS)
        S16 = [zt[:, 0, 1016 + 256 * i:1272 + 256 * i] for i in range(2)]
        CX = [zt[0:NCMP, 1 + u, 0:1024].rearrange("p (s c) -> p s c", s=4) for u in range(2)]
        SX = zt[:, 3, 0:512].rearrange("p (s i h) -> p s i h", s=4, h=8)
        QB = zt[:, 4, 0:64].rearrange("p (s h) -> p s h", h=8)
        KNEW = zt[:, 4, 64:80].rearrange("p (b s) -> p b s", b=2)
        GB = zt[:, 4, 80:272].rearrange("p (b n) -> p b n", b=3)
        OACC = zt[:, 4, 272:336]
        BS = zt[:, 4, 336:352].rearrange("p (s k) -> p s k", k=2)
        PCR = zt[0:64, 4, 352:479]
        PCT = gaT[0:NCMP, 0:64]
        PCG = gaT[0:NCMP, 64:80]
        SN = [gaT[0:NS, 80 + 64 * b:144 + 64 * b] for b in range(2)]
        M1 = gaT[:, 208:240]
        DG = gaT[0:32, 240:272]
        COEF = gaT[:, 272:304]
        GD = gaT[0:NS, 304:496].rearrange("p (b s h) -> p b s h", b=3, h=8)
        SELT = gaT[0:NSEL, 496:512]
        OT = stat[:, 128:192]
        SCO = stat[0:16, 192:225]
        RANK = stat[0:16, 225:258]
        CMAX = stat[0:64, 258:261]
        KST = stat[0:NCMP, 261:277].rearrange("p (s k) -> p s k", k=2)
        SM = stat[0:32, 277:278]
        SQX = zf[:, ZK:ZK + 4].rearrange("p a b -> p (a b)")[0:NCMP, 0:1024]
        T1 = zf[:, ZK:ZK + 4].rearrange("p a b -> p (a b)")[0:16, 0:NSEL * NSEL].rearrange("p (n m) -> p n m", m=NSEL)
        T2 = zt[0:16, 4, 440:440 + NSEL * NSEL].rearrange("p (n m) -> p n m", m=NSEL)
        T3 = zt[0:16, 3, 0:NSEL * NSEL].rearrange("p (n m) -> p n m", m=NSEL)
        ROUNDS = [(0, 0), (0, 4), (1, 0), (1, 4)]

        def xtile(b, s, i):
            if b == 0:
                t = X[s % 4][:, 256 * i:256 * i + 256]
            else:
                t = X[s // 4][:, 1024 * (s % 4) + 256 * i:1024 * (s % 4) + 256 * i + 256]
            return t[:, 0:128], t[:, 128:256]

        SG = [R[:, 12416 + T * i:12416 + T * (i + 1)] for i in range(3)]

        SQN = [R[:, 12288 + T * i:12288 + T * (i + 1)] for i in range(2)]
        RST = R[:, 13328:13328 + T]

        block = ctx.enter_context(nc.Block())
        UNITS = [(i, b, h) for i in range(TT) for b in range(2) for h in range(8)]

        @block.sync
        def _(sp):
            sp.dma_start(con[:], A["tables"]).then_inc(sem("ld_con"), 16)
            sp.dma_start(small[:], A["vectors"]).then_inc(sem("ld_con"), 16)
            for i in range(TT):
                sp.dma_start(XI[:, i], A["x_prompt"][0, 128 * i:128 * (i + 1), :]).then_inc(sem("ld_x"), 16)
            sp.dma_start(XI[0:NS, 4], A["x_sample"].rearrange("s o d -> (s o) d")).then_inc(sem("ld_x"), 16)
            sp.dma_start(wa2[0:GA, :], A["gla_wa2"][0]).then_inc(sem("ld_wa2"), 16)
            sp.dma_start(idx[:, 0:NS], A["pages"]).then_inc(sem("ld_idx"), 16)
            def load_in(n, cols=512):
                sp.dma_start(WA[n % 2][:, 0:KT * cols].rearrange("p (k n) -> p k n", k=KT),
                             w_in[:, :, 512 * n:512 * n + cols]).then_inc(sem(f"wa{n % 2}"), 16)
            load_in(0)
            load_in(1)
            with sp.Fori(1, 3) as i:
                for s in range(2):
                    sp.wait_ge(sem("prod"), i * 8 + 4 * s - 4)
                    sp.dma_start(WA[s].rearrange("p (k n) -> p k n", k=KT),
                                 w_in[:, :, bass.ds(i * 1024 + 512 * s, 512)]).then_inc(sem(f"wa{s}"), 16)
            for n, tiles in ((6, 20), (7, 25), (8, 30), (9, 35)):
                sp.wait_ge(sem("prod"), tiles)
                load_in(n, 512 if n < 9 else 296)
            sp.wait_ge(sem("o_mm"), 8)
            for m, name in enumerate(("state_gla", "state_hgrn")):
                src = A[name].rearrange("o s (k q) f v -> q f (o s) k v", q=2)
                for q in range(2):
                    sp.dma_start(SS[64 * q:64 * q + 64, m], src[q]).then_inc(sem("ld_ss"), 16)
            for g in range(4):
                sp.dma_start(poolw[:, g], A["pool_w"][0, g]).then_inc(sem("ld_pool"), 16)
            sp.dma_start(hist, A["state_pool"].rearrange("o s j (g c) -> (o s j) g c", g=4))\
              .then_inc(sem("ld_pool"), 16)
            sp.dma_start(A["pool_sample"][0, :, 0:HIST - 1], A["state_pool"][0, :, 1:HIST])\
              .then_inc(sem("stored"), 16)
            sp.wait_ge(sem("st"), 4)
            for m, name in enumerate(("gla_prompt", "hgrn_prompt")):
                dst = A[name].rearrange("o b (k q) f v -> q f (o b k) v", q=2)
                for q in range(2):
                    sp.dma_start(dst[q], ST[64 * q:64 * q + 64, 3, 2 * m:2 * m + 2]).then_inc(sem("st_out"), 16)
            sp.wait_ge(sem("ss_done"), 8)
            for m, name in enumerate(("gla_sample", "hgrn_sample")):
                dst = A[name].rearrange("o s (k q) f v -> q f (o s) k v", q=2)
                for q in range(2):
                    sp.dma_start(dst[q], SS[64 * q:64 * q + 64, m]).then_inc(sem("st_out"), 16)
            sp.wait_ge(*done("tail"))
            sp.dma_start(A["pool_prompt"][0, 0].rearrange("j (g c) -> j g c", g=4), tail[0:HIST])\
              .then_inc(sem("stored"), 16)
            sp.dma_start(A["pool_sample"][0, :, HIST - 1].rearrange("s (g c) -> s g c", g=4),
                         tail[HIST:HIST + NS]).then_inc(sem("stored"), 16)
            sp.wait_ge(*done("k_norm"))
            for name, col in (("cmp", CK), ("slc", CS), ("win", CW)):
                sp.dma_start(A[name + "_rows_prompt"].rearrange("o b (i p) a k d -> p (o b i) (a k d)", p=128),
                             zt[:, 0:4, col:col + 256]).then_inc(sem("rows_out"), 16)
                sp.dma_start(A[name + "_rows_sample"].rearrange("o s b a k d -> (o s b) (a k d)"),
                             zt[0:NS, 4, col:col + 256]).then_inc(sem("rows_out"), 16)
            sp.wait_ge(sem("sv_mm"), 2)
            for n in range(2):
                sp.dma_start(X[n].rearrange("p (s c) -> p s c", s=4),
                             A["cache_win_kv"].rearrange("o s (p i) a k d -> p (o s) (i a k d)", i=4)
                             [:, 4 * n:4 * n + 4]).then_inc(sem(f"xw{n}"), 16)
            sp.wait_ge(*done("nsa_done"))
            sp.wait_ge(sem("rows_out"), 96)
            with sp.Fori(0, 2) as hf:
                with sp.Fori(0, 2) as bp:
                    for s in range(2):
                        sp.wait_ge(sem("prod"), hf * 16 + bp * 8 + 4 * s + 42)
                        sp.dma_start(WA[s].rearrange("p (k n) -> p k n", k=KT),
                                     w_gate[:, :, bass.ds(bp * 2048 + hf * 512 + 1024 * s, 512)])\
                          .then_inc(sem(f"wa{s}"), 16)
                        sp.dma_start(WB[s].rearrange("p (c n) -> p c n", c=4),
                                     w_branch[:, bass.ds(bp * 2 + s, 1), :, bass.ds(hf * 512, 512)]
                                     .rearrange("p b c n -> p (b c) n")).then_inc(sem(f"wb{s}"), 16)
            for s in range(2):
                sp.wait_ge(sem("prod"), 74 + 4 * s)
                sp.dma_start(WA[s].rearrange("p (k n) -> p k n", k=KT),
                             w_out[:, :, 512 * s:512 * s + 512]).then_inc(sem(f"wa{s}"), 16)
            with sp.Fori(0, 4) as i:
                for s in range(2):
                    sp.wait_ge(sem("prod"), i * 8 + 4 * s + 82)
                    sp.dma_start(WA[s].rearrange("p (k n) -> p k n", k=KT),
                                 w1[:, :, bass.ds(i * 1024 + 512 * s, 512)]).then_inc(sem(f"wa{s}"), 16)
            with sp.Fori(0, 4) as i:
                for s in range(2):
                    sp.wait_ge(sem("prod"), i * 2 + s + 117)
                    sp.dma_start(WA[s].rearrange("p (k n) -> p k n", k=32),
                                 w2[:, :, bass.ds(i * 256 + 128 * s, 128)]).then_inc(sem(f"wa{s}"), 16)
            for i in range(5):
                sp.wait_ge(sem("y_ev"), 2 * i + 2)
                if i < TT:
                    sp.dma_start(A["y_prompt"][0, 128 * i:128 * i + 128], YT[:, i]).then_inc(sem("stored"), 16)
                else:
                    sp.dma_start(A["y_sample"].rearrange("s o d -> (s o) d"), YT[0:NS, i])\
                      .then_inc(sem("stored"), 16)
            sp.wait_ge(sem("stored"), 16 * 8)
            sp.wait_ge(sem("st_out"), 128)

        @block.tensor
        def _(pe):
            mm, tr = nc.tensor.matmul, nc.tensor.transpose

            def norm_sums(tag):
                for k in range(KT):
                    pe.wait_ge(sem(tag + "_sq"), k + 1)
                    for h in range(2):
                        last = mm(PS[:, h, 0:HALF], ones, SQN[k % 2][:, HALF * h:HALF * h + HALF],
                                  start=(k == 0), stop=(k == KT - 1))
                    last.then_inc(sem(tag + "_mm"), 1)

            def fm_tile(w, j, bank, rhs, k_tiles=KT, width=128):
                for k in range(k_tiles):
                    for h in range(2):
                        last = mm(PS[0:width, bank + h, 0:HALF], w[:, k, 128 * j:128 * j + width],
                                  rhs(k)[:, HALF * h:HALF * h + HALF], start=(k == 0), stop=(k == k_tiles - 1))
                return last

            hk = lambda k: hT[:, k]

            pe.wait_ge(sem("ld_con"), 32)
            pe.wait_ge(sem("ld_x"), 80)
            for n in range(10):
                i, k4, w = n // 2, 4 * (n % 2), (128 if n < 8 else NS)
                if n >= 8:
                    pe.wait_ge(sem("xt_ev"), n - 7)
                for j in range(4):
                    last = tr(PS[:, n % 8, w * j:w * (j + 1)], XI[0:w, i, 128 * (k4 + j):128 * (k4 + j + 1)],
                              ident[0:w, 0:w])
                last.then_inc(sem("xt"), 1)
            pe.wait_ge(sem("xt_ev"), 10)
            norm_sums("n1")

            pe.wait_ge(sem("n1_h"), KT)
            w8 = [w.rearrange("p (k n) -> p k n", k=KT) for w in WA]
            with pe.Fori(0, 2) as i:
                for s in range(2):
                    pe.wait_ge(sem(f"wa{s}"), i * 16 + 16)
                    for j in range(4):
                        pe.wait_ge(sem("fm_free"), i * 8 + 4 * s + j + 1)
                        fm_tile(w8[s], j, 2 * j, hk).then_inc(sem("prod"), 1)
            pe.wait_ge(sem("wa0"), 48)
            for j in range(4):
                pe.wait_ge(sem("fm_free"), 16 + j + 1)
                fm_tile(w8[0], j, 2 * j, hk).then_inc(sem("prod"), 1)

            pe.wait_ge(sem("fm_free"), 24)

            def tm_tile(w, i, cols):
                m = 128 if i < TT else NS
                for k in range(KT):
                    last = mm(PS[0:m, i, 0:cols], hT[:, k, 128 * i:128 * i + m], w[:, k, 0:cols],
                              start=(k == 0), stop=(k == KT - 1))
                last.then_inc(sem("prod"), 1)

            with pe.Fori(0, 2) as c:
                for s in (1, 0):
                    pe.wait_ge(sem(f"wa{s}"), c * 16 + (48 if s else 64))
                    for i in range(5):
                        pe.wait_ge(sem("tm_free"), c * 10 + 5 * (1 - s) + i + 1)
                        tm_tile(w8[s], i, 512)
            pe.wait_ge(sem("wa1"), 80)
            w_last = WA[1][:, 0:KT * 296].rearrange("p (k n) -> p k n", k=KT)
            for i in range(5):
                pe.wait_ge(sem("tm_free"), 20 + i + 1)
                tm_tile(w_last, i, 280)
            for k in range(KT):
                for h in range(2):
                    last = mm(PS[0:GA, 5 + h, 0:HALF], w_last[:, k, 280:296], hT[:, k, HALF * h:HALF * h + HALF],
                              start=(k == 0), stop=(k == KT - 1))
            last.then_inc(sem("prod"), 1)

            pe.wait_ge(*done("ga_ev"))
            pe.wait_ge(sem("ld_wa2"), 16)
            for k in range(2):
                for h in range(2):
                    last = mm(PS[:, 2 * k + h, 0:HALF], wa2[0:GA, 128 * k:128 * k + 128],
                              gaT[0:GA, HALF * h:HALF * h + HALF], start=True, stop=True)
            last.then_inc(once("la_mm"), 1)
            pe.wait_ge(sem("la_ev"), 1)
            pe.wait_ge(*done("qk"))
            for step in range(LEVELS + 1):
                if step:
                    pe.wait_ge(sem("a_ready"), 2 * step)
                for g in range(8):
                    c, par = g // 2, g % 2
                    if step:
                        pe.wait_ge(sem("sc_cp"), 8 * (step - 1) + g + 1)
                    for k in range(4):
                        r, t = slice(64 * par, 64 * par + 64), slice(128 * c, 128 * c + 128)
                        if step:
                            a = chunks(AL[(step - 1) % 2])[r, k, t]
                            last = mm(PS[:, g, 128 * k:128 * k + 128], a, a, start=True, stop=True)
                        else:
                            last = mm(PS[:, g, 128 * k:128 * k + 128], zf[r, ZK + k, t], zf[r, ZQ + k, t],
                                      start=True, stop=True)
                    last.then_inc(sem("sc_mm"), 1)
            pe.wait_ge(*done("kdec"))
            pe.wait_ge(sem("sc_cp"), 8 * LEVELS + 8)
            for c in range(4):
                for k in range(4):
                    last = tr(PS[:, c, 128 * k:128 * k + 128], chunks(A0)[:, k, 128 * c:128 * c + 128], ident)
                last.then_inc(sem("kt_mm"), 1)
            for c in range(4):
                pe.wait_ge(sem("kd_ev"), c + 1)
                for par in range(2):
                    for k in range(4):
                        last = mm(PS[64 * par:64 * par + 64, 4 + c, 128 * k:128 * k + 128],
                                  KD[:, c, k, 64 * par:64 * par + 64], zt[:, c, head_cols(k, par)[0]],
                                  start=True, stop=True)
                last.then_inc(sem("ds_mm"), 1)
            pe.wait_ge(sem("st"), 4)
            pe.wait_ge(*done("qdec"))
            for hh in range(8):
                k, par = hh // 2, hh % 2
                r = slice(64 * par, 64 * par + 64)
                for c in range(4):
                    o = PS[:, hh, 128 * c:128 * c + 128]
                    last = mm(o, zt[:, c, head_cols(k, par)[0]], SC[:, 2 * c + par, k], start=True, stop=(c == 0))
                    if c:
                        last = mm(o, ST[r, c - 1, k], chunks(A0)[r, k, 128 * c:128 * c + 128],
                                  start=False, stop=True)
                last.then_inc(sem("o_mm"), 1)
            pe.wait_ge(sem("ob"), 8)
            for g in range(8):
                m = g // 4
                v = zt[0:NS, 4, 512 * m:512 * m + 512].rearrange("p (k q v) -> p k q v", k=2, q=2)
                for par in range(2):
                    for j in range(2):
                        s = 2 * (g % 4) + j
                        last = mm(PS[64 * par:64 * par + 64, g, 256 * j:256 * j + 256],
                                  C("onehot", 64 * s, 64 * s + 64, NS), v[:, :, par, :], start=True, stop=True)
                last.then_inc(sem("vb_mm"), 1)
            pe.wait_ge(sem("ss_done"), 8)
            for par in range(2):
                for k in range(4):
                    for s in range(NS):
                        r = slice(64 * par, 64 * par + 64)
                        last = mm(PS[:, par, 8 * k + s:8 * k + s + 1], SS[r, k // 2, s, k % 2],
                                  zf[r, ZQ + k, L + s:L + s + 1], start=True, stop=True)
            last.then_inc(once("os_mm"), 1)
            pe.wait_ge(sem("os_ev"), 2)
            for hh in range(8):
                pe.wait_ge(sem("hn_sq"), hh + 1)
                if hh >= 4:
                    pe.wait_ge(sem("hn_ln"), hh - 3)
                for h in range(2):
                    last = mm(PS[:, 2 * (hh % 4) + h, 0:HALF], ones, SQ[hh % 2][:, HALF * h:HALF * h + HALF],
                              start=True, stop=True)
                last.then_inc(sem("hn_mm"), 1)

            pe.wait_ge(sem("hn_ln"), 8)
            pe.wait_ge(sem("ld_pool"), 80)
            for g in range(4):
                last = tr(PS[:, 0, 120 * g:120 * g + 120], hist[:, g], ident[0:120, 0:120])
            last.then_inc(once("hist_mm"), 1)
            for g in range(4):
                last = tr(PS[0:23, 1, 128 * g:128 * g + 128], zf[:, ZU + g, 497:520], ident)
            last.then_inc(once("tail_mm"), 1)
            for g in range(4):
                pe.wait_ge(sem("pd"), 2 * g + 2)
                if g >= 2:
                    pe.wait_ge(sem("pool_ev"), g - 1)
                for h in range(2):
                    last = mm(PS[:, 2 + 2 * (g % 2) + h, 0:HALF], poolw[:, g], PD[:, g, HALF * h:HALF * h + HALF],
                              start=True, stop=True)
                last.then_inc(sem("pool_mm"), 1)

            pe.wait_ge(sem("pool_ev"), 4)
            pe.wait_ge(*done("tail"))
            pe.wait_ge(*done("q_norm"))
            pe.wait_ge(*done("k_norm"))
            for i in range(5):
                w = 128 if i < TT else NS
                for g in range(G):
                    last = tr(PS[:, i, w * g:w * g + w], QN[0:w, i, g].rearrange("p k d -> p (k d)"),
                              ident[0:w, 0:w])
                last.then_inc(sem("qt_mm"), 1)
            for n, col in enumerate((CS, CW)):
                for i in range(TT):
                    last = tr(PS[:, 5 + n, 128 * i:128 * i + 128], zt[:, i, col:col + 128], ident)
                last.then_inc(sem("qt_mm"), 1)
            for n, col in enumerate((CS, CW)):
                last = tr(PS[:, 7, NS * n:NS * n + NS], zt[0:NS, 4, col:col + 128], ident[0:NS, 0:NS])
            last.then_inc(sem("qt_mm"), 1)
            pe.wait_ge(sem("qt_ev"), 8)
            for i in range(TT):
                last = mm(PS[0:32, 0, 0:256], C("pool", 32 * i, 32 * i + 32), zt[:, i, CK:CK + 256],
                          start=(i == 0), stop=(i == TT - 1))
            last.then_inc(once("ckv_mm"), 1)
            pe.wait_ge(*done("ckv"))
            tr(PS[:, 1, 0:32], CKV[:, 0:128], ident[0:32, 0:32]).then_inc(once("kct_mm"), 1)
            pe.wait_ge(*done("kct"))
            for k in range(HKV):
                r = slice(64 * k, 64 * k + 64)
                for i in range(TT):
                    for g in range(G):
                        last = mm(PS[:, 4 * k + i, 32 * g:32 * g + 32], QT[r, g, 128 * i:128 * i + 128],
                                  kcT[r, :], start=True, stop=True)
                    last.then_inc(sem("cs_mm"), 1)
            pe.wait_ge(*done("cp"))
            for i in range(TT):
                for k in range(HKV):
                    last = tr(PS[:, 2 * (i % 2) + k, 0:128],
                              CM[:, i, 4 * k:4 * k + 4].rearrange("p h c -> p (h c)"), ident)
                last.then_inc(sem("ct_mm"), 1)
                pe.wait_ge(sem("ct_ev"), i + 1)
                for k in range(HKV):
                    last = mm(PS[:, 4 + i, 256 * k:256 * k + 256], PTC[:, i, k], VBK[:, k],
                              start=True, stop=True)
                last.then_inc(sem("co_mm"), 1)
            pe.wait_ge(sem("co_ev"), 4)
            NU = len(UNITS)
            for u in range(NU + 2):
                if u < NU:
                    i, b, h = UNITS[u]
                    k, g = h // G, h % G
                    r, bank = slice(64 * k, 64 * k + 64), u % 3
                    if u >= 3:
                        pe.wait_ge(sem("ex"), u - 2)
                    mm(PS[:, bank, 0:128 * i + 128], QT[r, g, 128 * i:128 * i + 128],
                       (KTS, KTW)[b][r, 0:128 * i + 128], start=True, stop=False)
                    mm(PS[:, bank, 128 * i:128 * i + 128], ident, C("causal"), start=False, stop=True)\
                        .then_inc(sem("s_mm"), 1)
                if 1 <= u <= NU:
                    v = u - 1
                    i = UNITS[v][0]
                    pe.wait_ge(sem("ex"), v + 1)
                    if v >= 3:
                        pe.wait_ge(sem("pt_ev"), v - 2)
                    for j in range(i + 1):
                        last = tr(PS[:, 3 + v % 3, 128 * j:128 * j + 128], P[v % 3][:, 128 * j:128 * j + 128], ident)
                    last.then_inc(sem("t_mm"), 1)
                if u >= 2:
                    v = u - 2
                    i, b, h = UNITS[v]
                    pe.wait_ge(sem("pt_ev"), v + 1)
                    if v % 16 == 0 and i:
                        pe.wait_ge(sem("on"), i)
                    col = (CS, CW)[b] + 128 + 64 * (h // G)
                    for j in range(i + 1):
                        last = mm(PS[:, 6 + b, 64 * h:64 * h + 64], PT[v % 3][:, j], zt[:, j, col:col + 64],
                                  start=(j == 0), stop=(j == i))
                    last.then_inc(sem("pv_mm"), 1)
            for i in range(TT):
                pe.wait_ge(sem("on"), i + 1)
                if i == 0:
                    pe.wait_ge(sem("on"), TT)
                for c in range(4):
                    last = tr(PS[:, i, 128 * c:128 * c + 128], ON[:, i, 128 * c:128 * c + 128], ident)
                last.then_inc(sem("ont_mm"), 1)
            pe.wait_ge(sem("ont"), 4)
            pe.wait_ge(*done("q_saved"))
            for x in range(NS):
                pe.wait_ge(sem("c_red"), x + 1)
                mm(PS[0:NCMP, x, 0:256], C("shift", 0, NCMP), S16[x % 2], start=True, stop=True)\
                    .then_inc(sem("sh_mm"), 1)
            pe.wait_ge(*done("cx"))
            for u in range(2):
                for x in range(4):
                    last = tr(PS[:, u, NCMP * x:NCMP * x + NCMP], CX[u][:, x, 0:128], ident[0:NCMP, 0:NCMP])
                last.then_inc(sem("kx_mm"), 1)
            pe.wait_ge(sem("kx_ev"), 2)
            for x in range(NS):
                last = mm(PS[0:NCMP, 2, 8 * x:8 * x + 8], KCT[:, x], QB[:, x], start=True, stop=True)
            last.then_inc(once("cxs_mm"), 1)
            pe.wait_ge(*done("cxs"))
            tr(PS[0:64, 3, 0:NCMP], PCT, ident[0:NCMP, 0:NCMP]).then_inc(once("cxt_mm"), 1)
            pe.wait_ge(*done("cxp"))
            tr(PS[0:NCMP, 4, 0:64], PCR, ident[0:64, 0:64]).then_inc(once("cxp_mm"), 1)
            pe.wait_ge(*done("pct"))
            for x in range(NS):
                last = mm(PS[:, 5, 8 * x:8 * x + 8], CX[x // 4][:, x % 4, 128:256], PCT[:, 8 * x:8 * x + 8],
                          start=True, stop=True)
            last.then_inc(once("cxo_mm"), 1)
            pe.wait_ge(*done("gd"))
            mm(PS[:, 6, 0:192], ones[0:NS], GD.rearrange("p b s h -> p (b s h)"), start=True, stop=True)\
                .then_inc(once("gb_mm"), 1)
            pe.wait_ge(*done("pcg"))
            mm(PS[0:16, 7, 0:NSEL], PCG, C("overlap", p=NCMP), start=True, stop=True).then_inc(once("imp_mm"), 1)
            pe.wait_ge(*done("rank"))
            tr(PS[0:NSEL, 0, 0:16], RANK, ident[0:16, 0:16]).then_inc(once("sel_mm"), 1)
            pe.wait_ge(*done("selt"))
            mm(PS[:, 1, 0:16], C("expand", p=NSEL), SELT, start=True, stop=True).then_inc(once("bs_mm"), 1)
            for b in range(2):
                mm(PS[0:NS, 2 + b, 0:64], KNEW[:, b], QB.rearrange("p s h -> p (s h)"), start=True, stop=True)\
                    .then_inc(sem("sn_mm"), 1)
            pe.wait_ge(sem("sn"), 2)
            pe.wait_ge(*done("bs"))
            kt = 0
            for n, (b, s0) in enumerate(ROUNDS):
                per = 4 if b == 0 else 1
                for x in range(s0, s0 + 4):
                    if b == 0:
                        pe.wait_ge(sem(f"xs{x % 4}"), 16 * (2 * 1 + x // 4 + 1))
                    else:
                        pe.wait_ge(sem(f"xw{x // 4}"), 16)
                    for q in range(per):
                        if kt + q >= 4:
                            pe.wait_ge(sem("ktx"), kt + q - 3)
                        for i in range(4):
                            last = tr(PS[:, (kt + q) % 4, 128 * i:128 * i + 128], xtile(b, x, 4 * q + i)[0], ident)
                        last.then_inc(sem("ktx_mm"), 1)
                    m = 4 * n + x - s0
                    if m >= 2:
                        pe.wait_ge(sem("sx"), m - 1)
                    for q in range(per):
                        pe.wait_ge(sem("ktx"), kt + q + 1)
                        for i in range(4):
                            at = 8 * (4 * q + i)
                            last = mm(PS[:, 4 + m % 2, at:at + 8], KTX[:, 4 * ((kt + q) % 4) + i], QB[:, x],
                                      start=True, stop=True)
                        last.then_inc(sem("sx_mm"), 1)
                    kt += per
                pe.wait_ge(sem("m1"), n + 1)
                tr(PS[0:32, 6, 0:128], M1, ident)
                tr(PS[0:32, 6, 128:136], SN[b][:, 8 * s0:8 * s0 + 32], ident[0:NS, 0:NS]).then_inc(sem("mt_mm"), 1)
                pe.wait_ge(sem("dg"), n + 1)
                mm(PS[:, 6, 0:32], ones[0:32], DG, start=True, stop=True).then_inc(sem("mb_mm"), 1)
                pe.wait_ge(sem("r1"), n + 1)
                mm(PS[:, 6, 64:96], ones, M1, start=True, stop=False)
                mm(PS[:, 6, 64:96], ones[0:NS], SN[b][:, 8 * s0:8 * s0 + 32], start=False, stop=True)\
                    .then_inc(sem("sum_mm"), 1)
                if n:
                    pe.wait_ge(sem("oacc"), n + 1)
                for x in range(s0, s0 + 4):
                    o = PS[:, 7, 8 * (x - s0):8 * (x - s0) + 8]
                    for i in range(4 * per):
                        mm(o, xtile(b, x, i)[1], SX[:, x - s0, i], start=(i == 0), stop=False)
                    col = (CS, CW)[b] + 128
                    last = mm(o, zt[0:NS, 4, col:col + 128], SN[b][:, 8 * x:8 * x + 8], start=False, stop=True)
                last.then_inc(sem("sv_mm"), 1)

            pe.wait_ge(*done("nsa_done"))
            wb4 = [w.rearrange("p (c n) -> p c n", c=4) for w in WB]
            with pe.Fori(0, 2) as hf:
                with pe.Fori(0, 2) as bp:
                    for s in range(2):
                        n = hf * 2 + bp
                        pe.wait_ge(sem(f"wa{s}"), n * 16 + 96)
                        pe.wait_ge(sem(f"wb{s}"), n * 16 + 16)
                        for j in range(4):
                            pe.wait_ge(sem("mix_free"), n * 8 + 4 * s + j + 1)
                            fm_tile(w8[s], j, 4 * (j % 2), hk)
                            fm_tile(wb4[s], j, 4 * (j % 2) + 2,
                                    lambda c: zf[:, bass.ds(bp * 8 + 4 * s + c, 1)].rearrange("p k t -> p (k t)"),
                                    k_tiles=4).then_inc(sem("prod"), 1)
            pe.wait_ge(sem("mix_free"), 34)
            for n in range(8):
                if n % 4 == 0:
                    pe.wait_ge(sem(f"wa{n // 4}"), 160)
                if n >= 4:
                    pe.wait_ge(sem("wo_ev"), n - 3)
                fm_tile(w8[n // 4], n % 4, 2 * (n % 4), lambda k: mixT[:, k]).then_inc(sem("prod"), 1)
            pe.wait_ge(sem("wo_ev"), 8)
            norm_sums("n2")
            pe.wait_ge(sem("n2_h"), KT)
            with pe.Fori(0, 4) as i:
                for s in range(2):
                    pe.wait_ge(sem(f"wa{s}"), i * 16 + 176)
                    for j in range(4):
                        pe.wait_ge(sem("u_free"), i * 8 + 4 * s + j + 1)
                        fm_tile(w8[s], j, 2 * j, hk).then_inc(sem("prod"), 1)
            pe.wait_ge(sem("u_ev"), 32)
            w32 = [w.rearrange("p (k n) -> p k n", k=32) for w in WA]
            with pe.Fori(0, 4) as i:
                for s in range(2):
                    pe.wait_ge(sem(f"wa{s}"), i * 16 + 240)
                    pe.wait_ge(sem("y_free"), i * 2 + s + 1)
                    fm_tile(w32[s], 0, 4 * s, lambda k: uT[:, k], k_tiles=32).then_inc(sem("prod"), 1)
            pe.wait_ge(sem("y_free"), 10)
            for n in range(10):
                i, k4, w = n // 2, 4 * (n % 2), (128 if n < 8 else NS)
                if n >= 8:
                    pe.wait_ge(sem("y_ev"), n - 7)
                for j in range(4):
                    last = tr(PS[0:w, n % 8, 128 * j:128 * j + 128], xT[:, k4 + j, 128 * i:128 * i + w], ident)
                last.then_inc(sem("yt_mm"), 1)

        @block.scalar
        def _(act):
            f = nc.scalar.activation
            step = steps(act, "act_step")

            def norm(tag):
                for k in range(KT):
                    if k >= 2:
                        act.wait_ge(sem(tag + "_mm"), k - 1)
                    f(SQN[k % 2], xT[:, k], ACT.Square).then_inc(sem(tag + "_sq"), 1)
                act.wait_ge(sem(tag + "_mm"), KT)
                step(f(halves(RST), pair(0), ACT.Ln, bias=eps, scale=1.0 / D))
                f(RST, RST, ACT.Exp, scale=-0.5).then_inc(sem(tag + "_rs"), 1)

            act.wait_ge(*done("eps"))
            act.wait_ge(sem("xt_ev"), 10)
            norm("n1")

            act.wait_ge(sem("prod"), 46)
            act.wait_ge(sem("fm_free"), 24)
            f(SIGQ, zf[:, ZQ + 2:ZQ + 4], ACT.Sigmoid).then_inc(sem("sig"), 1)
            f(SIGF, zf[:, ZK + 2:ZK + 4], ACT.Sigmoid).then_inc(sem("sig"), 1)
            f(SIGG, zf[:, ZG:ZG + 8], ACT.Sigmoid).then_inc(sem("sig"), 1)
            act.wait_ge(sem("la_ev"), 2)
            step(f(TMPA, LF[:, 0:2], ACT.Abs))
            step(f(TMPA, TMPA, ACT.Exp, scale=-1.0))
            f(TMPA, TMPA, ACT.Ln, bias=1.0).then_inc(once("lsp"), 1)
            act.wait_ge(*done("lb_d"))
            f(lbv[:, :, 1], lbv[:, :, 0], ACT.Exp).then_inc(once("lb_e"), 1)
            act.wait_ge(*done("fg"))
            f(LF[:, 2:4], LF[:, 2:4], ACT.Ln).then_inc(once("lf_h"), 1)
            act.wait_ge(*done("lf_h"))
            act.wait_ge(*done("lf_g"))
            f(decS, LF[:, :, L:T], ACT.Exp).then_inc(once("decs"), 1)
            for lev in range(LEVELS):
                act.wait_ge(sem("dist"), 2 * lev + 2)
                f(EL[lev % 2], EL[lev % 2], ACT.Exp).then_inc(sem("e_ready"), 1)
            act.wait_ge(sem("a_ready"), 2 * LEVELS)
            f(E1, B, ACT.Exp).then_inc(sem("eb"), 1)
            act.wait_ge(sem("dist"), 2 * LEVELS + 1)
            f(E0, E0, ACT.Exp).then_inc(sem("eb"), 1)
            f(decC, B.rearrange("p (k c t) -> p k c t", k=4, c=4)[:, :, :, 127], ACT.Exp).then_inc(once("decc"), 1)
            act.wait_ge(sem("ob"), 8)
            act.wait_ge(sem("os_ev"), 2)
            for hh in range(9):
                if hh < 8:
                    if hh >= 2:
                        act.wait_ge(sem("hn_mm"), hh - 1)
                    f(SQ[hh % 2], OB[:, hh], ACT.Square).then_inc(sem("hn_sq"), 1)
                if hh:
                    j = hh - 1
                    act.wait_ge(sem("hn_mm"), j + 1)
                    if j >= 2:
                        act.wait_ge(sem("hn"), j - 1)
                    f(halves(RN[j % 2]), pair(2 * (j % 4)), ACT.Ln, bias=eps, scale=1.0 / 128)\
                        .then_inc(sem("hn_ln"), 1)
                    act.wait_ge(sem("hn_ln"), j + 1)
                    f(RN[j % 2], RN[j % 2], ACT.Exp, scale=-0.5).then_inc(sem("hn_rs"), 1)

            act.wait_ge(sem("hn"), 8)
            act.wait_ge(sem("o_mm"), 8)
            f(zt[:, :, CG:CG + 24], zt[:, :, CG:CG + 24], ACT.Sigmoid).then_inc(once("ng"), 1)
            f(TQ, zt[:, :, CQ:CQ + 512], ACT.Square).then_inc(sem("tq"), 1)
            f(TK[:, :, 0:128], zt[:, :, CS:CS + 128], ACT.Square).then_inc(sem("tq"), 1)
            f(TK[:, :, 128:256], zt[:, :, CW:CW + 128], ACT.Square).then_inc(sem("tq"), 1)
            act.wait_ge(sem("rq_sum"), 2)
            step(f(rq, rq, ACT.Ln, bias=eps, scale=1.0 / HD))
            f(rq, rq, ACT.Exp, scale=-0.5).then_inc(once("rq"), 1)
            act.wait_ge(*done("kst"))
            step(f(kst[:, 0:2], kst[:, 0:2], ACT.Ln, bias=eps[0:32], scale=1.0 / HD))
            f(kst[:, 0:2], kst[:, 0:2], ACT.Exp, scale=-0.5).then_inc(once("kst_rs"), 1)
            act.wait_ge(*done("cm"))
            f(CM, CM, ACT.Exp).then_inc(once("cm_e"), 1)
            for u in range(len(UNITS)):
                i, b, h = UNITS[u]
                act.wait_ge(sem("mx"), u + 1)
                if u >= 3:
                    act.wait_ge(sem("t_mm"), u - 2)
                f(P[u % 3][:, 0:128 * i + 128], PS[:, u % 3, 0:128 * i + 128], ACT.Exp, bias=nm[u % 3],
                  accum_out=rs[:, i, b, h:h + 1]).then_inc(sem("ex"), 1)
            act.wait_ge(*done("kst_x"))
            step(f(KST, KST, ACT.Ln, bias=eps[0:NCMP], scale=1.0 / HD))
            f(KST, KST, ACT.Exp, scale=-0.5).then_inc(once("kst_xr"), 1)
            act.wait_ge(*done("cxm"))
            f(PCR, PS[0:64, 3, 0:NCMP], ACT.Exp, bias=CMAX[:, 0:1], accum_out=CMAX[:, 1:2]).then_inc(once("cxe"), 1)
            for n, (b, s0) in enumerate(ROUNDS):
                act.wait_ge(sem("sxm"), n + 1)
                ni = 16 if b == 0 else 4
                f(SX[:, :, 0:ni], SX[:, :, 0:ni], ACT.Exp).then_inc(sem("sxe"), 1)
                new = SN[b][:, 8 * s0:8 * s0 + 32]
                f(new, new, ACT.Exp).then_inc(sem("sxe"), 1)

            with act.Fori(0, 2) as hf:
                with act.Fori(0, 2) as bp:
                    for s in range(2):
                        for j in range(4):
                            n = hf * 16 + bp * 8 + 4 * s + j
                            act.wait_ge(sem("prod"), n + 47)
                            act.wait_ge(sem("mix_free"), n + 1)
                            f(halves(SG[j % 2]), pair(4 * (j % 2)), ACT.Sigmoid,
                              bias=V("bg")[:, bass.ds(bp * 16 + hf * 4 + 8 * s + j, 1)]).then_inc(sem("sg"), 1)
            act.wait_ge(sem("wo_ev"), 8)
            norm("n2")
            with act.Fori(0, 4) as i:
                for s in range(2):
                    for j in range(4):
                        n = i * 8 + 4 * s + j
                        act.wait_ge(sem("prod"), n + 87)
                        f(halves(uT[:, bass.ds(n, 1)].rearrange("p k t -> p (k t)")), pair(2 * j), ACT.Relu)\
                            .then_inc(sem("u_free"), 1)

        @block.vector
        def _(dve):
            v = nc.vector
            step = steps(dve, "dve_step")

            def norm_apply(tag, g):
                dve.wait_ge(sem(tag + "_rs"), 1)
                for k in range(KT):
                    v.scalar_tensor_tensor(hT[:, k], xT[:, k], V(g, k, k + 1), RST, ALU.mult, ALU.mult)\
                        .then_inc(sem(tag + "_h"), 1)

            dve.sem_inc(sem("fm_free"), 4)
            dve.sem_inc(sem("tm_free"), 5)
            dve.sem_inc(sem("mix_free"), 2)
            dve.sem_inc(sem("y_free"), 2)
            dve.sem_inc(sem("u_free"), 4)
            v.memset(eps, EPS).then_inc(once("eps"), 1)
            for n in range(10):
                i, k4, w = n // 2, 4 * (n % 2), (128 if n < 8 else NS)
                dve.wait_ge(sem("xt"), n + 1)
                v.tensor_copy(xT[:, k4:k4 + 4, 128 * i:128 * i + w],
                              PS[:, n % 8, 0:4 * w].rearrange("p (k t) -> p k t", k=4)).then_inc(sem("xt_ev"), 1)
            dve.wait_ge(sem("ld_idx"), 16)
            dve.wait_ge(sem("ld_con"), 32)
            v.tensor_scalar(idx[:, NS:], idx[:, 0:NS], 8.0, V("r8"), ALU.mult, ALU.add).then_inc(once("idx"), 1)
            dve.wait_ge(sem("xt_ev"), 10)
            norm_apply("n1", "n1")

            with dve.Fori(0, 2) as i:
                for s in range(2):
                    for j in range(4):
                        n = i * 8 + 4 * s + j
                        dve.wait_ge(sem("prod"), n + 1)
                        v.tensor_copy(halves(zf[:, bass.ds(n, 1)].rearrange("p k t -> p (k t)")), pair(2 * j))\
                            .then_inc(sem("fm_free"), 1)
            for j in range(4):
                dve.wait_ge(sem("prod"), 17 + j)
                v.tensor_copy(halves(zf[:, 16 + j]), pair(2 * j)).then_inc(sem("fm_free"), 1)
            dve.wait_ge(sem("zt_zero"), 1)

            def tm_evac(n, i, c0, cols):
                m = 128 if i < TT else NS
                dve.wait_ge(sem("prod"), n + 21)
                v.tensor_copy(zt[0:m, i, c0], PS[0:m, i, 0:cols]).then_inc(sem("tm_free"), 1)

            with dve.Fori(0, 2) as c:
                for s in range(2):
                    for i in range(5):
                        tm_evac(c * 10 + 5 * s + i, i, bass.ds(c * 1024 + 512 * s, 512), 512)
            for i in range(5):
                tm_evac(20 + i, i, slice(2048, 2328), 280)
            dve.wait_ge(sem("prod"), 46)
            v.tensor_copy(halves(gaT[0:GA]), PS[0:GA, 5:7, 0:HALF]).then_inc(once("ga_ev"), 1)

            dve.wait_ge(sem("fm_free"), 24)
            dve.wait_ge(sem("ld_con"), 32)
            step(v.tensor_scalar(zf[:, ZQ:ZQ + 2], zf[:, ZQ:ZQ + 2], 0.125, None, ALU.mult))
            dve.wait_ge(sem("sig"), 1)
            v.scalar_tensor_tensor(zf[:, ZQ + 2:ZQ + 4], zf[:, ZQ + 2:ZQ + 4], 0.125, SIGQ, ALU.mult, ALU.mult)\
                .then_inc(once("q_act"), 1)
            dve.wait_ge(*done("la_mm"))
            for k in range(2):
                v.tensor_scalar(halves(LF[:, k]), pair(2 * k), V("ba", k, k + 1), None, ALU.add)\
                    .then_inc(sem("la_ev"), 1)
            v.tensor_tensor(lbv[:, :, 0], V("lb"), V("lb"), ALU.subtract).then_inc(once("lb_d"), 1)
            dve.wait_ge(*done("lb_e"))
            step(v.reciprocal(lbv[:, :, 2], lbv[:, :, 1]))
            step(v.tensor_tensor(lbv[:, :, 3], lbv[:, :, 1], lbv[:, :, 2], ALU.mult))
            step(v.tensor_tensor(lbv[:, :, 4], lbv[:, :, 3], lbv[:, :, 3], ALU.subtract))
            step(v.tensor_scalar(lbv[:, :, 5], lbv[:, :, 4], -1.0, 1.0, ALU.mult, ALU.add))
            dve.wait_ge(sem("sig"), 2)
            for k in range(2):
                step(v.tensor_scalar(LF[:, 2 + k], SIGF[:, k], lbv[:, k, 5:6], lbv[:, k, 4:5], ALU.mult, ALU.add))
            step(v.tensor_scalar(zf[:, ZK + 2:ZK + 4], LF[:, 2:4], -1.0, 1.0, ALU.mult, ALU.add))
            v.tensor_scalar(LF[:, 2:4], LF[:, 2:4], 2.0 ** -63, None, ALU.max).then_inc(once("fg"), 1)
            dve.wait_ge(sem("la_ev"), 2)
            dve.wait_ge(*done("lsp"))
            step(v.scalar_tensor_tensor(flat(LF[:, 0:2]), flat(LF[:, 0:2]), 0.0, flat(TMPA), ALU.min, ALU.subtract))
            v.tensor_scalar(LF[:, 0:2], LF[:, 0:2], 1.0 / 16, None, ALU.mult).then_inc(once("lf_g"), 1)
            dve.wait_ge(*done("lf_g"))
            dve.wait_ge(*done("lf_h"))
            for k in range(4):
                v.tensor_tensor_scan(chunks(B)[:, k], C("reset"), LF[:, k, 0:L], 0.0, ALU.mult, ALU.add)\
                    .then_inc(sem("cum"), 1)
            dve.wait_ge(sem("sig"), 3)
            v.tensor_tensor(flat(zf[:, ZG:ZG + 8]), flat(zf[:, ZG:ZG + 8]), flat(SIGG), ALU.mult)\
                .then_inc(once("qk"), 1)

            def score_copy(st):
                for g in range(8):
                    dve.wait_ge(sem("sc_mm"), 8 * st + g + 1)
                    mk = LEVELS if st == 0 else st - 1
                    mask = C("masks", 128 * mk, 128 * mk + 128)
                    ps = PS[:, g].rearrange("p (k t) -> p k t", k=4)
                    if st == 0:
                        v.tensor_tensor(SC[:, g], ps, mask.unsqueeze(1).to_broadcast([128, 4, 128]), ALU.mult)\
                            .then_inc(sem("sc_cp"), 1)
                    else:
                        v.copy_predicated(SC[:, g], mask.bitcast(i32).unsqueeze(1).to_broadcast([128, 4, 128]), ps)\
                            .then_inc(sem("sc_cp"), 1)

            dve.wait_ge(*done("qk"))
            for lev in range(LEVELS):
                half = 1 << lev
                dve.wait_ge(sem("e_ready"), lev + 1)
                if lev >= 2:
                    dve.wait_ge(sem("sc_mm"), 8 * lev)
                if lev == 0:
                    dve.wait_ge(*done("lsp"))
                for side, z0 in ((0, ZK), (1, ZQ)):
                    blk = lambda ap: ap.rearrange("p k (n q h) -> p k n q h", q=2, h=half)[:, :, :, side]
                    a, e = blk(chunks(AL[lev % 2])), blk(chunks(EL[lev % 2]))
                    x = zf[:, z0:z0 + 4, 0:L].rearrange("p k (n q h) -> p k n q h", q=2, h=half)[:, :, :, side]
                    v.tensor_tensor(a, x, e, ALU.mult).then_inc(sem("a_ready"), 1)
                score_copy(lev)
                dve.wait_ge(sem("sc_cp"), 8 * lev + 8)
            score_copy(LEVELS)

            dve.wait_ge(sem("eb"), 2)
            dve.wait_ge(sem("sc_mm"), 8 * LEVELS + 8)
            v.tensor_tensor(chunks(A0), zf[:, ZK:ZK + 4, 0:L], chunks(E0), ALU.mult).then_inc(once("kdec"), 1)
            dve.wait_ge(*done("decs"))
            dve.wait_ge(sem("cum"), 4)
            for c in range(4):
                dve.wait_ge(sem("kt_mm"), c + 1)
                v.tensor_copy(KD[:, c].rearrange("p k f -> p (k f)"), PS[:, c]).then_inc(sem("kd_ev"), 1)
            v.tensor_tensor(chunks(A0), zf[:, ZQ:ZQ + 4, 0:L], chunks(E1), ALU.mult).then_inc(once("qdec"), 1)
            dve.wait_ge(*done("decc"))
            for c in range(4):
                dve.wait_ge(sem("ds_mm"), c + 1)
                ds = PS[:, 4 + c].rearrange("p (k v) -> p k v", k=4)
                if c == 0:
                    v.tensor_copy(ST[:, 0], ds).then_inc(sem("st"), 1)
                else:
                    dve.wait_ge(sem("st"), c)
                    step(v.tensor_tensor(ST[:, c], ST[:, c - 1], bc(decC[:, :, c], 128), ALU.mult))
                    v.tensor_tensor(ST[:, c], ST[:, c], ds, ALU.add).then_inc(sem("st"), 1)
            dve.wait_ge(sem("o_mm"), 8)
            for hh in range(8):
                v.tensor_copy(OB[:, hh, 0:L], PS[:, hh]).then_inc(sem("ob"), 1)
            dve.wait_ge(sem("ld_ss"), 64)
            for m in range(2):
                d = decS[:, 2 * m:2 * m + 2].rearrange("p k s -> p s k")
                step(v.tensor_tensor(SS[:, m], SS[:, m], bc(d, 128), ALU.mult))
            for g in range(8):
                m, s0 = g // 4, 2 * (g % 4)
                dve.wait_ge(sem("vb_mm"), g + 1)
                k = zf[:, ZK + 2 * m:ZK + 2 * m + 2, L + s0:L + s0 + 2].rearrange("p k s -> p s k")
                step(v.tensor_tensor(VB[g % 2], PS[:, g].rearrange("p (s k v) -> p s k v", s=2, k=2), bc(k, 128), ALU.mult))
                v.tensor_tensor(SS[:, m, s0:s0 + 2], SS[:, m, s0:s0 + 2], VB[g % 2], ALU.add)\
                    .then_inc(sem("ss_done"), 1)
            dve.wait_ge(*done("os_mm"))
            for par in range(2):
                v.tensor_copy(OB[:, par:8:2, L:T], PS[:, par, 0:32].rearrange("p (k s) -> p k s", k=4))\
                    .then_inc(sem("os_ev"), 1)
            dve.wait_ge(sem("os_ev"), 2)
            for hh in range(8):
                dve.wait_ge(sem("hn_rs"), hh + 1)
                gain = V("gn") if hh < 4 else V("hn")
                step(v.scalar_tensor_tensor(OB[:, hh], OB[:, hh], gain, RN[hh % 2], ALU.mult, ALU.mult))
                v.tensor_tensor(zf[:, ZG + hh], zf[:, ZG + hh], OB[:, hh], ALU.mult).then_inc(sem("hn"), 1)

            dve.wait_ge(*done("hist_mm"))
            dve.wait_ge(sem("hn"), 8)
            hs = stat[:, 60:92].rearrange("p (g s) -> p g s", g=4)
            for g, w in enumerate(WINDOWS):
                step(v.tensor_reduce(hs[:, g], PS[:, 0, 120 * g:120 * g + 120].rearrange("p (s j) -> p s j", s=NS)
                                     [:, :, HIST + 1 - w:HIST], AX, ALU.add))
            step(v.tensor_tensor(hs, hs, zf[:, ZU:ZU + 4, L:T], ALU.add))
            dve.wait_ge(*done("tail_mm"))
            v.tensor_copy(tail, PS[0:23, 1].rearrange("p (g c) -> p g c", g=4)).then_inc(once("tail"), 1)
            dve.wait_ge(sem("win"), 1)
            for g, w in enumerate(WINDOWS):
                win = WP[(1, 0, 1, 0)[g]][:, g, HIST:HIST + L]
                v.scalar_tensor_tensor(PD[:, g, 0:L], win, 1.0 / w, zf[:, ZU + g, 0:L], ALU.mult, ALU.subtract)\
                    .then_inc(sem("pd"), 1)
                v.scalar_tensor_tensor(PD[:, g, L:T], hs[:, g], 1.0 / w, zf[:, ZU + g, L:T], ALU.mult, ALU.subtract)\
                    .then_inc(sem("pd"), 1)
            for g in range(4):
                dve.wait_ge(sem("pool_mm"), g + 1)
                v.tensor_scalar(halves(zf[:, ZU + g]), pair(2 + 2 * (g % 2)), V("psc", g, g + 1), None, ALU.mult)\
                    .then_inc(sem("pool_ev"), 1)

            dve.wait_ge(sem("pd"), 8)
            step(v.tensor_scalar(gq8, V("qg"), 0.125, None, ALU.mult))
            dve.wait_ge(sem("tq"), 3)
            v.tensor_reduce(rq[:, :, 0:8], TQ.rearrange("p i (h d) -> p i h d", d=HD), AX, ALU.add)\
                .then_inc(sem("rq_sum"), 1)
            v.tensor_reduce(rq[:, :, 8:12], TK.rearrange("p i (h d) -> p i h d", d=HD), AX, ALU.add)\
                .then_inc(sem("rq_sum"), 1)
            dve.wait_ge(*done("rq"))
            for n, col in enumerate((CS, CW)):
                kk = zt[:, :, col:col + 128].rearrange("p i (h d) -> p i h d", d=HD)
                step(v.tensor_tensor(kk, kk, bc(rq[:, :, 8 + 2 * n:10 + 2 * n], HD), ALU.mult))
                gain = V("kg", 64 * (n + 1), 64 * (n + 2)).unsqueeze(1).unsqueeze(1).to_broadcast([128, 5, 2, HD])
                ins = v.tensor_tensor(kk, kk, gain, ALU.mult)
                if n == 0:
                    step(ins)
                else:
                    ins.then_inc(once("k_norm"), 1)
            for i in range(5):
                for k in range(HKV):
                    q = zt[:, i, CQ + 256 * k:CQ + 256 * k + 256].rearrange("p (g d) -> p g d", g=G)
                    step(v.tensor_tensor(QN[:, i, :, k], q, bc(rq[:, i, 4 * k:4 * k + 4], HD), ALU.mult))
            qv = R[:, 2560:5120].rearrange("p (n d) -> p n d", d=HD)
            v.tensor_tensor(qv, qv, gq8.unsqueeze(1).to_broadcast([128, 40, HD]), ALU.mult)\
                .then_inc(once("q_norm"), 1)
            for i in range(5):
                w = 128 if i < TT else NS
                dve.wait_ge(sem("qt_mm"), i + 1)
                v.tensor_copy(QT[:, :, 128 * i:128 * i + w], PS[:, i, 0:4 * w].rearrange("p (g t) -> p g t", g=G))\
                    .then_inc(sem("qt_ev"), 1)
            dve.wait_ge(sem("qt_mm"), 8)
            v.tensor_copy(KTS[:, 0:L], PS[:, 5]).then_inc(sem("qt_ev"), 1)
            v.tensor_copy(KTW[:, 0:L], PS[:, 6]).then_inc(sem("qt_ev"), 1)
            new = R[:, 7200:8240].rearrange("p (b t) -> p b t", b=2)[:, :, L:T]
            v.tensor_copy(new, PS[:, 7, 0:16].rearrange("p (b s) -> p b s", b=2)).then_inc(sem("qt_ev"), 1)
            dve.wait_ge(*done("ckv_mm"))
            step(v.tensor_copy(CKV, PS[0:32, 0, 0:256]))
            sq = gaT[0:32, 256:384]
            step(v.tensor_tensor(sq, CKV[:, 0:128], CKV[:, 0:128], ALU.mult))
            v.tensor_reduce(kst[:, 0:2], sq.rearrange("p (k d) -> p k d", d=HD), AX, ALU.add).then_inc(once("kst"), 1)
            dve.wait_ge(sem("hn"), 8)
            step(v.memset(VBK, 0.0))
            for j in range(4):
                step(v.tensor_copy(VBK[32 * j:32 * j + 32, :, 64 * j:64 * j + 64],
                                   CKV[:, 128:256].rearrange("p (k d) -> p k d", d=HD)))
            dve.wait_ge(*done("kst_rs"))
            ck = CKV[:, 0:128].rearrange("p (k d) -> p k d", d=HD)
            step(v.tensor_tensor(ck, ck, bc(kst[:, 0:2], HD), ALU.mult))
            v.tensor_tensor(ck, ck, V("kg", 0, 64, 32).unsqueeze(1).to_broadcast([32, 2, HD]), ALU.mult)\
                .then_inc(once("ckv"), 1)
            dve.wait_ge(*done("kct_mm"))
            v.tensor_copy(kcT, PS[:, 1, 0:32]).then_inc(once("kct"), 1)
            for k in range(HKV):
                for i in range(TT):
                    dve.wait_ge(sem("cs_mm"), 4 * k + i + 1)
                    neg = C("cmpneg", 32 * i, 32 * i + 32).unsqueeze(1).to_broadcast([128, 4, 32])
                    step(v.tensor_tensor(CM[:, i, 4 * k:4 * k + 4],
                                         PS[:, 4 * k + i, 0:128].rearrange("p (h c) -> p h c", h=4), neg, ALU.add))
            cm = CM.rearrange("p i h c -> p (i h) c")
            step(v.tensor_reduce(nmc, cm, AX, ALU.max, negate=True))
            v.tensor_tensor(cm, cm, bc(nmc, 32), ALU.add).then_inc(once("cm"), 1)
            dve.wait_ge(*done("cm_e"))
            step(v.tensor_reduce(rsc.rearrange("p i h -> p (i h)"), cm, AX, ALU.add))
            v.tensor_tensor(CM, CM, C("cmp01").rearrange("p (i c) -> p i c", i=4).unsqueeze(2)
                            .to_broadcast([128, 4, 8, 32]), ALU.mult).then_inc(once("cp"), 1)
            step(v.reciprocal(rsc, rsc))
            dve.wait_ge(*done("ng"))
            gate = zt[:, :, CG:CG + 24].rearrange("p i (h b) -> p i h b", b=3)
            step(v.tensor_tensor(rsc, rsc, gate[:, 0:4, :, 0], ALU.mult))
            for i in range(TT):
                dve.wait_ge(sem("ct_mm"), i + 1)
                v.tensor_copy(PTC[:, i], PS[:, 2 * (i % 2):2 * (i % 2) + 2, 0:128]).then_inc(sem("ct_ev"), 1)
                dve.wait_ge(sem("co_mm"), i + 1)
                v.tensor_tensor(ON[:, i].rearrange("p (h d) -> p h d", d=HD),
                                PS[:, 4 + i].rearrange("p (h d) -> p h d", d=HD), bc(rsc[:, i], HD), ALU.mult)\
                    .then_inc(sem("co_ev"), 1)
            NU = len(UNITS)
            for u in range(NU + 1):
                if u < NU:
                    i = UNITS[u][0]
                    dve.wait_ge(sem("s_mm"), u + 1)
                    if u >= 3:
                        dve.wait_ge(sem("ex"), u - 2)
                    v.tensor_reduce(nm[u % 3], PS[:, u % 3, 0:128 * i + 128], AX, ALU.max, negate=True)\
                        .then_inc(sem("mx"), 1)
                if u:
                    w = u - 1
                    i = UNITS[w][0]
                    dve.wait_ge(sem("t_mm"), w + 1)
                    if w >= 3:
                        dve.wait_ge(sem("pv_mm"), w - 2)
                    v.tensor_copy(PT[w % 3][:, 0:i + 1].rearrange("p k t -> p (k t)"),
                                  PS[:, 3 + w % 3, 0:128 * i + 128]).then_inc(sem("pt_ev"), 1)
                if u % 16 == 0 and u:
                    i = u // 16 - 1
                    step(v.reciprocal(rs[:, i], rs[:, i]))
                    step(v.tensor_tensor(rs[:, i].rearrange("p b h -> p h b"),
                                         rs[:, i].rearrange("p b h -> p h b"), gate[:, i, :, 1:3], ALU.mult))
                    dve.wait_ge(sem("pv_mm"), u)
                    dve.wait_ge(sem("co_ev"), 4)
                    on = ON[:, i].rearrange("p (h d) -> p h d", d=HD)
                    for b in range(2):
                        t = TQ[:, b].rearrange("p (h d) -> p h d", d=HD)
                        step(v.tensor_tensor(t, PS[:, 6 + b].rearrange("p (h d) -> p h d", d=HD),
                                             bc(rs[:, i, b], HD), ALU.mult))
                        ins = v.tensor_tensor(on, on, t, ALU.add)
                        if b == 0:
                            step(ins)
                        else:
                            ins.then_inc(sem("on"), 1)
            for i in range(TT):
                dve.wait_ge(sem("ont_mm"), i + 1)
                v.tensor_copy(ONT[:, :, 128 * i:128 * i + 128], PS[:, i].rearrange("p (c t) -> p c t", c=4))\
                    .then_inc(sem("ont"), 1)
            dve.wait_ge(sem("rows_out"), 96)
            dve.wait_ge(sem("stored"), 48)
            dve.wait_ge(sem("qt_ev"), 8)
            dve.wait_ge(sem("ont_mm"), 4)
            step(v.memset(QB, 0.0))
            for k in range(HKV):
                r = slice(64 * k, 64 * k + 64)
                step(v.tensor_copy(QB[r, :, 4 * k:4 * k + 4], QT[r, :, L:T].rearrange("p g s -> p s g")))
            v.tensor_copy(KNEW, new).then_inc(once("q_saved"), 1)
            dve.wait_ge(*done("ng"))
            g8 = zt[0:NS, 4, CG:CG + 24].rearrange("p (h b) -> p b h", b=3)
            one = C("onehot", p=NS).rearrange("p (s c) -> p s c", s=NS)[:, :, 0:8]
            for b in range(3):
                ins = v.tensor_tensor(GD[:, b], g8[:, b].unsqueeze(1).to_broadcast([NS, NS, 8]), one, ALU.mult)
                if b < 2:
                    step(ins)
                else:
                    ins.then_inc(once("gd"), 1)
            for x in range(NS + 1):
                if x < NS:
                    dve.wait_ge(sem(f"xs{x % 4}"), 16 * (x // 4 + 1))
                    if x >= 2:
                        dve.wait_ge(sem("sh_mm"), x - 1)
                    v.tensor_reduce(S16[x % 2], X[x % 4].rearrange("p (t c) -> p c t", t=16), AX, ALU.add)\
                        .then_inc(sem("c_red"), 1)
                if x:
                    dve.wait_ge(sem("sh_mm"), x)
                    v.tensor_copy(CX[(x - 1) // 4][:, (x - 1) % 4], PS[0:NCMP, x - 1, 0:256]).then_inc(sem("sh_ev"), 1)
            dve.wait_ge(sem("sh_ev"), 8)
            for u in range(2):
                sq = SQX[:, 512 * u:512 * u + 512].rearrange("p (s c) -> p s c", s=4)
                step(v.tensor_tensor(sq, CX[u][:, :, 0:128], CX[u][:, :, 0:128], ALU.mult))
            v.tensor_reduce(KST, SQX.rearrange("p (s k d) -> p s k d", s=NS, k=2), AX, ALU.add)\
                .then_inc(once("kst_x"), 1)
            dve.wait_ge(*done("kst_xr"))
            for u in range(2):
                ck = CX[u][:, :, 0:128].rearrange("p s (k d) -> p s k d", d=HD)
                step(v.tensor_tensor(ck, ck, bc(KST[:, 4 * u:4 * u + 4], HD), ALU.mult))
                gain = V("kg", 0, 64, NCMP).unsqueeze(1).unsqueeze(1).to_broadcast([NCMP, 4, 2, HD])
                ins = v.tensor_tensor(ck, ck, gain, ALU.mult)
                if u == 0:
                    step(ins)
                else:
                    ins.then_inc(once("cx"), 1)
            for u in range(2):
                dve.wait_ge(sem("kx_mm"), u + 1)
                v.tensor_copy(KCT[:, 4 * u:4 * u + 4].rearrange("p s c -> p (s c)"), PS[:, u, 0:4 * NCMP])\
                    .then_inc(sem("kx_ev"), 1)
            dve.wait_ge(*done("cxs_mm"))
            v.tensor_copy(PCT, PS[0:NCMP, 2, 0:64]).then_inc(once("cxs"), 1)
            dve.wait_ge(*done("cxt_mm"))
            v.tensor_reduce(CMAX[:, 0:1], PS[0:64, 3, 0:NCMP], AX, ALU.max, negate=True).then_inc(once("cxm"), 1)
            dve.wait_ge(*done("cxe"))
            step(v.reciprocal(CMAX[:, 2:3], CMAX[:, 1:2]))
            v.tensor_scalar(PCR, PCR, CMAX[:, 2:3], None, ALU.mult).then_inc(once("cxp"), 1)
            dve.wait_ge(*done("cxp_mm"))
            v.tensor_copy(PCT, PS[0:NCMP, 4, 0:64]).then_inc(once("pct"), 1)
            dve.wait_ge(*done("pct"))
            v.tensor_reduce(PCG, PCT.rearrange("p (n g) -> p n g", g=G), AX, ALU.add).then_inc(once("pcg"), 1)
            dve.wait_ge(*done("gb_mm"))
            v.tensor_copy(GB.rearrange("p b n -> p (b n)"), PS[:, 6, 0:192]).then_inc(once("gb"), 1)
            dve.wait_ge(*done("gb"))
            dve.wait_ge(*done("cxo_mm"))
            v.tensor_tensor(OACC, PS[:, 5, 0:64], GB[:, 0], ALU.mult).then_inc(sem("oacc"), 1)
            dve.wait_ge(*done("imp_mm"))
            step(v.tensor_tensor(SCO, PS[0:16, 7, 0:NSEL], C("bonus", p=16), ALU.add))
            sq3 = [16, NSEL, NSEL]
            by_m = lambda a: a.unsqueeze(1).to_broadcast(sq3)
            num = C("number", p=16)
            step(v.tensor_tensor(T1, by_m(SCO), bc(SCO, NSEL), ALU.is_gt))
            step(v.tensor_tensor(T2, by_m(SCO), bc(SCO, NSEL), ALU.is_equal))
            step(v.tensor_tensor(T3, by_m(num), bc(num, NSEL), ALU.is_lt))
            step(v.tensor_tensor(T2, T2, T3, ALU.mult))
            step(v.tensor_tensor(T1, T1, T2, ALU.add))
            step(v.tensor_reduce(RANK, T1, AX, ALU.add))
            v.tensor_scalar(RANK, RANK, float(TOPK), None, ALU.is_lt).then_inc(once("rank"), 1)
            dve.wait_ge(*done("sel_mm"))
            v.tensor_copy(SELT, PS[0:NSEL, 0, 0:16]).then_inc(once("selt"), 1)
            dve.wait_ge(*done("bs_mm"))
            v.tensor_scalar(BS.rearrange("p s k -> p (s k)"), PS[:, 1, 0:16], -1.0, -NEG, ALU.add, ALU.mult)\
                .then_inc(once("bs"), 1)
            for b in range(2):
                dve.wait_ge(sem("sn_mm"), b + 1)
                v.tensor_tensor(SN[b], PS[0:NS, 2 + b, 0:64], C("newmask", p=NS), ALU.add).then_inc(sem("sn"), 1)
            dve.wait_ge(sem("sn"), 2)
            dve.wait_ge(*done("bs"))
            kt = 0
            for n, (b, s0) in enumerate(ROUNDS):
                per = 4 if b == 0 else 1
                ni = 4 * per
                if n:
                    dve.wait_ge(sem("sv_mm"), n)
                for x in range(s0, s0 + 4):
                    m = 4 * n + x - s0
                    for q in range(per):
                        dve.wait_ge(sem("ktx_mm"), kt + q + 1)
                        if kt + q >= 4:
                            dve.wait_ge(sem("sx_mm"), kt + q - 3)
                        at = 4 * ((kt + q) % 4)
                        v.tensor_copy(KTX[:, at:at + 4].rearrange("p i t -> p (i t)"), PS[:, (kt + q) % 4])\
                            .then_inc(sem("ktx"), 1)
                    kt += per
                    dve.wait_ge(sem("sx_mm"), kt)
                    ps = PS[:, 4 + m % 2, 0:8 * ni]
                    if b == 0:
                        bias = BS[:, x].unsqueeze(1).unsqueeze(3).to_broadcast([128, 16, 2, 4])
                        v.tensor_tensor(SX[:, x - s0].rearrange("p i (k g) -> p i k g", k=2),
                                        ps.rearrange("p (i k g) -> p i k g", k=2, g=4), bias, ALU.add)\
                            .then_inc(sem("sx"), 1)
                    else:
                        v.tensor_copy(SX[:, x - s0, 0:ni].rearrange("p i h -> p (i h)"), ps).then_inc(sem("sx"), 1)
                dve.wait_ge(sem("sx"), 4 * n + 4)
                m1 = M1.rearrange("p (s h) -> p s h", s=4)
                v.tensor_reduce(m1, SX[:, :, 0:ni].rearrange("p s i h -> p s h i"), AX, ALU.max).then_inc(sem("m1"), 1)
                dve.wait_ge(sem("mt_mm"), n + 1)
                step(v.tensor_reduce(SM, PS[0:32, 6, 0:136], AX, ALU.max))
                v.tensor_scalar(DG, ident[0:32, 0:32], SM, None, ALU.mult).then_inc(sem("dg"), 1)
                dve.wait_ge(sem("mb_mm"), n + 1)
                mb = PS[:, 6, 0:32]
                v.tensor_tensor(SX[:, :, 0:ni], SX[:, :, 0:ni],
                                mb.rearrange("p (s h) -> p s h", s=4).unsqueeze(2).to_broadcast([128, 4, ni, 8]),
                                ALU.subtract).then_inc(sem("sxs"), 1)
                new = SN[b][:, 8 * s0:8 * s0 + 32]
                v.tensor_tensor(new, new, mb[0:NS], ALU.subtract).then_inc(sem("sxm"), 1)
                dve.wait_ge(sem("sxe"), 2 * n + 2)
                v.tensor_reduce(m1, SX[:, :, 0:ni].rearrange("p s i h -> p s h i"), AX, ALU.add).then_inc(sem("r1"), 1)
                dve.wait_ge(sem("sum_mm"), n + 1)
                step(v.reciprocal(COEF, PS[:, 6, 64:96]))
                step(v.tensor_tensor(COEF, COEF, GB[:, 1 + b, 8 * s0:8 * s0 + 32], ALU.mult))
                dve.wait_ge(sem("sv_mm"), n + 1)
                step(v.tensor_tensor(OT[:, 0:32], PS[:, 7, 0:32], COEF, ALU.mult))
                v.tensor_tensor(OACC[:, 8 * s0:8 * s0 + 32], OACC[:, 8 * s0:8 * s0 + 32], OT[:, 0:32], ALU.add)\
                    .then_inc(sem("oacc"), 1)
            dve.wait_ge(sem("oacc"), 5)
            oa = OACC.rearrange("p (s k j q) -> p k q j s", k=2, j=2, q=2)
            for k in range(2):
                for q in range(2):
                    ins = v.tensor_copy(ONT[64 * q:64 * q + 64, 2 * k:2 * k + 2, L:T], oa[64 * k:64 * k + 64, k, q])
                    if k + q < 2:
                        step(ins)
                    else:
                        ins.then_inc(once("nsa_done"), 1)


            v.memset(mixT, 0.0).then_inc(once("mix_zero"), 1)
            dve.wait_ge(*done("mix_zero"))
            with dve.Fori(0, 2) as hf:
                with dve.Fori(0, 2) as bp:
                    for s in range(2):
                        for j in range(4):
                            n = hf * 16 + bp * 8 + 4 * s + j
                            dve.wait_ge(sem("sg"), n + 1)
                            v.tensor_tensor(halves(SG[2]), pair(4 * (j % 2) + 2), halves(SG[j % 2]), ALU.mult)\
                                .then_inc(sem("mix_mul"), 1)
                            dve.wait_ge(sem("mix_mul"), n + 1)
                            m = mixT[:, bass.ds(hf * 4 + j, 1)].rearrange("p k t -> p (k t)")
                            v.tensor_tensor(m, m, SG[2], ALU.add).then_inc(sem("mix_free"), 1)
                            dve.wait_ge(sem("mix_free"), n + 3)
            for n in range(8):
                dve.wait_ge(sem("prod"), 79 + n)
                v.tensor_tensor(halves(xT[:, n]), halves(xT[:, n]), pair(2 * (n % 4)), ALU.add)\
                    .then_inc(sem("wo_ev"), 1)
            dve.wait_ge(sem("wo_ev"), 8)
            norm_apply("n2", "n2")
            with dve.Fori(0, 4) as i:
                for s in range(2):
                    for j in range(4):
                        n = i * 8 + 4 * s + j
                        dve.wait_ge(sem("u_free"), n + 5)
                        u = uT[:, bass.ds(n, 1)].rearrange("p k t -> p (k t)")
                        v.tensor_tensor(u, u, u, ALU.mult).then_inc(sem("u_ev"), 1)
            with dve.Fori(0, 4) as i:
                for s in range(2):
                    dve.wait_ge(sem("prod"), i * 2 + s + 119)
                    x = halves(xT[:, bass.ds(i * 2 + s, 1)].rearrange("p k t -> p (k t)"))
                    v.tensor_tensor(x, x, pair(4 * s), ALU.add).then_inc(sem("y_free"), 1)
            for n in range(10):
                w = 128 if n < 8 else NS
                dve.wait_ge(sem("yt_mm"), n + 1)
                v.tensor_copy(YT[0:w, n // 2, 512 * (n % 2):512 * (n % 2) + 512], PS[0:w, n % 8])\
                    .then_inc(sem("y_ev"), 1)

        @block.gpsimd
        def _(gp):
            p = nc.gpsimd
            step = steps(gp, "pool_step")
            p.memset(zt[:, 4, :], 0.0).then_inc(sem("zt_zero"), 1)
            gp.wait_ge(sem("cum"), 4)
            gp.wait_ge(*done("q_act"))
            gp.wait_ge(*done("fg"))
            for lev in range(LEVELS):
                half = 1 << lev
                if lev >= 2:
                    gp.wait_ge(sem("a_ready"), 2 * lev - 2)
                blk = lambda ap: ap.rearrange("p (n q h) -> p n q h", q=2, h=half)
                b, e = blk(B), blk(EL[lev % 2])
                mid = b[:, :, 0, half - 1:half].to_broadcast([128, 2048 // (2 * half), half])
                p.tensor_tensor(e[:, :, 0], mid, b[:, :, 0], ALU.subtract).then_inc(sem("dist"), 1)
                p.tensor_tensor(e[:, :, 1], b[:, :, 1], mid, ALU.subtract).then_inc(sem("dist"), 1)
            gp.wait_ge(sem("a_ready"), 2 * LEVELS)
            b = B.rearrange("p (n t) -> p n t", t=128)
            p.tensor_tensor(E0.rearrange("p (n t) -> p n t", t=128), b[:, :, 127:128].to_broadcast([128, 16, 128]),
                            b, ALU.subtract).then_inc(sem("dist"), 1)

            gp.wait_ge(sem("ss_done"), 8)
            gp.wait_ge(sem("st_out"), 128)
            for w in WP:
                step(p.memset(w[:, :, 0:HIST], 0.0))
            step(p.tensor_copy(WP[0][:, :, HIST:], zf[:, ZU:ZU + 4, 0:L]))
            for n in range(4):
                src, dst, sh = WP[n % 2], WP[1 - n % 2], 1 << n
                step(p.tensor_tensor(dst[:, n:4, HIST:], src[:, n:4, HIST:], src[:, n:4, HIST - sh:HIST + L - sh],
                                     ALU.add))
            for g in range(4):
                first = WP[(1, 0, 1, 0)[g]][:, g, HIST:HIST + 16]
                ins = p.tensor_tensor(first, first, C("corr", 16 * g, 16 * g + 16), ALU.mult)
                if g < 3:
                    step(ins)
                else:
                    ins.then_inc(sem("win"), 1)
            row = lambda name: A[name].rearrange("o n (r t) a k d -> (o n r) (t a k d)", t=16)
            gp.wait_ge(*done("idx"))
            gp.wait_ge(sem("on"), 4)
            gp.wait_ge(sem("pd"), 8)
            gp.wait_ge(*done("q_saved"))
            for n in range(2 * NS):
                if 4 <= n < 12:
                    gp.wait_ge(sem("c_red"), n - 3)
                if n >= 12:
                    gp.wait_ge(sem("sv_mm"), 1)
                p.indirect_dma_start(X[n % 4], None, row("cache_cmp_kv" if n < NS else "cache_slc_kv"),
                                     bass.IndirectOffsetOnAxis(idx[:, NS + n % NS:NS + n % NS + 1], 0))\
                    .then_inc(sem(f"xs{n % 4}"), 16)


NAMES = ["x_prompt", "x_sample", "state_gla", "state_hgrn", "state_pool", "cache_cmp_kv", "cache_slc_kv",
         "cache_win_kv", "gla_wa2", "pool_w", "w_branch", "w_gate", "w_out", "mlp_w1", "mlp_w2"]
OUTS = [("y_prompt", (1, 512, 1024)), ("y_sample", (8, 1, 1024)), ("gla_prompt", (1, 1, 4, 64, 128)),
        ("gla_sample", (1, 8, 4, 64, 128)), ("hgrn_prompt", (1, 1, 4, 64, 128)), ("hgrn_sample", (1, 8, 4, 64, 128)),
        ("pool_prompt", (1, 1, 15, 512)), ("pool_sample", (1, 8, 15, 512)),
        ("cmp_rows_prompt", (1, 1, 512, 2, 2, 64)), ("cmp_rows_sample", (1, 8, 1, 2, 2, 64)),
        ("slc_rows_prompt", (1, 1, 512, 2, 2, 64)), ("slc_rows_sample", (1, 8, 1, 2, 2, 64)),
        ("win_rows_prompt", (1, 1, 512, 2, 2, 64)), ("win_rows_sample", (1, 8, 1, 2, 2, 64))]


def kernel(**inputs):
    import concourse.bacc as bacc
    from concourse.bass_utils import run_bass_kernel_spmd

    a = {k: np.asarray(v) for k, v in inputs.items()}
    arrays = {n: np.ascontiguousarray(a[n]) for n in NAMES}
    w = a["w_in"][0]
    sizes = (256, 256, 512, 512, 16, 256, 256, 512, 512, 512, 512, 128, 128, 128, 128, 128, 128, 24)
    at = np.cumsum((0,) + sizes)
    gq, gk, gv, gr, ga, hq, hf, hi, hg, pu, nq, ck, cv, sk, sv, wk, wv, ng = (
        slice(at[i], at[i + 1]) for i in range(len(sizes)))
    order = (gr, hg, pu, gq, hq, gk, hf, gv, hi, nq, ck, cv, sk, sv, wk, wv, ng, ga)
    arrays["w_in"] = np.ascontiguousarray(np.concatenate([w[:, o] for o in order], 1))
    cols = lambda v, k: v.reshape(k, 128).T
    rows = lambda v: np.broadcast_to(v.reshape(1, -1), (128, v.size))
    arrays["vectors"] = np.ascontiguousarray(np.concatenate([
        cols(a["norm1_g"][0], 8), cols(a["norm2_g"][0], 8), cols(a["b_gate"][0], 32), cols(a["pool_scale"][0], 4),
        cols(a["gla_ba"][0], 2), cols(a["hgrn_lb_param"][0], 2), cols(a["gla_norm_g"][0], 1),
        cols(a["hgrn_norm_g"][0], 1), rows(a["nsa_q_norm_g"][0]), rows(a["nsa_k_norm_g"][0]),
        (np.arange(128) % 8).astype(np.float32)[:, None]], 1))
    arrays["tables"] = constants()[0]
    arrays["pages"] = np.ascontiguousarray(np.repeat(a["page_table"].T, 8, axis=0))

    nc = bacc.Bacc("TRN2", target_bir_lowering=False, num_devices=1)
    A = {n: nc.dram_tensor(n, x.shape, mybir.dt.from_np(x.dtype), kind="ExternalInput").ap()
         for n, x in arrays.items()}
    for n, shape in OUTS:
        A[n] = nc.dram_tensor(n, shape, mybir.dt.float32, kind="ExternalOutput").ap()
    build(nc, A)
    r = run_bass_kernel_spmd(nc, [arrays], core_ids=[0])
    return tuple(r.results[0][n] for n, _ in OUTS)
```

```python
import concourse.bass as bass
from concourse import mybir
from contextlib import ExitStack
import numpy as np

D, L, NS, T = 1024, 512, 8, 520
HALF = T // 2
KT = D // 128
TT = 4
FM, TM, GA = 2560, 2328, 16
CHUNK = 256
HKV, HD, G = 2, 64, 4
PAGES, PAGE = 16, 128
NCMP, NSEL, TOPK = 127, 33, 16
NEG = -1e30
EPS = 1e-6
LEVELS = 7
WINDOWS = (2, 4, 8, 16)
HIST = 15

CV, CQ, CK, CS, CW, CG = 0, 1024, 1536, 1792, 2048, 2304
ZG, ZU, ZQ, ZK = 0, 8, 12, 16


def constants():
    p = np.arange(128)
    parts = {}

    def put(name, a):
        full = np.zeros((128, a.shape[1]), np.float32)
        full[:a.shape[0]] = a
        parts[name] = full

    put("ident", np.eye(128))
    put("ones", np.ones((128, 128)))
    put("causal", np.where(p[None, :] <= p[:, None], 0.0, NEG))
    masks = []
    for lev in range(LEVELS):
        half = 1 << lev
        same = (p[:, None] // (2 * half)) == (p[None, :] // (2 * half))
        masks.append(same & (p[:, None] % (2 * half) < half) & (p[None, :] % (2 * half) >= half))
    masks.append(np.eye(128, dtype=bool))
    put("masks", np.concatenate(masks, 1).astype(np.float32))
    tok = np.arange(L)[:, None]
    c32 = np.arange(32)[None, :]
    pm = ((tok >= 16 * c32) & (tok < 16 * c32 + 32) & (c32 < 31)) / 32.0
    put("pool", pm.reshape(TT, 128, 32).transpose(1, 0, 2).reshape(128, TT * 32))
    c = np.arange(128)[None, :]
    put("shift", np.where((p[:, None] == c) | (p[:, None] == c + 1), 1 / 32.0, 0.0))
    n = np.arange(NSEL)[None, :]
    put("overlap", ((p[:NCMP, None] // 4 == n) | ((p[:NCMP, None] + 1) // 4 == n)).astype(np.float32))
    put("expand", (np.arange(NSEL)[:, None] == p[None, :] // 4).astype(np.float32))
    seen = ((16 * c32 + 31 <= tok) & (c32 < 31)).astype(np.float32)
    seen = seen.reshape(TT, 128, 32).transpose(1, 0, 2).reshape(128, TT * 32)
    put("cmp01", seen)
    put("cmpneg", np.where(seen > 0, 0.0, NEG))
    t16 = np.arange(16)
    put("corr", np.tile(np.concatenate([w / np.minimum(w, t16 + 1.0) for w in WINDOWS]), (128, 1)))
    put("newmask", np.where(np.arange(NS)[:, None] == np.arange(64)[None, :] // 8, 0.0, NEG))
    put("onehot", np.repeat(np.eye(NS), 64, 1))
    bonus = np.zeros((16, NSEL))
    bonus[:, [0, NSEL - 2, NSEL - 1]] = 1000.0
    put("bonus", bonus)
    put("number", np.tile(np.arange(NSEL, dtype=np.float32), (16, 1)))
    put("reset", np.tile((np.arange(L) % 128 != 0).astype(np.float32), (128, 1)))
    off, at = {}, 0
    for k, a in parts.items():
        off[k] = (at, at + a.shape[1])
        at += a.shape[1]
    return np.concatenate(list(parts.values()), 1), off


EVENTS = {
    "pe_event": """la_mm os_mm hist_mm tail_mm ckv_mm kct_mm cxs_mm cxt_mm cxp_mm cxo_mm gb_mm imp_mm sel_mm
           bs_mm""".split(),
    "act_event": """lsp lb_e lf_h decs decc ng rq kst_rs cm_e kst_xr cxe""".split(),
    "dve_event": """eps idx ga_ev q_act lb_d fg lf_g qk kdec qdec tail k_norm q_norm kst ckv kct cm cp gd
           kst_x cx cxs cxm cxp pcg rank selt bs nsa_done""".split(),
}


UNITS_OF = [2] * 10 + [1] + [5] * 10 + [2, 2, 4] * 8 + [2] * 4 + [2] * 32
N_MIX, N_OUT, N_MLP = 21, 45, 49


def units_before(n):
    return sum(UNITS_OF[:n])


SMALL = {}
for _n, _k in (("n1", 8), ("n2", 8), ("bg", 32), ("psc", 4), ("ba", 2), ("lb", 2), ("gn", 1), ("hn", 1),
               ("qg", 64), ("kg", 192), ("r8", 1)):
    SMALL[_n] = (sum(b - a for a, b in SMALL.values()), sum(b - a for a, b in SMALL.values()) + _k)
NSMALL = SMALL["r8"][1]
NCON = constants()[0].shape[1]


def build(nc, A):
    f32, f32r, i32 = mybir.dt.float32, mybir.dt.float32r, mybir.dt.int32
    ACT, ALU, AX = mybir.ActivationFunctionType, mybir.AluOpType, mybir.AxisListType.X
    _, COFF = constants()
    ctx = ExitStack()
    with ctx:
        def sb(name, n, dt=f32):
            return ctx.enter_context(nc.sbuf_tensor(name, [128, n], dt))

        con = sb("con", NCON)
        small = sb("small", NSMALL)
        xT = sb("xT", KT * T)[:].rearrange("p (k t) -> p k t", t=T)
        stat = sb("stat", 400)
        eps = stat[:, 396:397]
        idx = sb("idx", 2 * NS, i32)
        gaT = sb("gaT", T)
        wa2 = sb("wa2", 256)
        tmp = sb("tmp", 3 * T)
        RST, TH = tmp[:, 0:T], [tmp[:, T * i:T * (i + 1)] for i in (1, 2)]
        ZW = 20 * T + 5 * TM
        W0 = ZW + 2 * KT * T

        def place(name, at, n, dt=f32r):
            with ExitStack() as below:
                if at:
                    below.enter_context(nc.sbuf_tensor(name + "_below", [128, at], f32))
                return below.enter_context(nc.sbuf_tensor(name, [128, n], dt))[:]

        def parts(name, at, tiles):
            return place(name, at, tiles * T).rearrange("p (k t) -> p k t", t=T)

        hH, hL = parts("hH", ZW, KT), parts("hL", ZW + KT * T, KT)
        bL = [parts(f"bL{b}", 4 * b * T, 4) for b in range(4)]
        bH = [parts(f"bH{b}", (16 + 4 * b) * T, 4) for b in range(4)]
        mL, mH = parts("mL", 32 * T, KT), parts("mH", 16 * T, KT)
        uH, uL = parts("uH", 0, 16), parts("uL", 16 * T, 16)
        slot = lambda ap: ap.rearrange("p (k n) -> p k n", k=KT)
        WL, WH = [[slot(place(f"{name}{i}", W0 + at + 2048 * i, 2048)) for i in range(2)]
                  for name, at in (("WL", 0), ("WH", 4096))]
        M = sb("M", W0 + 12288)
        WR = [slot(M[:, W0 + 8192 + 2048 * i:W0 + 8192 + 2048 * (i + 1)]) for i in range(2)]
        Z = M[:, 0:ZW]
        zf = Z[:, 0:20 * T].rearrange("p (k t) -> p k t", t=T)
        zt = Z[:, 20 * T:].rearrange("p (i c) -> p i c", c=TM)
        R = M[:, ZW:W0 + 12288]
        PS = ctx.enter_context(nc.psum_tensor("PS", [128, 8, 512], f32))

        def C(name, a=0, b=None, p=128):
            lo, hi = COFF[name]
            return con[0:p, lo + a:(hi if b is None else lo + b)]

        def V(name, a=0, b=None, p=128):
            lo, hi = SMALL[name]
            return small[0:p, lo + a:(hi if b is None else lo + b)]

        ident, ones = C("ident"), C("ones")
        S = {}

        def sem(name):
            if name not in S:
                S[name] = ctx.enter_context(nc.semaphore(name))
            return S[name]

        signalled = {e: 0 for e in EVENTS}

        def once(name):
            e = [e for e in EVENTS if name in EVENTS[e]][0]
            assert EVENTS[e][signalled[e]] == name, name
            signalled[e] += 1
            return sem(e)

        def done(name):
            e = [e for e in EVENTS if name in EVENTS[e]][0]
            return sem(e), EVENTS[e].index(name) + 1

        def steps(eng, name):
            own, n = sem(name), [0]

            def step(ins):
                n[0] += 1
                ins.then_inc(own, 1)
                eng.wait_ge(own, n[0])
            return step

        def pair(bank):
            return PS[:, bank:bank + 2, 0:HALF]

        def halves(ap):
            return ap.rearrange("p (h n) -> p h n", h=2)

        def bc(ap, n):
            return ap.unsqueeze(len(ap.shape)).to_broadcast(list(ap.shape) + [n])


        LF = R[:, 0:4 * T].rearrange("p (k t) -> p k t", t=T)
        KD = R[:, 0:2048].rearrange("p (c k f) -> p c k f", c=4, k=4)
        B = R[:, 2080:4128]
        E0 = R[:, 4160:6208]
        A0 = R[:, 6240:8288]
        A1 = R[:, 12416:14464]
        E1 = R[:, 14464:16512]
        AL, EL = [A0, A1], [E0, E1]
        SIGQ = R[:, 4160:5200].rearrange("p (k t) -> p k t", t=T)
        SIGF = R[:, 5200:6240].rearrange("p (k t) -> p k t", t=T)
        TMPA = R[:, 6240:7280].rearrange("p (k t) -> p k t", t=T)
        SIGG = R[:, 8320:8320 + 8 * T].rearrange("p (k t) -> p k t", t=T)
        SC = R[:, 8320:12416].rearrange("p (g k t) -> p g k t", g=8, k=4)
        ST = R[:, 12416:14464].rearrange("p (c k v) -> p c k v", c=4, k=4)
        OB = R[:, 4160:4160 + 8 * T].rearrange("p (k t) -> p k t", t=T)
        SS = R[:, 8320:12416].rearrange("p (m s k v) -> p m s k v", m=2, s=NS, k=2)
        VB = [R[:, 14464 + 512 * i:14464 + 512 * (i + 1)].rearrange("p (s k v) -> p s k v", s=2, k=2)
              for i in range(2)]
        SQ = [zf[:, ZK + i] for i in range(2)]
        RN = [zf[:, ZK + 2 + i] for i in range(2)]
        decS = stat[:, 0:32].rearrange("p (k s) -> p k s", k=4)
        decC = stat[:, 32:48].rearrange("p (k c) -> p k c", k=4)
        lbv = stat[:, 48:60].rearrange("p (k a) -> p k a", k=2)
        gq8 = stat[:, 60:124]

        def flat(ap):
            return ap.rearrange("p a b -> p (a b)")

        def chunks(buf):
            return buf.rearrange("p (k t) -> p k t", k=4)

        def head_cols(k, par):
            h = (k // 2) * 4 + (k % 2) * 2 + par
            return slice(CV + 128 * h, CV + 128 * (h + 1)), h

        w_in = A["w_in"].rearrange("(k p) n -> p k n", p=128)
        w_gate = A["w_gate"].rearrange("o (k p) n -> p (o k) n", p=128)
        w_branch = A["w_branch"].rearrange("o b (c p) n -> p (o b c) n", p=128)
        w_out = A["w_out"].rearrange("o (k p) n -> p (o k) n", p=128)
        w1 = A["mlp_w1"].rearrange("o (k p) n -> p (o k) n", p=128)
        w2 = A["mlp_w2"].rearrange("o (k p) n -> p (o k) n", p=128)
        mixT = M[:, 32 * T:40 * T].rearrange("p (k t) -> p k t", t=T)
        SG = [M[:, 40 * T + T * i:40 * T + T * (i + 1)] for i in range(2)] + [RST, TH[0]]
        GP = TH[1]
        UR = [M[:, 32 * T + T * i:32 * T + T * (i + 1)] for i in range(2)]
        US = TH
        YT = Z[:, 0:5120].rearrange("p (i d) -> p i d", i=5)
        XI = Z[:, 0:5120].rearrange("p (i d) -> p i d", i=5)


        WP = [R[:, a:a + n * (HIST + L)].rearrange("p (g t) -> p g t", g=n)
              for a, n in ((16512, 4), (18624, 3))]
        WIN = [WP[0][:, 0], WP[1][:, 0], WP[0][:, 2], WP[1][:, 2]]
        poolw = zt[:, 0:4, 0:128]
        hist = zt[0:NS * HIST, 0:4, 128:256]
        tail = zt[0:23, 0:4, 256:384]
        PD = zt[:, 0:4, 504:1024]

        TQ = R[:, 0:2560].rearrange("p (i c) -> p i c", i=5)
        QN = R[:, 2560:5120].rearrange("p (i g k d) -> p i g k d", i=5, g=G, k=HKV)
        TK = R[:, 2560:3840].rearrange("p (i c) -> p i c", i=5)
        QT = R[:, 5120:7200].rearrange("p (g t) -> p g t", t=T)
        KTS, KTW = R[:, 7200:7720], R[:, 7720:8240]
        P = [R[:, 8240 + 512 * i:8752 + 512 * i] for i in range(3)]
        PT = [R[:, 9776 + 512 * i:10288 + 512 * i].rearrange("p (k t) -> p k t", k=4) for i in range(3)]
        PTC = R[:, 8240:9264].rearrange("p (i k t) -> p i k t", i=4, k=2)
        CM = R[:, 11312:12336].rearrange("p (i h c) -> p i h c", i=4, h=8)
        CKV = gaT[0:32, 0:256]
        VBK = zf[:, ZK, 0:512].rearrange("p (k c) -> p k c", k=2)
        ON = zt[:, :, 1024:1536]
        ONT = zf[:, ZQ:ZQ + 4]
        rq = stat[:, 128:188].rearrange("p (i h) -> p i h", i=5)
        kcT = stat[:, 188:220]
        nmc = stat[:, 220:252]
        rsc = stat[:, 252:284].rearrange("p (i h) -> p i h", i=4)
        nm = [stat[:, 284 + i:285 + i] for i in range(3)]
        rs = stat[:, 288:352].rearrange("p (i b h) -> p i b h", i=4, b=2)
        kst = stat[0:32, 352:360]

        KTX = zf[:, ZK:ZK + 4].rearrange("p a b -> p (a b)")[:, 0:2048].rearrange("p (i t) -> p i t", i=16)
        KCT = zt[:, 0, 0:8 * NCMP].rearrange("p (s c) -> p s c", s=NS)
        S16 = [zt[:, 3 * (x < 4), 256 * (x % 4):256 * (x % 4) + 256] for x in range(NS)]
        Y = [R[:, 12416 + 4096 * i:12416 + 4096 * (i + 1)] for i in range(2)]
        X = [R[:, 4096 * i:4096 * (i + 1)] for i in range(4)] + [Y[1]]
        XS = [X[x % 5] for x in range(NS)]
        CX = [zt[0:NCMP, 1 + u, 0:1024].rearrange("p (s c) -> p s c", s=4) for u in range(2)]
        SX = zt[:, 3, 0:512].rearrange("p (s i h) -> p s i h", s=4, h=8)
        QB = zt[:, 4, 0:64].rearrange("p (s h) -> p s h", h=8)
        KNEW = zt[:, 4, 64:80].rearrange("p (b s) -> p b s", b=2)
        GB = zt[:, 4, 80:272].rearrange("p (b n) -> p b n", b=3)
        OACC = zt[:, 4, 272:336]
        BS = zt[:, 4, 336:352].rearrange("p (s k) -> p s k", k=2)
        PCR = zt[0:64, 4, 352:479]
        PCT = gaT[0:NCMP, 0:64]
        PCG = gaT[0:NCMP, 64:80]
        SN = [gaT[0:NS, 80 + 64 * b:144 + 64 * b] for b in range(2)]
        M1 = gaT[:, 208:240]
        DG = gaT[0:32, 240:272]
        COEF = gaT[:, 272:304]
        GD = gaT[0:NS, 304:496].rearrange("p (b s h) -> p b s h", b=3, h=8)
        SELT = gaT[0:NSEL, 496:512]
        OT = stat[:, 128:192]
        SO = zt[0:8, 4, 480:992]
        SCO = stat[0:16, 192:225]
        RANK = stat[0:16, 225:258]
        CMAX = stat[0:64, 258:261]
        KST = stat[0:NCMP, 261:277].rearrange("p (s k) -> p s k", k=2)
        SM = stat[0:32, 277:278]
        SQX = zf[:, ZK:ZK + 4].rearrange("p a b -> p (a b)")[0:NCMP, 0:1024]
        T1 = zf[:, ZK:ZK + 4].rearrange("p a b -> p (a b)")[0:16, 0:NSEL * NSEL].rearrange("p (n m) -> p n m", m=NSEL)
        T2 = zt[0:16, 4, 440:440 + NSEL * NSEL].rearrange("p (n m) -> p n m", m=NSEL)
        T3 = con[0:16, COFF["masks"][0]:COFF["masks"][0] + NSEL * NSEL].rearrange("p (n m) -> p n m", m=NSEL)
        ROUNDS = [(1, 0), (1, 4), (0, 0), (0, 4)]

        def xtile(b, s, i):
            if b == 0:
                t = XS[s][:, 256 * i:256 * i + 256]
            else:
                t = Y[s // 4][:, 1024 * (s % 4) + 256 * i:1024 * (s % 4) + 256 * i + 256]
            return t[:, 0:128], t[:, 128:256]

        SQN = TH

        block = ctx.enter_context(nc.Block())
        UNITS = [(i, b, h) for i in range(TT) for b in range(2) for h in range(8)]

        @block.sync
        def _(sp):
            sp.dma_start(con[:], A["tables"]).then_inc(sem("ld_con"), 16)
            sp.dma_start(small[:], A["vectors"]).then_inc(sem("ld_con"), 16)
            for i in range(TT):
                sp.dma_start(XI[:, i], A["x_prompt"][0, 128 * i:128 * (i + 1), :]).then_inc(sem("ld_x"), 16)
            sp.dma_start(XI[0:NS, 4], A["x_sample"].rearrange("s o d -> (s o) d")).then_inc(sem("ld_x"), 16)
            sp.dma_start(wa2[0:GA, :], A["gla_wa2"][0]).then_inc(sem("ld_wa2"), 16)
            sp.dma_start(idx[:, 0:NS], A["pages"]).then_inc(sem("ld_idx"), 16)
            def load(n, src, cols=CHUNK):
                sp.dma_start(WR[n % 2][:, :, 0:cols], src).then_inc(sem(f"raw{n % 2}"), 16)

            def reload(first, i, src):
                sp.wait_ge(sem("w_lo"), i * 2 + first - 1)
                load(first, src)

            load(0, w_in[:, :, 0:CHUNK])
            load(1, w_in[:, :, CHUNK:2 * CHUNK])
            with sp.Fori(0, 4) as i:
                for u in range(2):
                    reload(2 + u, i, w_in[:, :, bass.ds(i * 512 + 512 + 256 * u, CHUNK)])
            sp.wait_ge(sem("w_lo"), 9)
            load(10, w_in[:, :, FM:FM + 128], 128)
            sp.wait_ge(sem("w_lo"), 10)
            load(11, w_in[:, :, FM + GA:FM + GA + CHUNK])
            with sp.Fori(0, 4) as i:
                for u in range(2):
                    reload(12 + u, i, w_in[:, :, bass.ds(i * 512 + FM + GA + 256 + 256 * u, CHUNK)])
            sp.wait_ge(sem("w_lo"), 19)
            load(20, w_in[:, :, FM + GA + 9 * CHUNK:FM + GA + TM], 24)
            sp.wait_ge(sem("o_mm"), 8)
            for m, name in enumerate(("state_gla", "state_hgrn")):
                src = A[name].rearrange("o s (k q) f v -> q f (o s) k v", q=2)
                for q in range(2):
                    sp.dma_start(SS[64 * q:64 * q + 64, m], src[q]).then_inc(sem("ld_ss"), 16)
            for g in range(4):
                sp.dma_start(poolw[:, g], A["pool_w"][0, g]).then_inc(sem("ld_pool"), 16)
            sp.dma_start(hist, A["state_pool"].rearrange("o s j (g c) -> (o s j) g c", g=4))\
              .then_inc(sem("ld_pool"), 16)
            sp.dma_start(A["pool_sample"][0, :, 0:HIST - 1], A["state_pool"][0, :, 1:HIST])\
              .then_inc(sem("stored"), 16)
            sp.wait_ge(sem("st"), 4)
            for m, name in enumerate(("gla_prompt", "hgrn_prompt")):
                dst = A[name].rearrange("o b (k q) f v -> q f (o b k) v", q=2)
                for q in range(2):
                    sp.dma_start(dst[q], ST[64 * q:64 * q + 64, 3, 2 * m:2 * m + 2]).then_inc(sem("st_out"), 16)
            sp.wait_ge(sem("ss_done"), 8)
            for m, name in enumerate(("gla_sample", "hgrn_sample")):
                dst = A[name].rearrange("o s (k q) f v -> q f (o s) k v", q=2)
                for q in range(2):
                    sp.dma_start(dst[q], SS[64 * q:64 * q + 64, m]).then_inc(sem("st_out"), 16)
            sp.wait_ge(*done("tail"))
            sp.dma_start(A["pool_prompt"][0, 0].rearrange("j (g c) -> j g c", g=4), tail[0:HIST])\
              .then_inc(sem("stored"), 16)
            sp.dma_start(A["pool_sample"][0, :, HIST - 1].rearrange("s (g c) -> s g c", g=4),
                         tail[HIST:HIST + NS]).then_inc(sem("stored"), 16)
            sp.wait_ge(*done("k_norm"))
            for name, col in (("cmp", CK), ("slc", CS), ("win", CW)):
                sp.dma_start(A[name + "_rows_prompt"].rearrange("o b (i p) a k d -> p (o b i) (a k d)", p=128),
                             zt[:, 0:4, col:col + 256]).then_inc(sem("rows_out"), 16)
                sp.dma_start(A[name + "_rows_sample"].rearrange("o s b a k d -> (o s b) (a k d)"),
                             zt[0:NS, 4, col:col + 256]).then_inc(sem("rows_out"), 16)
            for n in range(2):
                sp.wait_ge(sem("c_red"), 7 + n)
                sp.dma_start(Y[n].rearrange("p (s c) -> p s c", s=4),
                             A["cache_win_kv"].rearrange("o s (p i) a k d -> p (o s) (i a k d)", i=4)
                             [:, 4 * n:4 * n + 4]).then_inc(sem(f"xw{n}"), 16)
            sp.wait_ge(sem("rows_out"), 96)
            sp.wait_ge(sem("sv_mm"), 13)
            with sp.Fori(0, 4) as dq:
                for v in range(6):
                    bp, kind = v // 3, v % 3
                    sp.wait_ge(sem("w_lo"), dq * 6 + N_MIX + v - 1)
                    if kind < 2:
                        src = w_gate[:, :, bass.ds(dq * 256 + 2048 * bp + 1024 * kind, CHUNK)]
                    else:
                        src = w_branch[:, 8 * bp:8 * bp + 8, bass.ds(dq * 256, CHUNK)]
                    load(N_MIX + v, src)
            with sp.Fori(0, 2) as i:
                for u in range(2):
                    reload(N_OUT + u, i, w_out[:, :, bass.ds(i * 512 + 256 * u, CHUNK)])
            with sp.Fori(0, 2) as hf:
                with sp.Fori(0, 4) as i:
                    for u in range(2):
                        reload(N_MLP + u, hf * 8 + i, w1[:, :, bass.ds(hf * 2048 + i * 512 + 256 * u, CHUNK)])
                with sp.Fori(0, 4) as dq:
                    for kq in range(2):
                        reload(N_MLP + 8 + kq, hf * 8 + dq,
                               w2[:, bass.ds(hf * 16 + 8 * kq, 8), bass.ds(dq * 256, CHUNK)])
            for i in range(5):
                sp.wait_ge(sem("y_ev"), 2 * i + 2)
                if i < TT:
                    sp.dma_start(A["y_prompt"][0, 128 * i:128 * i + 128], YT[:, i]).then_inc(sem("stored"), 16)
                else:
                    sp.dma_start(A["y_sample"].rearrange("s o d -> (s o) d"), YT[0:NS, i])\
                      .then_inc(sem("stored"), 16)
            sp.wait_ge(sem("stored"), 16 * 8)
            sp.wait_ge(sem("st_out"), 128)

        @block.tensor
        def _(pe):
            mm, tr = nc.tensor.matmul, nc.tensor.transpose

            def norm_sums(tag):
                for k in range(KT):
                    pe.wait_ge(sem(tag + "_sq"), k + 1)
                    for h in range(2):
                        last = mm(PS[:, h, 0:HALF], ones, SQN[k % 2][:, HALF * h:HALF * h + HALF],
                                  start=(k == 0), stop=(k == KT - 1))
                    last.then_inc(sem(tag + "_mm"), 1)

            def fm_unit(n, j, bank, rhs, k0=0, k1=KT, start=True, stop=True, ready=None):
                for k in range(k0, k1):
                    if ready:
                        pe.wait_ge(sem(ready), k + 1)
                    hi, lo = rhs(k - k0)
                    for w, x in ((WH, hi), (WH, lo), (WL, hi)):
                        for h in range(2):
                            last = mm(PS[:, bank + h, 0:HALF], w[n % 2][:, k, 128 * j:128 * j + 128],
                                      x[:, HALF * h:HALF * h + HALF], start=(start and k == k0 and w is WH and x is hi),
                                      stop=(stop and k == k1 - 1 and w is WL))
                last.then_inc(sem("prod"), 1)

            hk = lambda k: (hH[:, k], hL[:, k])

            pe.wait_ge(sem("ld_con"), 32)
            pe.wait_ge(sem("ld_x"), 80)
            for n in range(10):
                i, k4, w = n // 2, 4 * (n % 2), (128 if n < 8 else NS)
                if n >= 8:
                    pe.wait_ge(sem("xt_ev"), n - 7)
                for j in range(4):
                    last = tr(PS[:, n % 8, w * j:w * (j + 1)], XI[0:w, i, 128 * (k4 + j):128 * (k4 + j + 1)],
                              ident[0:w, 0:w])
                last.then_inc(sem("xt"), 1)
            pe.wait_ge(sem("xt_ev"), 10)
            norm_sums("n1")

            with pe.Fori(0, 5) as i:
                for u in range(2):
                    pe.wait_ge(sem("w_lo"), i * 2 + u + 1)
                    for j in range(2):
                        pe.wait_ge(sem("fm_free"), i * 4 + 2 * u + j + 1)
                        fm_unit(u, j, 2 * (2 * u + j), hk, ready="n1_h" if u + j == 0 else None)
            pe.wait_ge(sem("w_lo"), 11)
            pe.wait_ge(sem("fm_free"), 21)
            fm_unit(10, 0, 0, hk)
            pe.wait_ge(sem("fm_free"), 24)
            pe.wait_ge(*done("ga_ev"))

            def tm_unit(n, i, cols):
                m = 128 if i < TT else NS
                t = slice(128 * i, 128 * i + m)
                for k in range(KT):
                    for x, w in ((hH, WH), (hH, WL), (hL, WH)):
                        last = mm(PS[0:m, i, 0:cols], x[:, k, t], w[n % 2][:, k, 0:cols],
                                  start=(k == 0 and x is hH and w is WH), stop=(k == KT - 1 and x is hL))
                last.then_inc(sem("prod"), 1)

            pe.wait_ge(sem("w_lo"), 12)
            for i in range(5):
                pe.wait_ge(sem("tm_free"), i + 1)
                tm_unit(11, i, CHUNK)
            with pe.Fori(0, 4) as c:
                for u in range(2):
                    pe.wait_ge(sem("w_lo"), c * 2 + u + 13)
                    for i in range(5):
                        pe.wait_ge(sem("tm_free"), c * 10 + 5 * u + i + 6)
                        tm_unit(12 + u, i, CHUNK)
            pe.wait_ge(sem("w_lo"), 21)
            for i in range(5):
                pe.wait_ge(sem("tm_free"), 45 + i + 1)
                tm_unit(20, i, 24)

            pe.wait_ge(sem("tm_free"), 55)
            pe.wait_ge(sem("ld_wa2"), 16)
            for k in range(2):
                for h in range(2):
                    last = mm(PS[:, 2 * k + h, 0:HALF], wa2[0:GA, 128 * k:128 * k + 128],
                              gaT[0:GA, HALF * h:HALF * h + HALF], start=True, stop=True)
            last.then_inc(once("la_mm"), 1)
            pe.wait_ge(sem("la_ev"), 1)
            pe.wait_ge(*done("qk"))
            for step in range(LEVELS + 1):
                if step:
                    pe.wait_ge(sem("a_ready"), 2 * step)
                for g in range(8):
                    c, par = g // 2, g % 2
                    if step:
                        pe.wait_ge(sem("sc_cp"), 8 * (step - 1) + g + 1)
                    for k in range(4):
                        r, t = slice(64 * par, 64 * par + 64), slice(128 * c, 128 * c + 128)
                        if step:
                            a = chunks(AL[(step - 1) % 2])[r, k, t]
                            last = mm(PS[:, g, 128 * k:128 * k + 128], a, a, start=True, stop=True)
                        else:
                            last = mm(PS[:, g, 128 * k:128 * k + 128], zf[r, ZK + k, t], zf[r, ZQ + k, t],
                                      start=True, stop=True)
                    last.then_inc(sem("sc_mm"), 1)
            pe.wait_ge(*done("kdec"))
            pe.wait_ge(sem("sc_cp"), 8 * LEVELS + 8)
            for c in range(4):
                for k in range(4):
                    last = tr(PS[:, c, 128 * k:128 * k + 128], chunks(A0)[:, k, 128 * c:128 * c + 128], ident)
                last.then_inc(sem("kt_mm"), 1)
            for c in range(4):
                pe.wait_ge(sem("kd_ev"), c + 1)
                for par in range(2):
                    for k in range(4):
                        last = mm(PS[64 * par:64 * par + 64, 4 + c, 128 * k:128 * k + 128],
                                  KD[:, c, k, 64 * par:64 * par + 64], zt[:, c, head_cols(k, par)[0]],
                                  start=True, stop=True)
                last.then_inc(sem("ds_mm"), 1)
            pe.wait_ge(sem("st"), 4)
            pe.wait_ge(*done("qdec"))
            for hh in range(8):
                k, par = hh // 2, hh % 2
                r = slice(64 * par, 64 * par + 64)
                for c in range(4):
                    o = PS[:, hh, 128 * c:128 * c + 128]
                    last = mm(o, zt[:, c, head_cols(k, par)[0]], SC[:, 2 * c + par, k], start=True, stop=(c == 0))
                    if c:
                        last = mm(o, ST[r, c - 1, k], chunks(A0)[r, k, 128 * c:128 * c + 128],
                                  start=False, stop=True)
                last.then_inc(sem("o_mm"), 1)
            pe.wait_ge(sem("ob"), 8)
            for g in range(8):
                m = g // 4
                v = zt[0:NS, 4, 512 * m:512 * m + 512].rearrange("p (k q v) -> p k q v", k=2, q=2)
                for par in range(2):
                    for j in range(2):
                        s = 2 * (g % 4) + j
                        last = mm(PS[64 * par:64 * par + 64, g, 256 * j:256 * j + 256],
                                  C("onehot", 64 * s, 64 * s + 64, NS), v[:, :, par, :], start=True, stop=True)
                last.then_inc(sem("vb_mm"), 1)
            pe.wait_ge(sem("ss_done"), 8)
            for par in range(2):
                for k in range(4):
                    for s in range(NS):
                        r = slice(64 * par, 64 * par + 64)
                        last = mm(PS[:, par, 8 * k + s:8 * k + s + 1], SS[r, k // 2, s, k % 2],
                                  zf[r, ZQ + k, L + s:L + s + 1], start=True, stop=True)
            last.then_inc(once("os_mm"), 1)
            pe.wait_ge(sem("os_ev"), 2)
            for hh in range(8):
                pe.wait_ge(sem("hn_sq"), hh + 1)
                if hh >= 4:
                    pe.wait_ge(sem("hn_ln"), hh - 3)
                for h in range(2):
                    last = mm(PS[:, 2 * (hh % 4) + h, 0:HALF], ones, SQ[hh % 2][:, HALF * h:HALF * h + HALF],
                              start=True, stop=True)
                last.then_inc(sem("hn_mm"), 1)

            pe.wait_ge(sem("hn_ln"), 8)
            pe.wait_ge(sem("ld_pool"), 80)
            for g in range(4):
                last = tr(PS[:, 0, 120 * g:120 * g + 120], hist[:, g], ident[0:120, 0:120])
            last.then_inc(once("hist_mm"), 1)
            for g in range(4):
                last = tr(PS[0:23, 1, 128 * g:128 * g + 128], zf[:, ZU + g, 497:520], ident)
            last.then_inc(once("tail_mm"), 1)
            for g in range(4):
                pe.wait_ge(sem("pd"), 2 * g + 2)
                if g >= 2:
                    pe.wait_ge(sem("pool_ev"), g - 1)
                for h in range(2):
                    last = mm(PS[:, 2 + 2 * (g % 2) + h, 0:HALF], poolw[:, g], PD[:, g, HALF * h:HALF * h + HALF],
                              start=True, stop=True)
                last.then_inc(sem("pool_mm"), 1)

            pe.wait_ge(sem("pool_ev"), 4)
            pe.wait_ge(*done("tail"))
            pe.wait_ge(*done("q_norm"))
            pe.wait_ge(*done("k_norm"))
            for i in range(5):
                w = 128 if i < TT else NS
                for g in range(G):
                    last = tr(PS[:, i, w * g:w * g + w], QN[0:w, i, g].rearrange("p k d -> p (k d)"),
                              ident[0:w, 0:w])
                last.then_inc(sem("qt_mm"), 1)
            for n, col in enumerate((CS, CW)):
                for i in range(TT):
                    last = tr(PS[:, 5 + n, 128 * i:128 * i + 128], zt[:, i, col:col + 128], ident)
                last.then_inc(sem("qt_mm"), 1)
            for n, col in enumerate((CS, CW)):
                last = tr(PS[:, 7, NS * n:NS * n + NS], zt[0:NS, 4, col:col + 128], ident[0:NS, 0:NS])
            last.then_inc(sem("qt_mm"), 1)
            pe.wait_ge(sem("qt_ev"), 8)
            for i in range(TT):
                last = mm(PS[0:32, 0, 0:256], C("pool", 32 * i, 32 * i + 32), zt[:, i, CK:CK + 256],
                          start=(i == 0), stop=(i == TT - 1))
            last.then_inc(once("ckv_mm"), 1)
            pe.wait_ge(*done("ckv"))
            tr(PS[:, 1, 0:32], CKV[:, 0:128], ident[0:32, 0:32]).then_inc(once("kct_mm"), 1)
            pe.wait_ge(*done("kct"))
            for k in range(HKV):
                r = slice(64 * k, 64 * k + 64)
                for i in range(TT):
                    for g in range(G):
                        last = mm(PS[:, 4 * k + i, 32 * g:32 * g + 32], QT[r, g, 128 * i:128 * i + 128],
                                  kcT[r, :], start=True, stop=True)
                    last.then_inc(sem("cs_mm"), 1)
            pe.wait_ge(*done("cp"))
            for i in range(TT):
                for k in range(HKV):
                    last = tr(PS[:, 2 * (i % 2) + k, 0:128],
                              CM[:, i, 4 * k:4 * k + 4].rearrange("p h c -> p (h c)"), ident)
                last.then_inc(sem("ct_mm"), 1)
                pe.wait_ge(sem("ct_ev"), i + 1)
                for k in range(HKV):
                    last = mm(PS[:, 4 + i, 256 * k:256 * k + 256], PTC[:, i, k], VBK[:, k],
                              start=True, stop=True)
                last.then_inc(sem("co_mm"), 1)
            pe.wait_ge(sem("co_ev"), 4)
            def compressed_step(u):
                if u in (8, 10, 12, 14):
                    x = u - 8
                    pe.wait_ge(sem("c_red"), x + 2)
                    if x:
                        pe.wait_ge(sem("sh_ev"), x // 2)
                    for y in range(2):
                        last = mm(PS[0:NCMP, 5, 256 * y:256 * y + 256], C("shift", 0, NCMP), S16[x + y],
                                  start=True, stop=True)
                    last.then_inc(sem("sh_mm"), 1)
                elif u in (22, 25):
                    n = (u - 22) // 3
                    pe.wait_ge(*done("cx"))
                    if n:
                        pe.wait_ge(sem("kx_ev"), 1)
                    for x in range(4):
                        last = tr(PS[:, 5, NCMP * x:NCMP * x + NCMP], CX[n][:, x, 0:128], ident[0:NCMP, 0:NCMP])
                    last.then_inc(sem("kx_mm"), 1)
                elif u == 28:
                    pe.wait_ge(sem("kx_ev"), 2)
                    for x in range(NS):
                        last = mm(PS[0:NCMP, 5, 8 * x:8 * x + 8], KCT[:, x], QB[:, x], start=True, stop=True)
                    last.then_inc(once("cxs_mm"), 1)
                elif u == 31:
                    pe.wait_ge(*done("cxs"))
                    tr(PS[0:64, 5, 0:NCMP], PCT, ident[0:NCMP, 0:NCMP]).then_inc(once("cxt_mm"), 1)
                elif u == 37:
                    pe.wait_ge(*done("cxp"))
                    tr(PS[0:NCMP, 5, 0:64], PCR, ident[0:64, 0:64]).then_inc(once("cxp_mm"), 1)
                elif u == 40:
                    pe.wait_ge(*done("pcg"))
                    for x in range(NS):
                        last = mm(PS[:, 5, 8 * x:8 * x + 8], CX[x // 4][:, x % 4, 128:256], PCT[:, 8 * x:8 * x + 8],
                                  start=True, stop=True)
                    last.then_inc(once("cxo_mm"), 1)
                    mm(PS[:, 5, 64:256], ones[0:NS], GD.rearrange("p b s h -> p (b s h)"), start=True, stop=True)\
                        .then_inc(once("gb_mm"), 1)
                    mm(PS[0:16, 5, 256:256 + NSEL], PCG, C("overlap", p=NCMP), start=True, stop=True)\
                        .then_inc(once("imp_mm"), 1)
                elif u == 48:
                    pe.wait_ge(*done("rank"))
                    tr(PS[0:NSEL, 5, 0:16], RANK, ident[0:16, 0:16]).then_inc(once("sel_mm"), 1)
                elif u == 51:
                    pe.wait_ge(*done("selt"))
                    mm(PS[:, 5, 0:16], C("expand", p=NSEL), SELT, start=True, stop=True).then_inc(once("bs_mm"), 1)
                    for b in range(2):
                        mm(PS[0:NS, 5, 64 + 64 * b:128 + 64 * b], KNEW[:, b], QB.rearrange("p s h -> p (s h)"),
                           start=True, stop=True).then_inc(sem("sn_mm"), 1)

            NU = len(UNITS)
            pe.wait_ge(*done("gd"))
            for u in range(NU + 2):
                compressed_step(u)
                if u < NU:
                    i, b, h = UNITS[u]
                    k, g = h // G, h % G
                    r, bank = slice(64 * k, 64 * k + 64), u % 3
                    if u >= 3:
                        pe.wait_ge(sem("ex"), u - 2)
                    mm(PS[:, bank, 0:128 * i + 128], QT[r, g, 128 * i:128 * i + 128],
                       (KTS, KTW)[b][r, 0:128 * i + 128], start=True, stop=False)
                    mm(PS[:, bank, 128 * i:128 * i + 128], ident, C("causal"), start=False, stop=True)\
                        .then_inc(sem("s_mm"), 1)
                if 1 <= u <= NU:
                    v = u - 1
                    i = UNITS[v][0]
                    pe.wait_ge(sem("ex"), v + 1)
                    if v >= 2:
                        pe.wait_ge(sem("pt_ev"), v - 1)
                    for j in range(i + 1):
                        last = tr(PS[:, 3 + v % 2, 128 * j:128 * j + 128], P[v % 3][:, 128 * j:128 * j + 128], ident)
                    last.then_inc(sem("t_mm"), 1)
                if u >= 2:
                    v = u - 2
                    i, b, h = UNITS[v]
                    pe.wait_ge(sem("pt_ev"), v + 1)
                    if v % 16 == 0 and i:
                        pe.wait_ge(sem("on"), i)
                    col = (CS, CW)[b] + 128 + 64 * (h // G)
                    for j in range(i + 1):
                        last = mm(PS[:, 6 + b, 64 * h:64 * h + 64], PT[v % 3][:, j], zt[:, j, col:col + 64],
                                  start=(j == 0), stop=(j == i))
                    last.then_inc(sem("pv_mm"), 1)
            for i in range(TT):
                pe.wait_ge(sem("on"), i + 1)
                if i == 0:
                    pe.wait_ge(sem("on"), TT)
                for c in range(4):
                    last = tr(PS[:, i, 128 * c:128 * c + 128], ON[:, i, 128 * c:128 * c + 128], ident)
                last.then_inc(sem("ont_mm"), 1)
            pe.wait_ge(sem("ont"), 4)
            pe.wait_ge(sem("sn"), 2)
            kt = 0
            for n, (b, s0) in enumerate(ROUNDS):
                per = 4 if b == 0 else 1
                for x in range(s0, s0 + 4):
                    if b == 0:
                        pe.wait_ge(sem(f"xs{x % 5}"), 16 * (x // 5 + 1))
                    else:
                        pe.wait_ge(sem(f"xw{x // 4}"), 16)
                    for q in range(per):
                        if kt + q >= 4:
                            pe.wait_ge(sem("ktx"), kt + q - 3)
                        for i in range(4):
                            last = tr(PS[:, (kt + q) % 4, 128 * i:128 * i + 128], xtile(b, x, 4 * q + i)[0], ident)
                        last.then_inc(sem("ktx_mm"), 1)
                    m = 4 * n + x - s0
                    if m >= 2:
                        pe.wait_ge(sem("sx"), m - 1)
                    for q in range(per):
                        pe.wait_ge(sem("ktx"), kt + q + 1)
                        for i in range(4):
                            at = 8 * (4 * q + i)
                            last = mm(PS[:, 4 + m % 2, at:at + 8], KTX[:, 4 * ((kt + q) % 4) + i], QB[:, x],
                                      start=True, stop=True)
                        last.then_inc(sem("sx_mm"), 1)
                    kt += per
                pe.wait_ge(sem("m1"), n + 1)
                if n:
                    pe.wait_ge(sem("oacc"), n + 1)
                tr(PS[0:32, 6, 0:128], M1, ident)
                tr(PS[0:32, 6, 128:136], SN[b][:, 8 * s0:8 * s0 + 32], ident[0:NS, 0:NS]).then_inc(sem("mt_mm"), 1)
                pe.wait_ge(sem("dg"), n + 1)
                mm(PS[:, 6, 0:32], ones[0:32], DG, start=True, stop=True).then_inc(sem("mb_mm"), 1)
                pe.wait_ge(sem("r1"), n + 1)
                mm(PS[:, 6, 64:96], ones, M1, start=True, stop=False)
                mm(PS[:, 6, 64:96], ones[0:NS], SN[b][:, 8 * s0:8 * s0 + 32], start=False, stop=True)\
                    .then_inc(sem("sum_mm"), 1)
                for x in range(s0, s0 + 4):
                    o = PS[0:8, 7, 128 * (x - s0):128 * (x - s0) + 128]
                    for i in range(4 * per):
                        mm(o, SX[:, x - s0, i], xtile(b, x, i)[1], start=(i == 0), stop=False)
                    col = (CS, CW)[b] + 128
                    mm(o, SN[b][:, 8 * x:8 * x + 8], zt[0:NS, 4, col:col + 128], start=False, stop=True)\
                        .then_inc(sem("sv_mm"), 1)
                pe.wait_ge(sem("so"), n + 1)
                for j in range(4):
                    last = tr(PS[:, 6, 128 + 8 * j:136 + 8 * j], SO[:, 128 * j:128 * j + 128], ident[0:8, 0:8])
                last.then_inc(sem("so_mm"), 1)

            pe.wait_ge(*done("nsa_done"))
            with pe.Fori(0, 4) as dq:
                for v in range(6):
                    bp, kind = v // 3, v % 3
                    pe.wait_ge(sem("w_lo"), dq * 6 + N_MIX + v + 1)
                    if kind < 2:
                        for j in range(2):
                            q = 2 * kind + j
                            pe.wait_ge(sem("mix_mul"), dq * 8 + 4 * bp + q + 1)
                            fm_unit(N_MIX + v, j, 2 * q, hk, ready="n3_h" if v + q == 0 else None)
                    else:
                        pe.wait_ge(sem("b_lo"), 2 * bp + 2)
                        for q in range(4):
                            pe.wait_ge(sem("sg"), dq * 8 + 4 * bp + q + 1)
                            b = 2 * bp + q // 2
                            fm_unit(N_MIX + v, q % 2, 2 * q, lambda c: (bH[b][:, c], bL[b][:, c]),
                                    k0=4 * (q // 2), k1=4 * (q // 2) + 4)
            pe.wait_ge(sem("mix_mul"), 36)
            for n in range(8):
                if n % 2 == 0:
                    pe.wait_ge(sem("w_lo"), N_OUT + n // 2 + 1)
                if n >= 4:
                    pe.wait_ge(sem("wo_ev"), n - 3)
                fm_unit(N_OUT + n // 2, n % 2, 2 * (n % 4), lambda k: (mH[:, k], mL[:, k]),
                        ready="m_lo" if n == 0 else None)
            pe.wait_ge(sem("wo_ev"), 8)
            norm_sums("n2")
            with pe.Fori(0, 2) as hf:
                with pe.Fori(0, 4) as i:
                    for u in range(2):
                        pe.wait_ge(sem("y_free"), hf * 8 + 4)
                        pe.wait_ge(sem("w_lo"), hf * 16 + i * 2 + N_MLP + u + 1)
                        for j in range(2):
                            pe.wait_ge(sem("u_free"), hf * 16 + i * 4 + 2 * u + j + 1)
                            fm_unit(N_MLP + u, j, 2 * (2 * u + j), hk, ready="n2_h" if u + j == 0 else None)
                with pe.Fori(0, 2) as e:
                    for f in range(2):
                        for kq in range(2):
                            pe.wait_ge(sem("u_free"), hf * 16 + 20)
                            pe.wait_ge(sem("w_lo"), hf * 16 + e * 4 + N_MLP + 8 + 2 * f + kq + 1)
                            pe.wait_ge(sem("u_lo"), hf * 16 + 8 * kq + 8)
                            for j in range(2):
                                if kq == 0:
                                    pe.wait_ge(sem("y_free"), hf * 8 + e * 4 + 2 * f + j + 1)
                                fm_unit(N_MLP + kq, j, 4 * f + 2 * j,
                                        lambda k: (uH[:, 8 * kq + k], uL[:, 8 * kq + k]),
                                        start=(kq == 0), stop=(kq == 1))
            pe.wait_ge(sem("y_free"), 20)
            for n in range(10):
                i, k4, w = n // 2, 4 * (n % 2), (128 if n < 8 else NS)
                if n >= 8:
                    pe.wait_ge(sem("y_ev"), n - 7)
                for j in range(4):
                    last = tr(PS[0:w, n % 8, 128 * j:128 * j + 128], xT[:, k4 + j, 128 * i:128 * i + w], ident)
                last.then_inc(sem("yt_mm"), 1)

        @block.scalar
        def _(act):
            f = nc.scalar.activation
            step = steps(act, "act_step")

            def norm(tag):
                for k in range(KT):
                    if k >= 2:
                        act.wait_ge(sem(tag + "_mm"), k - 1)
                    f(SQN[k % 2], xT[:, k], ACT.Square).then_inc(sem(tag + "_sq"), 1)
                act.wait_ge(sem(tag + "_mm"), KT)
                step(f(halves(RST), pair(0), ACT.Ln, bias=eps, scale=1.0 / D))
                f(RST, RST, ACT.Exp, scale=-0.5).then_inc(sem(tag + "_rs"), 1)

            def upper(n, i=0, tiles=None, cols=CHUNK):
                act.wait_ge(sem(f"raw{n % 2}"), i * 16 + 16 * (n // 2) + 16)
                if tiles is not None:
                    act.wait_ge(sem("prod"), tiles)
                nc.scalar.copy(WH[n % 2][:, :, 0:cols], WR[n % 2][:, :, 0:cols]).then_inc(sem("w_hi"), 1)

            def h_upper(tag):
                for k in range(KT):
                    act.wait_ge(sem(tag + "_raw"), k + 1)
                    nc.scalar.copy(hH[:, k], TH[k % 2]).then_inc(sem(tag + "_hi"), 1)

            act.wait_ge(*done("eps"))
            act.wait_ge(sem("xt_ev"), 10)
            norm("n1")
            upper(0)
            h_upper("n1")
            upper(1)
            with act.Fori(0, 4) as i:
                for u in range(2):
                    upper(2 + u, i, i * 4 + 2 * u + 2)
            for n in (10, 11):
                upper(n, 0, units_before(n - 1), 128 if n == 10 else CHUNK)
            with act.Fori(0, 4) as i:
                for u in range(2):
                    upper(12 + u, i, i * 10 + 5 * u + 21)
            upper(20, 0, units_before(19), 24)

            act.wait_ge(sem("prod"), units_before(N_MIX))
            act.wait_ge(sem("fm_free"), 24)
            f(SIGQ, zf[:, ZQ + 2:ZQ + 4], ACT.Sigmoid).then_inc(sem("sig"), 1)
            f(SIGF, zf[:, ZK + 2:ZK + 4], ACT.Sigmoid).then_inc(sem("sig"), 1)
            f(SIGG, zf[:, ZG:ZG + 8], ACT.Sigmoid).then_inc(sem("sig"), 1)
            act.wait_ge(sem("la_ev"), 2)
            step(f(TMPA, LF[:, 0:2], ACT.Abs))
            step(f(TMPA, TMPA, ACT.Exp, scale=-1.0))
            f(TMPA, TMPA, ACT.Ln, bias=1.0).then_inc(once("lsp"), 1)
            act.wait_ge(*done("lb_d"))
            f(lbv[:, :, 1], lbv[:, :, 0], ACT.Exp).then_inc(once("lb_e"), 1)
            act.wait_ge(*done("fg"))
            f(LF[:, 2:4], LF[:, 2:4], ACT.Ln).then_inc(once("lf_h"), 1)
            act.wait_ge(*done("lf_h"))
            act.wait_ge(*done("lf_g"))
            f(decS, LF[:, :, L:T], ACT.Exp).then_inc(once("decs"), 1)
            for lev in range(LEVELS):
                act.wait_ge(sem("dist"), 2 * lev + 2)
                f(EL[lev % 2], EL[lev % 2], ACT.Exp).then_inc(sem("e_ready"), 1)
            act.wait_ge(sem("a_ready"), 2 * LEVELS)
            f(E1, B, ACT.Exp).then_inc(sem("eb"), 1)
            act.wait_ge(sem("dist"), 2 * LEVELS + 1)
            f(E0, E0, ACT.Exp).then_inc(sem("eb"), 1)
            f(decC, B.rearrange("p (k c t) -> p k c t", k=4, c=4)[:, :, :, 127], ACT.Exp).then_inc(once("decc"), 1)
            nc.scalar.preload_act_table_set("natural_log_exp_and_others")
            act.wait_ge(sem("ob"), 8)
            act.wait_ge(sem("os_ev"), 2)
            for hh in range(9):
                if hh < 8:
                    if hh >= 2:
                        act.wait_ge(sem("hn_mm"), hh - 1)
                    f(SQ[hh % 2], OB[:, hh], ACT.Square).then_inc(sem("hn_sq"), 1)
                if hh:
                    j = hh - 1
                    act.wait_ge(sem("hn_mm"), j + 1)
                    if j >= 2:
                        act.wait_ge(sem("hn"), j - 1)
                    f(halves(RN[j % 2]), pair(2 * (j % 4)), ACT.Ln, bias=eps, scale=1.0 / 128)\
                        .then_inc(sem("hn_ln"), 1)
                    act.wait_ge(sem("hn_ln"), j + 1)
                    f(RN[j % 2], RN[j % 2], ACT.Exp, scale=-0.5).then_inc(sem("hn_rs"), 1)

            act.wait_ge(sem("hn"), 8)
            act.wait_ge(sem("o_mm"), 8)
            f(zt[:, :, CG:CG + 24], zt[:, :, CG:CG + 24], ACT.Sigmoid).then_inc(once("ng"), 1)
            f(TQ, zt[:, :, CQ:CQ + 512], ACT.Square).then_inc(sem("tq"), 1)
            f(TK[:, :, 0:128], zt[:, :, CS:CS + 128], ACT.Square).then_inc(sem("tq"), 1)
            f(TK[:, :, 128:256], zt[:, :, CW:CW + 128], ACT.Square).then_inc(sem("tq"), 1)
            act.wait_ge(sem("rq_sum"), 2)
            step(f(rq, rq, ACT.Ln, bias=eps, scale=1.0 / HD))
            f(rq, rq, ACT.Exp, scale=-0.5).then_inc(once("rq"), 1)
            act.wait_ge(*done("kst"))
            step(f(kst[:, 0:2], kst[:, 0:2], ACT.Ln, bias=eps[0:32], scale=1.0 / HD))
            f(kst[:, 0:2], kst[:, 0:2], ACT.Exp, scale=-0.5).then_inc(once("kst_rs"), 1)
            act.wait_ge(*done("cm"))
            f(CM, CM, ACT.Exp).then_inc(once("cm_e"), 1)
            for u in range(len(UNITS)):
                if u == 19:
                    act.wait_ge(*done("kst_x"))
                    step(f(KST, KST, ACT.Ln, bias=eps[0:NCMP], scale=1.0 / HD))
                    f(KST, KST, ACT.Exp, scale=-0.5).then_inc(once("kst_xr"), 1)
                if u == 34:
                    act.wait_ge(*done("cxm"))
                    f(PCR, PS[0:64, 5, 0:NCMP], ACT.Exp, bias=CMAX[:, 0:1], accum_out=CMAX[:, 1:2])\
                        .then_inc(once("cxe"), 1)
                i, b, h = UNITS[u]
                act.wait_ge(sem("mx"), u + 1)
                if u >= 3:
                    act.wait_ge(sem("t_mm"), u - 2)
                f(P[u % 3][:, 0:128 * i + 128], PS[:, u % 3, 0:128 * i + 128], ACT.Exp, bias=nm[u % 3],
                  accum_out=rs[:, i, b, h:h + 1]).then_inc(sem("ex"), 1)
            for n, (b, s0) in enumerate(ROUNDS):
                act.wait_ge(sem("sxm"), n + 1)
                ni = 16 if b == 0 else 4
                f(SX[:, :, 0:ni], SX[:, :, 0:ni], ACT.Exp).then_inc(sem("sxe"), 1)
                new = SN[b][:, 8 * s0:8 * s0 + 32]
                f(new, new, ACT.Exp).then_inc(sem("sxe"), 1)

            h_upper("n3")
            act.wait_ge(*done("nsa_done"))
            for n in (N_MIX, N_MIX + 1):
                upper(n)
            for b in range(4):
                nc.scalar.copy(bH[b], zf[:, 4 * b:4 * b + 4]).then_inc(sem("b_hi"), 1)
            with act.Fori(0, 4) as dq:
                for v in range(6):
                    bp, kind = v // 3, v % 3
                    first = units_before(N_MIX + v)
                    for j in range(2):
                        if j == 1:
                            n = N_MIX + v + 2
                            act.wait_ge(sem(f"raw{n % 2}"), dq * 48 + 16 * (n // 2) + 16)
                            act.wait_ge(sem("prod"), dq * 16 + units_before(n - 1))
                            nc.scalar.copy(WH[n % 2], WR[n % 2]).then_inc(sem("w_hi"), 1)
                        if kind < 2:
                            q = 2 * kind + j
                            act.wait_ge(sem("prod"), dq * 16 + first + j + 1)
                            act.wait_ge(sem("mix_mul"), dq * 8 + 4 * bp + q + 1)
                            f(halves(SG[q]), pair(2 * q), ACT.Sigmoid,
                              bias=V("bg")[:, bass.ds(dq * 2 + 16 * bp + 8 * kind + j, 1)]).then_inc(sem("sg"), 1)
            for k in range(KT):
                act.wait_ge(sem("mix_add"), 25)
                nc.scalar.copy(mH[:, k], mixT[:, k]).then_inc(sem("m_hi"), 1)
            for n in (47, 48, 49, 50):
                upper(n, 0, units_before(n - 1))
            act.wait_ge(sem("wo_ev"), 8)
            norm("n2")
            h_upper("n2")
            for hf in range(2):
                with act.Fori(0, 4) as i:
                    for u in range(2):
                        n = N_MLP + u
                        for j in range(2):
                            if j == 1:
                                upper(n + 2, i + hf * 8, i * 4 + hf * 32 + units_before(n + 1))
                            q = 2 * u + j
                            act.wait_ge(sem("prod"), i * 4 + hf * 32 + units_before(n) + j + 1)
                            act.wait_ge(sem("u_sq"), i * 4 + hf * 16 + q + 1)
                            f(halves(UR[j]), pair(2 * q), ACT.Relu).then_inc(sem("u_free"), 1)
                with act.Fori(0, 3) as dq:
                    for kq in range(2):
                        n = N_MLP + 8 + kq
                        upper(n + 2, dq + hf * 8, dq * 4 + hf * 32 + units_before(n + 1))
                if hf == 0:
                    for n in (N_MLP + 14, N_MLP + 15):
                        upper(n + 2, 0, units_before(n + 1))

        @block.vector
        def _(dve):
            v = nc.vector
            step = steps(dve, "dve_step")

            def norm_apply(tag, g):
                for k in range(KT + 1):
                    if k < KT:
                        if k >= 2:
                            dve.wait_ge(sem(tag + "_h"), k - 1)
                        v.scalar_tensor_tensor(TH[k % 2], xT[:, k], V(g, k, k + 1), RST, ALU.mult, ALU.mult)\
                            .then_inc(sem(tag + "_raw"), 1)
                    if k:
                        dve.wait_ge(sem(tag + "_hi"), k)
                        v.tensor_tensor(hL[:, k - 1], TH[(k - 1) % 2], hH[:, k - 1], ALU.subtract)\
                            .then_inc(sem(tag + "_h"), 1)

            dve.sem_inc(sem("fm_free"), 4)
            dve.sem_inc(sem("tm_free"), 5)
            dve.sem_inc(sem("mix_mul"), 4)
            dve.sem_inc(sem("mix_add"), 1)
            dve.sem_inc(sem("y_free"), 4)
            dve.sem_inc(sem("u_sq"), 2)
            dve.sem_inc(sem("u_free"), 4)
            v.memset(eps, EPS).then_inc(once("eps"), 1)
            for n in range(10):
                i, k4, w = n // 2, 4 * (n % 2), (128 if n < 8 else NS)
                dve.wait_ge(sem("xt"), n + 1)
                v.tensor_copy(xT[:, k4:k4 + 4, 128 * i:128 * i + w],
                              PS[:, n % 8, 0:4 * w].rearrange("p (k t) -> p k t", k=4)).then_inc(sem("xt_ev"), 1)
            dve.wait_ge(sem("ld_idx"), 16)
            dve.wait_ge(sem("ld_con"), 32)
            v.tensor_scalar(idx[:, NS:], idx[:, 0:NS], 8.0, V("r8"), ALU.mult, ALU.add).then_inc(once("idx"), 1)
            dve.wait_ge(sem("xt_ev"), 10)
            dve.wait_ge(sem("n1_rs"), 1)
            norm_apply("n1", "n1")

            with dve.Fori(0, 5) as i:
                for j in range(4):
                    dve.wait_ge(sem("prod"), i * 4 + j + 1)
                    v.tensor_copy(halves(zf[:, bass.ds(i * 4 + j, 1)].rearrange("p k t -> p (k t)")), pair(2 * j))\
                        .then_inc(sem("fm_free"), 1)
            dve.wait_ge(sem("prod"), 21)
            v.tensor_copy(halves(gaT[0:GA]), PS[0:GA, 0:2, 0:HALF]).then_inc(once("ga_ev"), 1)
            dve.wait_ge(sem("zt_zero"), 1)

            def tm_evac(n, i, c0, cols):
                m = 128 if i < TT else NS
                dve.wait_ge(sem("prod"), n + 22)
                v.tensor_copy(zt[0:m, i, c0], PS[0:m, i, 0:cols]).then_inc(sem("tm_free"), 1)

            for i in range(5):
                tm_evac(i, i, slice(0, CHUNK), CHUNK)
            with dve.Fori(0, 4) as c:
                for u in range(2):
                    for i in range(5):
                        tm_evac(c * 10 + 5 * u + 5 + i, i, bass.ds(c * 512 + 256 * u + 256, CHUNK), CHUNK)
            for i in range(5):
                tm_evac(45 + i, i, slice(9 * CHUNK, TM), 24)

            dve.wait_ge(sem("fm_free"), 24)
            dve.wait_ge(sem("ld_con"), 32)
            step(v.tensor_scalar(zf[:, ZQ:ZQ + 2], zf[:, ZQ:ZQ + 2], 0.125, None, ALU.mult))
            dve.wait_ge(sem("sig"), 1)
            v.scalar_tensor_tensor(zf[:, ZQ + 2:ZQ + 4], zf[:, ZQ + 2:ZQ + 4], 0.125, SIGQ, ALU.mult, ALU.mult)\
                .then_inc(once("q_act"), 1)
            dve.wait_ge(*done("la_mm"))
            for k in range(2):
                v.tensor_scalar(halves(LF[:, k]), pair(2 * k), V("ba", k, k + 1), None, ALU.add)\
                    .then_inc(sem("la_ev"), 1)
            v.tensor_tensor(lbv[:, :, 0], V("lb"), V("lb"), ALU.subtract).then_inc(once("lb_d"), 1)
            dve.wait_ge(*done("lb_e"))
            step(v.reciprocal(lbv[:, :, 2], lbv[:, :, 1]))
            step(v.tensor_tensor(lbv[:, :, 3], lbv[:, :, 1], lbv[:, :, 2], ALU.mult))
            step(v.tensor_tensor(lbv[:, :, 4], lbv[:, :, 3], lbv[:, :, 3], ALU.subtract))
            step(v.tensor_scalar(lbv[:, :, 5], lbv[:, :, 4], -1.0, 1.0, ALU.mult, ALU.add))
            dve.wait_ge(sem("sig"), 2)
            for k in range(2):
                step(v.tensor_scalar(LF[:, 2 + k], SIGF[:, k], lbv[:, k, 5:6], lbv[:, k, 4:5], ALU.mult, ALU.add))
            step(v.tensor_scalar(zf[:, ZK + 2:ZK + 4], LF[:, 2:4], -1.0, 1.0, ALU.mult, ALU.add))
            v.tensor_scalar(LF[:, 2:4], LF[:, 2:4], 2.0 ** -63, None, ALU.max).then_inc(once("fg"), 1)
            dve.wait_ge(sem("la_ev"), 2)
            dve.wait_ge(*done("lsp"))
            step(v.scalar_tensor_tensor(flat(LF[:, 0:2]), flat(LF[:, 0:2]), 0.0, flat(TMPA), ALU.min, ALU.subtract))
            v.tensor_scalar(LF[:, 0:2], LF[:, 0:2], 1.0 / 16, None, ALU.mult).then_inc(once("lf_g"), 1)
            dve.wait_ge(*done("lf_g"))
            dve.wait_ge(*done("lf_h"))
            for k in range(4):
                v.tensor_tensor_scan(chunks(B)[:, k], C("reset"), LF[:, k, 0:L], 0.0, ALU.mult, ALU.add)\
                    .then_inc(sem("cum"), 1)
            dve.wait_ge(sem("sig"), 3)
            v.tensor_tensor(flat(zf[:, ZG:ZG + 8]), flat(zf[:, ZG:ZG + 8]), flat(SIGG), ALU.mult)\
                .then_inc(once("qk"), 1)

            def score_copy(st):
                for g in range(8):
                    dve.wait_ge(sem("sc_mm"), 8 * st + g + 1)
                    mk = LEVELS if st == 0 else st - 1
                    mask = C("masks", 128 * mk, 128 * mk + 128)
                    ps = PS[:, g].rearrange("p (k t) -> p k t", k=4)
                    if st == 0:
                        v.tensor_tensor(SC[:, g], ps, mask.unsqueeze(1).to_broadcast([128, 4, 128]), ALU.mult)\
                            .then_inc(sem("sc_cp"), 1)
                    else:
                        v.copy_predicated(SC[:, g], mask.bitcast(i32).unsqueeze(1).to_broadcast([128, 4, 128]), ps)\
                            .then_inc(sem("sc_cp"), 1)

            dve.wait_ge(*done("qk"))
            for lev in range(LEVELS):
                half = 1 << lev
                dve.wait_ge(sem("e_ready"), lev + 1)
                if lev >= 2:
                    dve.wait_ge(sem("sc_mm"), 8 * lev)
                if lev == 0:
                    dve.wait_ge(*done("lsp"))
                for side, z0 in ((0, ZK), (1, ZQ)):
                    blk = lambda ap: ap.rearrange("p k (n q h) -> p k n q h", q=2, h=half)[:, :, :, side]
                    a, e = blk(chunks(AL[lev % 2])), blk(chunks(EL[lev % 2]))
                    x = zf[:, z0:z0 + 4, 0:L].rearrange("p k (n q h) -> p k n q h", q=2, h=half)[:, :, :, side]
                    v.tensor_tensor(a, x, e, ALU.mult).then_inc(sem("a_ready"), 1)
                score_copy(lev)
                dve.wait_ge(sem("sc_cp"), 8 * lev + 8)
            score_copy(LEVELS)

            dve.wait_ge(sem("eb"), 2)
            dve.wait_ge(sem("sc_mm"), 8 * LEVELS + 8)
            v.tensor_tensor(chunks(A0), zf[:, ZK:ZK + 4, 0:L], chunks(E0), ALU.mult).then_inc(once("kdec"), 1)
            dve.wait_ge(*done("decs"))
            dve.wait_ge(sem("cum"), 4)
            for c in range(4):
                dve.wait_ge(sem("kt_mm"), c + 1)
                v.tensor_copy(KD[:, c].rearrange("p k f -> p (k f)"), PS[:, c]).then_inc(sem("kd_ev"), 1)
            v.tensor_tensor(chunks(A0), zf[:, ZQ:ZQ + 4, 0:L], chunks(E1), ALU.mult).then_inc(once("qdec"), 1)
            dve.wait_ge(*done("decc"))
            for c in range(4):
                dve.wait_ge(sem("ds_mm"), c + 1)
                ds = PS[:, 4 + c].rearrange("p (k v) -> p k v", k=4)
                if c == 0:
                    v.tensor_copy(ST[:, 0], ds).then_inc(sem("st"), 1)
                else:
                    dve.wait_ge(sem("st"), c)
                    step(v.tensor_tensor(ST[:, c], ST[:, c - 1], bc(decC[:, :, c], 128), ALU.mult))
                    v.tensor_tensor(ST[:, c], ST[:, c], ds, ALU.add).then_inc(sem("st"), 1)
            dve.wait_ge(sem("o_mm"), 8)
            for hh in range(8):
                v.tensor_copy(OB[:, hh, 0:L], PS[:, hh]).then_inc(sem("ob"), 1)
            dve.wait_ge(sem("ld_ss"), 64)
            for m in range(2):
                d = decS[:, 2 * m:2 * m + 2].rearrange("p k s -> p s k")
                step(v.tensor_tensor(SS[:, m], SS[:, m], bc(d, 128), ALU.mult))
            for g in range(8):
                m, s0 = g // 4, 2 * (g % 4)
                dve.wait_ge(sem("vb_mm"), g + 1)
                k = zf[:, ZK + 2 * m:ZK + 2 * m + 2, L + s0:L + s0 + 2].rearrange("p k s -> p s k")
                step(v.tensor_tensor(VB[g % 2], PS[:, g].rearrange("p (s k v) -> p s k v", s=2, k=2), bc(k, 128), ALU.mult))
                v.tensor_tensor(SS[:, m, s0:s0 + 2], SS[:, m, s0:s0 + 2], VB[g % 2], ALU.add)\
                    .then_inc(sem("ss_done"), 1)
            dve.wait_ge(*done("os_mm"))
            for par in range(2):
                v.tensor_copy(OB[:, par:8:2, L:T], PS[:, par, 0:32].rearrange("p (k s) -> p k s", k=4))\
                    .then_inc(sem("os_ev"), 1)
            dve.wait_ge(sem("os_ev"), 2)
            for hh in range(8):
                dve.wait_ge(sem("hn_rs"), hh + 1)
                gain = V("gn") if hh < 4 else V("hn")
                step(v.scalar_tensor_tensor(OB[:, hh], OB[:, hh], gain, RN[hh % 2], ALU.mult, ALU.mult))
                v.tensor_tensor(zf[:, ZG + hh], zf[:, ZG + hh], OB[:, hh], ALU.mult).then_inc(sem("hn"), 1)

            dve.wait_ge(*done("hist_mm"))
            dve.wait_ge(sem("hn"), 8)
            hs = stat[:, 60:92].rearrange("p (g s) -> p g s", g=4)
            for g, w in enumerate(WINDOWS):
                step(v.tensor_reduce(hs[:, g], PS[:, 0, 120 * g:120 * g + 120].rearrange("p (s j) -> p s j", s=NS)
                                     [:, :, HIST + 1 - w:HIST], AX, ALU.add))
            step(v.tensor_tensor(hs, hs, zf[:, ZU:ZU + 4, L:T], ALU.add))
            dve.wait_ge(*done("tail_mm"))
            v.tensor_copy(tail, PS[0:23, 1].rearrange("p (g c) -> p g c", g=4)).then_inc(once("tail"), 1)
            dve.wait_ge(sem("win"), 1)
            for g, w in enumerate(WINDOWS):
                win = WIN[g][:, HIST:HIST + L]
                v.scalar_tensor_tensor(PD[:, g, 0:L], win, 1.0 / w, zf[:, ZU + g, 0:L], ALU.mult, ALU.subtract)\
                    .then_inc(sem("pd"), 1)
                v.scalar_tensor_tensor(PD[:, g, L:T], hs[:, g], 1.0 / w, zf[:, ZU + g, L:T], ALU.mult, ALU.subtract)\
                    .then_inc(sem("pd"), 1)
            for g in range(4):
                dve.wait_ge(sem("pool_mm"), g + 1)
                v.tensor_scalar(halves(zf[:, ZU + g]), pair(2 + 2 * (g % 2)), V("psc", g, g + 1), None, ALU.mult)\
                    .then_inc(sem("pool_ev"), 1)

            dve.wait_ge(sem("pd"), 8)
            dve.wait_ge(sem("st_out"), 128)
            step(v.tensor_scalar(gq8, V("qg"), 0.125, None, ALU.mult))
            dve.wait_ge(sem("tq"), 3)
            v.tensor_reduce(rq[:, :, 0:8], TQ.rearrange("p i (h d) -> p i h d", d=HD), AX, ALU.add)\
                .then_inc(sem("rq_sum"), 1)
            v.tensor_reduce(rq[:, :, 8:12], TK.rearrange("p i (h d) -> p i h d", d=HD), AX, ALU.add)\
                .then_inc(sem("rq_sum"), 1)
            dve.wait_ge(*done("rq"))
            for n, col in enumerate((CS, CW)):
                kk = zt[:, :, col:col + 128].rearrange("p i (h d) -> p i h d", d=HD)
                step(v.tensor_tensor(kk, kk, bc(rq[:, :, 8 + 2 * n:10 + 2 * n], HD), ALU.mult))
                gain = V("kg", 64 * (n + 1), 64 * (n + 2)).unsqueeze(1).unsqueeze(1).to_broadcast([128, 5, 2, HD])
                ins = v.tensor_tensor(kk, kk, gain, ALU.mult)
                if n == 0:
                    step(ins)
                else:
                    ins.then_inc(once("k_norm"), 1)
            for i in range(5):
                for k in range(HKV):
                    q = zt[:, i, CQ + 256 * k:CQ + 256 * k + 256].rearrange("p (g d) -> p g d", g=G)
                    step(v.tensor_tensor(QN[:, i, :, k], q, bc(rq[:, i, 4 * k:4 * k + 4], HD), ALU.mult))
            qv = R[:, 2560:5120].rearrange("p (n d) -> p n d", d=HD)
            v.tensor_tensor(qv, qv, gq8.unsqueeze(1).to_broadcast([128, 40, HD]), ALU.mult)\
                .then_inc(once("q_norm"), 1)
            for i in range(5):
                w = 128 if i < TT else NS
                dve.wait_ge(sem("qt_mm"), i + 1)
                v.tensor_copy(QT[:, :, 128 * i:128 * i + w], PS[:, i, 0:4 * w].rearrange("p (g t) -> p g t", g=G))\
                    .then_inc(sem("qt_ev"), 1)
            dve.wait_ge(sem("qt_mm"), 8)
            v.tensor_copy(KTS[:, 0:L], PS[:, 5]).then_inc(sem("qt_ev"), 1)
            v.tensor_copy(KTW[:, 0:L], PS[:, 6]).then_inc(sem("qt_ev"), 1)
            new = R[:, 7200:8240].rearrange("p (b t) -> p b t", b=2)[:, :, L:T]
            v.tensor_copy(new, PS[:, 7, 0:16].rearrange("p (b s) -> p b s", b=2)).then_inc(sem("qt_ev"), 1)
            dve.wait_ge(*done("ckv_mm"))
            step(v.tensor_copy(CKV, PS[0:32, 0, 0:256]))
            sq = gaT[0:32, 256:384]
            step(v.tensor_tensor(sq, CKV[:, 0:128], CKV[:, 0:128], ALU.mult))
            v.tensor_reduce(kst[:, 0:2], sq.rearrange("p (k d) -> p k d", d=HD), AX, ALU.add).then_inc(once("kst"), 1)
            dve.wait_ge(sem("hn"), 8)
            step(v.memset(VBK, 0.0))
            for j in range(4):
                step(v.tensor_copy(VBK[32 * j:32 * j + 32, :, 64 * j:64 * j + 64],
                                   CKV[:, 128:256].rearrange("p (k d) -> p k d", d=HD)))
            dve.wait_ge(*done("kst_rs"))
            ck = CKV[:, 0:128].rearrange("p (k d) -> p k d", d=HD)
            step(v.tensor_tensor(ck, ck, bc(kst[:, 0:2], HD), ALU.mult))
            v.tensor_tensor(ck, ck, V("kg", 0, 64, 32).unsqueeze(1).to_broadcast([32, 2, HD]), ALU.mult)\
                .then_inc(once("ckv"), 1)
            dve.wait_ge(*done("kct_mm"))
            v.tensor_copy(kcT, PS[:, 1, 0:32]).then_inc(once("kct"), 1)
            for k in range(HKV):
                for i in range(TT):
                    dve.wait_ge(sem("cs_mm"), 4 * k + i + 1)
                    neg = C("cmpneg", 32 * i, 32 * i + 32).unsqueeze(1).to_broadcast([128, 4, 32])
                    step(v.tensor_tensor(CM[:, i, 4 * k:4 * k + 4],
                                         PS[:, 4 * k + i, 0:128].rearrange("p (h c) -> p h c", h=4), neg, ALU.add))
            cm = CM.rearrange("p i h c -> p (i h) c")
            step(v.tensor_reduce(nmc, cm, AX, ALU.max, negate=True))
            v.tensor_tensor(cm, cm, bc(nmc, 32), ALU.add).then_inc(once("cm"), 1)
            dve.wait_ge(*done("cm_e"))
            step(v.tensor_reduce(rsc.rearrange("p i h -> p (i h)"), cm, AX, ALU.add))
            v.tensor_tensor(CM, CM, C("cmp01").rearrange("p (i c) -> p i c", i=4).unsqueeze(2)
                            .to_broadcast([128, 4, 8, 32]), ALU.mult).then_inc(once("cp"), 1)
            step(v.reciprocal(rsc, rsc))
            dve.wait_ge(*done("ng"))
            gate = zt[:, :, CG:CG + 24].rearrange("p i (h b) -> p i h b", b=3)
            step(v.tensor_tensor(rsc, rsc, gate[:, 0:4, :, 0], ALU.mult))
            for i in range(TT):
                dve.wait_ge(sem("ct_mm"), i + 1)
                v.tensor_copy(PTC[:, i], PS[:, 2 * (i % 2):2 * (i % 2) + 2, 0:128]).then_inc(sem("ct_ev"), 1)
                dve.wait_ge(sem("co_mm"), i + 1)
                v.tensor_tensor(ON[:, i].rearrange("p (h d) -> p h d", d=HD),
                                PS[:, 4 + i].rearrange("p (h d) -> p h d", d=HD), bc(rsc[:, i], HD), ALU.mult)\
                    .then_inc(sem("co_ev"), 1)
            dve.wait_ge(sem("rows_out"), 96)
            dve.wait_ge(sem("stored"), 48)
            step(v.memset(QB, 0.0))
            for k in range(HKV):
                r = slice(64 * k, 64 * k + 64)
                step(v.tensor_copy(QB[r, :, 4 * k:4 * k + 4], QT[r, :, L:T].rearrange("p g s -> p s g")))
            step(v.tensor_copy(KNEW, new))
            g8 = zt[0:NS, 4, CG:CG + 24].rearrange("p (h b) -> p b h", b=3)
            one = C("onehot", p=NS).rearrange("p (s c) -> p s c", s=NS)[:, :, 0:8]
            for b in range(3):
                ins = v.tensor_tensor(GD[:, b], g8[:, b].unsqueeze(1).to_broadcast([NS, NS, 8]), one, ALU.mult)
                if b < 2:
                    step(ins)
                else:
                    ins.then_inc(once("gd"), 1)

            sq3 = [16, NSEL, NSEL]
            by_m = lambda a: a.unsqueeze(1).to_broadcast(sq3)
            num = C("number", p=16)

            def compressed_step(u):
                if u in (9, 11, 13, 15):
                    x = u - 9
                    dve.wait_ge(sem("sh_mm"), x // 2 + 1)
                    v.tensor_copy(CX[x // 4][:, x % 4:x % 4 + 2].rearrange("p s c -> p (s c)"), PS[0:NCMP, 5])\
                        .then_inc(sem("sh_ev"), 1)
                elif u in (16, 17):
                    if u == 16:
                        dve.wait_ge(sem("sh_ev"), 4)
                    sq = SQX[:, 512 * (u - 16):512 * (u - 16) + 512].rearrange("p (s c) -> p s c", s=4)
                    step(v.tensor_tensor(sq, CX[u - 16][:, :, 0:128], CX[u - 16][:, :, 0:128], ALU.mult))
                elif u == 18:
                    v.tensor_reduce(KST, SQX.rearrange("p (s k d) -> p s k d", s=NS, k=2), AX, ALU.add)\
                        .then_inc(once("kst_x"), 1)
                elif u in (20, 21):
                    n = u - 20
                    dve.wait_ge(*done("kst_xr"))
                    ck = CX[n][:, :, 0:128].rearrange("p s (k d) -> p s k d", d=HD)
                    step(v.tensor_tensor(ck, ck, bc(KST[:, 4 * n:4 * n + 4], HD), ALU.mult))
                    gain = V("kg", 0, 64, NCMP).unsqueeze(1).unsqueeze(1).to_broadcast([NCMP, 4, 2, HD])
                    ins = v.tensor_tensor(ck, ck, gain, ALU.mult)
                    if n == 0:
                        step(ins)
                    else:
                        ins.then_inc(once("cx"), 1)
                elif u in (23, 26):
                    n = (u - 23) // 3
                    dve.wait_ge(sem("kx_mm"), n + 1)
                    v.tensor_copy(KCT[:, 4 * n:4 * n + 4].rearrange("p s c -> p (s c)"), PS[:, 5, 0:4 * NCMP])\
                        .then_inc(sem("kx_ev"), 1)
                elif u == 29:
                    dve.wait_ge(*done("cxs_mm"))
                    v.tensor_copy(PCT, PS[0:NCMP, 5, 0:64]).then_inc(once("cxs"), 1)
                elif u == 32:
                    dve.wait_ge(*done("cxt_mm"))
                    v.tensor_reduce(CMAX[:, 0:1], PS[0:64, 5, 0:NCMP], AX, ALU.max, negate=True)\
                        .then_inc(once("cxm"), 1)
                elif u == 35:
                    dve.wait_ge(*done("cxe"))
                    step(v.reciprocal(CMAX[:, 2:3], CMAX[:, 1:2]))
                    v.tensor_scalar(PCR, PCR, CMAX[:, 2:3], None, ALU.mult).then_inc(once("cxp"), 1)
                elif u == 38:
                    dve.wait_ge(*done("cxp_mm"))
                    step(v.tensor_copy(PCT, PS[0:NCMP, 5, 0:64]))
                    v.tensor_reduce(PCG, PCT.rearrange("p (n g) -> p n g", g=G), AX, ALU.add).then_inc(once("pcg"), 1)
                elif u == 41:
                    dve.wait_ge(*done("gb_mm"))
                    step(v.tensor_copy(GB.rearrange("p b n -> p (b n)"), PS[:, 5, 64:256]))
                    v.tensor_tensor(OACC, PS[:, 5, 0:64], GB[:, 0], ALU.mult).then_inc(sem("oacc"), 1)
                    dve.wait_ge(*done("imp_mm"))
                    step(v.tensor_tensor(SCO, PS[0:16, 5, 256:256 + NSEL], C("bonus", p=16), ALU.add))
                elif u == 42:
                    step(v.tensor_tensor(T1, by_m(SCO), bc(SCO, NSEL), ALU.is_gt))
                elif u == 43:
                    step(v.tensor_tensor(T2, by_m(SCO), bc(SCO, NSEL), ALU.is_equal))
                elif u == 44:
                    step(v.tensor_tensor(T3, by_m(num), bc(num, NSEL), ALU.is_lt))
                elif u == 45:
                    step(v.tensor_tensor(T2, T2, T3, ALU.mult))
                elif u == 46:
                    step(v.tensor_tensor(T1, T1, T2, ALU.add))
                elif u == 47:
                    step(v.tensor_reduce(RANK, T1, AX, ALU.add))
                    v.tensor_scalar(RANK, RANK, float(TOPK), None, ALU.is_lt).then_inc(once("rank"), 1)
                elif u == 49:
                    dve.wait_ge(*done("sel_mm"))
                    v.tensor_copy(SELT, PS[0:NSEL, 5, 0:16]).then_inc(once("selt"), 1)
                elif u == 52:
                    dve.wait_ge(*done("bs_mm"))
                    v.tensor_scalar(BS.rearrange("p s k -> p (s k)"), PS[:, 5, 0:16], -1.0, -NEG, ALU.add, ALU.mult)\
                        .then_inc(once("bs"), 1)
                    for b in range(2):
                        dve.wait_ge(sem("sn_mm"), b + 1)
                        v.tensor_tensor(SN[b], PS[0:NS, 5, 64 + 64 * b:128 + 64 * b], C("newmask", p=NS), ALU.add)\
                            .then_inc(sem("sn"), 1)

            NU = len(UNITS)
            for u in range(NU + 1):
                compressed_step(u)
                if u < NU:
                    i = UNITS[u][0]
                    dve.wait_ge(sem("s_mm"), u + 1)
                    if u >= 3:
                        dve.wait_ge(sem("ex"), u - 2)
                    v.tensor_reduce(nm[u % 3], PS[:, u % 3, 0:128 * i + 128], AX, ALU.max, negate=True)\
                        .then_inc(sem("mx"), 1)
                if u:
                    w = u - 1
                    i = UNITS[w][0]
                    dve.wait_ge(sem("t_mm"), w + 1)
                    if w >= 3:
                        dve.wait_ge(sem("pv_mm"), w - 2)
                    v.tensor_copy(PT[w % 3][:, 0:i + 1].rearrange("p k t -> p (k t)"),
                                  PS[:, 3 + w % 2, 0:128 * i + 128]).then_inc(sem("pt_ev"), 1)
                if u % 16 == 0 and u:
                    i = u // 16 - 1
                    step(v.reciprocal(rs[:, i], rs[:, i]))
                    step(v.tensor_tensor(rs[:, i].rearrange("p b h -> p h b"),
                                         rs[:, i].rearrange("p b h -> p h b"), gate[:, i, :, 1:3], ALU.mult))
                    dve.wait_ge(sem("pv_mm"), u)
                    dve.wait_ge(sem("co_ev"), 4)
                    on = ON[:, i].rearrange("p (h d) -> p h d", d=HD)
                    for b in range(2):
                        t = TQ[:, b].rearrange("p (h d) -> p h d", d=HD)
                        step(v.tensor_tensor(t, PS[:, 6 + b].rearrange("p (h d) -> p h d", d=HD),
                                             bc(rs[:, i, b], HD), ALU.mult))
                        ins = v.tensor_tensor(on, on, t, ALU.add)
                        if b == 0:
                            step(ins)
                        else:
                            ins.then_inc(sem("on"), 1)
            for i in range(TT):
                dve.wait_ge(sem("ont_mm"), i + 1)
                v.tensor_copy(ONT[:, :, 128 * i:128 * i + 128], PS[:, i].rearrange("p (c t) -> p c t", c=4))\
                    .then_inc(sem("ont"), 1)
            dve.wait_ge(sem("sn"), 2)
            dve.wait_ge(*done("bs"))
            kt = 0
            for n, (b, s0) in enumerate(ROUNDS):
                per = 4 if b == 0 else 1
                ni = 4 * per
                if n:
                    dve.wait_ge(sem("sv_mm"), 4 * n)
                for x in range(s0, s0 + 4):
                    m = 4 * n + x - s0
                    for q in range(per):
                        dve.wait_ge(sem("ktx_mm"), kt + q + 1)
                        if kt + q >= 4:
                            dve.wait_ge(sem("sx_mm"), kt + q - 3)
                        at = 4 * ((kt + q) % 4)
                        v.tensor_copy(KTX[:, at:at + 4].rearrange("p i t -> p (i t)"), PS[:, (kt + q) % 4])\
                            .then_inc(sem("ktx"), 1)
                    kt += per
                    dve.wait_ge(sem("sx_mm"), kt)
                    ps = PS[:, 4 + m % 2, 0:8 * ni]
                    if b == 0:
                        bias = BS[:, x].unsqueeze(1).unsqueeze(3).to_broadcast([128, 16, 2, 4])
                        v.tensor_tensor(SX[:, x - s0].rearrange("p i (k g) -> p i k g", k=2),
                                        ps.rearrange("p (i k g) -> p i k g", k=2, g=4), bias, ALU.add)\
                            .then_inc(sem("sx"), 1)
                    else:
                        v.tensor_copy(SX[:, x - s0, 0:ni].rearrange("p i h -> p (i h)"), ps).then_inc(sem("sx"), 1)
                dve.wait_ge(sem("sx"), 4 * n + 4)
                m1 = M1.rearrange("p (s h) -> p s h", s=4)
                v.tensor_reduce(m1, SX[:, :, 0:ni].rearrange("p s i h -> p s h i"), AX, ALU.max).then_inc(sem("m1"), 1)
                dve.wait_ge(sem("mt_mm"), n + 1)
                step(v.tensor_reduce(SM, PS[0:32, 6, 0:136], AX, ALU.max))
                v.tensor_scalar(DG, ident[0:32, 0:32], SM, None, ALU.mult).then_inc(sem("dg"), 1)
                dve.wait_ge(sem("mb_mm"), n + 1)
                mb = PS[:, 6, 0:32]
                v.tensor_tensor(SX[:, :, 0:ni], SX[:, :, 0:ni],
                                mb.rearrange("p (s h) -> p s h", s=4).unsqueeze(2).to_broadcast([128, 4, ni, 8]),
                                ALU.subtract).then_inc(sem("sxs"), 1)
                new = SN[b][:, 8 * s0:8 * s0 + 32]
                v.tensor_tensor(new, new, mb[0:NS], ALU.subtract).then_inc(sem("sxm"), 1)
                dve.wait_ge(sem("sxe"), 2 * n + 2)
                v.tensor_reduce(m1, SX[:, :, 0:ni].rearrange("p s i h -> p s h i"), AX, ALU.add).then_inc(sem("r1"), 1)
                dve.wait_ge(sem("sum_mm"), n + 1)
                step(v.reciprocal(COEF, PS[:, 6, 64:96]))
                step(v.tensor_tensor(COEF, COEF, GB[:, 1 + b, 8 * s0:8 * s0 + 32], ALU.mult))
                dve.wait_ge(sem("sv_mm"), 4 * n + 4)
                v.tensor_copy(SO, PS[0:8, 7]).then_inc(sem("so"), 1)
                dve.wait_ge(sem("so_mm"), n + 1)
                step(v.tensor_tensor(OT[:, 0:32], PS[:, 6, 128:160], COEF, ALU.mult))
                v.tensor_tensor(OACC[:, 8 * s0:8 * s0 + 32], OACC[:, 8 * s0:8 * s0 + 32], OT[:, 0:32], ALU.add)\
                    .then_inc(sem("oacc"), 1)
            dve.wait_ge(sem("oacc"), 5)
            oa = OACC.rearrange("p (s k j q) -> p k q j s", k=2, j=2, q=2)
            for k in range(2):
                for q in range(2):
                    ins = v.tensor_copy(ONT[64 * q:64 * q + 64, 2 * k:2 * k + 2, L:T], oa[64 * k:64 * k + 64, k, q])
                    if k + q < 2:
                        step(ins)
                    else:
                        ins.then_inc(once("nsa_done"), 1)


            norm_apply("n3", "n1")
            for b in range(4):
                dve.wait_ge(sem("b_hi"), b + 1)
                v.tensor_tensor(bL[b], zf[:, 4 * b:4 * b + 4], bH[b], ALU.subtract).then_inc(sem("b_lo"), 1)
            with dve.Fori(0, 4) as dq:
                adds = 0
                for bp in range(2):
                    for q in range(4):
                        dve.wait_ge(sem("sg"), dq * 8 + 4 * bp + q + 1)
                        dve.wait_ge(sem("prod"), dq * 16 + units_before(N_MIX + 3 * bp + 2) + q + 1)
                        m = mixT[:, bass.ds(dq * 2 + q % 2, 1)].rearrange("p k t -> p (k t)")
                        if bp == 0 and q < 2:
                            v.tensor_tensor(halves(m), pair(2 * q), halves(SG[q]), ALU.mult)\
                                .then_inc(sem("mix_mul"), 1)
                            continue
                        dve.wait_ge(sem("mix_add"), dq * 6 + adds + 1)
                        v.tensor_tensor(halves(GP), pair(2 * q), halves(SG[q]), ALU.mult).then_inc(sem("mix_mul"), 1)
                        dve.wait_ge(sem("mix_mul"), dq * 8 + 4 * bp + q + 5)
                        v.tensor_tensor(m, m, GP, ALU.add).then_inc(sem("mix_add"), 1)
                        adds += 1
            for k in range(KT):
                dve.wait_ge(sem("m_hi"), k + 1)
                v.tensor_tensor(mL[:, k], mixT[:, k], mH[:, k], ALU.subtract).then_inc(sem("m_lo"), 1)
            for n in range(8):
                dve.wait_ge(sem("prod"), units_before(N_OUT) + n + 1)
                v.tensor_tensor(halves(xT[:, n]), halves(xT[:, n]), pair(2 * (n % 4)), ALU.add)\
                    .then_inc(sem("wo_ev"), 1)
            dve.wait_ge(sem("wo_ev"), 8)
            dve.wait_ge(sem("n2_rs"), 1)
            norm_apply("n2", "n2")
            with dve.Fori(0, 2) as hf:
                with dve.Fori(0, 4) as i:
                    for q in range(4):
                        n = hf * 16 + i * 4 + q
                        tile = lambda part: part[:, bass.ds(i * 4 + q, 1)].rearrange("p k t -> p (k t)")
                        dve.wait_ge(sem("u_free"), n + 5)
                        v.tensor_tensor(US[q % 2], UR[q % 2], UR[q % 2], ALU.mult).then_inc(sem("u_sq"), 1)
                        dve.wait_ge(sem("u_sq"), n + 3)
                        v.tensor_copy(tile(uH), US[q % 2]).then_inc(sem("u_hi"), 1)
                        dve.wait_ge(sem("u_hi"), n + 1)
                        v.tensor_tensor(tile(uL), US[q % 2], tile(uH), ALU.subtract).then_inc(sem("u_lo"), 1)
                        dve.wait_ge(sem("u_lo"), n + 1)
                with dve.Fori(0, 2) as e:
                    for f in range(2):
                        for j in range(2):
                            dve.wait_ge(sem("prod"), hf * 32 + e * 8 + units_before(N_MLP + 8) + 4 * f + j + 3)
                            x = halves(xT[:, bass.ds(e * 4 + 2 * f + j, 1)].rearrange("p k t -> p (k t)"))
                            v.tensor_tensor(x, x, pair(4 * f + 2 * j), ALU.add).then_inc(sem("y_free"), 1)
            for n in range(10):
                w = 128 if n < 8 else NS
                dve.wait_ge(sem("yt_mm"), n + 1)
                v.tensor_copy(YT[0:w, n // 2, 512 * (n % 2):512 * (n % 2) + 512], PS[0:w, n % 8])\
                    .then_inc(sem("y_ev"), 1)

        @block.gpsimd
        def _(gp):
            p = nc.gpsimd
            step = steps(gp, "pool_step")
            p.memset(zt[:, 4, :], 0.0).then_inc(sem("zt_zero"), 1)

            def lower(n, i=0, cols=CHUNK):
                gp.wait_ge(sem("w_hi"), i + n + 1)
                c = slice(0, cols)
                p.tensor_tensor(WL[n % 2][:, :, c], WR[n % 2][:, :, c], WH[n % 2][:, :, c], ALU.subtract)\
                    .then_inc(sem("w_lo"), 1)

            with gp.Fori(0, 5) as i:
                for u in range(2):
                    lower(u, i * 2)
            lower(10, cols=128)
            lower(11)
            with gp.Fori(0, 4) as i:
                for u in range(2):
                    lower(12 + u, i * 2)
            lower(20, cols=24)
            gp.wait_ge(sem("cum"), 4)
            gp.wait_ge(*done("q_act"))
            gp.wait_ge(*done("fg"))
            for lev in range(LEVELS):
                half = 1 << lev
                if lev >= 2:
                    gp.wait_ge(sem("a_ready"), 2 * lev - 2)
                blk = lambda ap: ap.rearrange("p (n q h) -> p n q h", q=2, h=half)
                b, e = blk(B), blk(EL[lev % 2])
                mid = b[:, :, 0, half - 1:half].to_broadcast([128, 2048 // (2 * half), half])
                p.tensor_tensor(e[:, :, 0], mid, b[:, :, 0], ALU.subtract).then_inc(sem("dist"), 1)
                p.tensor_tensor(e[:, :, 1], b[:, :, 1], mid, ALU.subtract).then_inc(sem("dist"), 1)
            gp.wait_ge(sem("a_ready"), 2 * LEVELS)
            b = B.rearrange("p (n t) -> p n t", t=128)
            p.tensor_tensor(E0.rearrange("p (n t) -> p n t", t=128), b[:, :, 127:128].to_broadcast([128, 16, 128]),
                            b, ALU.subtract).then_inc(sem("dist"), 1)

            gp.wait_ge(sem("prod"), units_before(N_MIX))
            for w in WP:
                step(p.memset(w[:, :, 0:HIST], 0.0))
            u = zf[:, ZU:ZU + 4]
            step(p.tensor_copy(WP[0][:, :, HIST:HIST + 1], u[:, :, 0:1]))
            step(p.tensor_tensor(WP[0][:, :, HIST + 1:], u[:, :, 1:L], u[:, :, 0:L - 1], ALU.add))
            for n in (1, 2, 3):
                sh = 1 << n
                src, dst = WP[(n - 1) % 2], WP[n % 2]
                a, b = (n - (n - 1) % 2, n - n % 2)
                step(p.tensor_tensor(dst[:, b:, HIST:], src[:, a:, HIST:], src[:, a:, HIST - sh:HIST + L - sh], ALU.add))
            for g in range(4):
                first = WIN[g][:, HIST:HIST + 16]
                ins = p.tensor_tensor(first, first, C("corr", 16 * g, 16 * g + 16), ALU.mult)
                if g < 3:
                    step(ins)
                else:
                    ins.then_inc(sem("win"), 1)
            row = lambda name: A[name].rearrange("o n (r t) a k d -> (o n r) (t a k d)", t=16)
            gather = lambda slot, x, name: p.indirect_dma_start(
                slot, None, row(name), bass.IndirectOffsetOnAxis(idx[:, NS + x:NS + x + 1], 0))
            gp.wait_ge(*done("idx"))
            gp.wait_ge(sem("pd"), 8)
            gp.wait_ge(sem("ss_done"), 8)
            gp.wait_ge(sem("st_out"), 128)
            for x in range(NS + 1):
                if x < NS:
                    if x >= 2:
                        gp.wait_ge(sem("c_red"), x - 1)
                    gather(Y[x % 2], x, "cache_cmp_kv").then_inc(sem(f"xc{x % 2}"), 16)
                if x:
                    y = x - 1
                    gp.wait_ge(sem(f"xc{y % 2}"), 16 * (y // 2 + 1))
                    if y == 0:
                        gp.wait_ge(sem("pool_mm"), 4)
                        gp.wait_ge(sem("stored"), 48)
                    t = Y[y % 2].rearrange("p (t c) -> p t c", t=16)
                    for n in (8, 4, 2):
                        step(p.tensor_tensor(t[:, 0:n], t[:, 0:n], t[:, n:2 * n], ALU.add))
                    p.tensor_tensor(S16[y], t[:, 0], t[:, 1], ALU.add).then_inc(sem("c_red"), 1)
            gp.wait_ge(sem("on"), 4)
            for x in range(NS):
                if x == 3:
                    gp.wait_ge(sem("sv_mm"), 4)
                if x == 4:
                    gp.wait_ge(sem("sv_mm"), 8)
                if x > 4:
                    gp.wait_ge(sem("sv_mm"), 8 + x - 4)
                gather(XS[x], x, "cache_slc_kv").then_inc(sem(f"xs{x % 5}"), 16)
            with gp.Fori(0, 30) as i:
                for u in range(2):
                    lower(N_MIX + u, i * 2)


NAMES = ["x_prompt", "x_sample", "state_gla", "state_hgrn", "state_pool", "cache_cmp_kv", "cache_slc_kv",
         "cache_win_kv", "gla_wa2", "pool_w", "w_branch", "w_gate", "w_out", "mlp_w1", "mlp_w2"]
OUTS = [("y_prompt", (1, 512, 1024)), ("y_sample", (8, 1, 1024)), ("gla_prompt", (1, 1, 4, 64, 128)),
        ("gla_sample", (1, 8, 4, 64, 128)), ("hgrn_prompt", (1, 1, 4, 64, 128)), ("hgrn_sample", (1, 8, 4, 64, 128)),
        ("pool_prompt", (1, 1, 15, 512)), ("pool_sample", (1, 8, 15, 512)),
        ("cmp_rows_prompt", (1, 1, 512, 2, 2, 64)), ("cmp_rows_sample", (1, 8, 1, 2, 2, 64)),
        ("slc_rows_prompt", (1, 1, 512, 2, 2, 64)), ("slc_rows_sample", (1, 8, 1, 2, 2, 64)),
        ("win_rows_prompt", (1, 1, 512, 2, 2, 64)), ("win_rows_sample", (1, 8, 1, 2, 2, 64))]


def kernel(**inputs):
    import concourse.bacc as bacc
    from concourse.bass_utils import run_bass_kernel_spmd

    a = {k: np.asarray(v) for k, v in inputs.items()}
    arrays = {n: np.ascontiguousarray(a[n]) for n in NAMES}
    w = a["w_in"][0]
    sizes = (256, 256, 512, 512, 16, 256, 256, 512, 512, 512, 512, 128, 128, 128, 128, 128, 128, 24)
    at = np.cumsum((0,) + sizes)
    gq, gk, gv, gr, ga, hq, hf, hi, hg, pu, nq, ck, cv, sk, sv, wk, wv, ng = (
        slice(at[i], at[i + 1]) for i in range(len(sizes)))
    order = (gr, hg, pu, gq, hq, gk, hf, ga, gv, hi, nq, ck, cv, sk, sv, wk, wv, ng)
    arrays["w_in"] = np.ascontiguousarray(np.concatenate([w[:, o] for o in order], 1))
    cols = lambda v, k: v.reshape(k, 128).T
    rows = lambda v: np.broadcast_to(v.reshape(1, -1), (128, v.size))
    arrays["vectors"] = np.ascontiguousarray(np.concatenate([
        cols(a["norm1_g"][0], 8), cols(a["norm2_g"][0], 8), cols(a["b_gate"][0], 32), cols(a["pool_scale"][0], 4),
        cols(a["gla_ba"][0], 2), cols(a["hgrn_lb_param"][0], 2), cols(a["gla_norm_g"][0], 1),
        cols(a["hgrn_norm_g"][0], 1), rows(a["nsa_q_norm_g"][0]), rows(a["nsa_k_norm_g"][0]),
        (np.arange(128) % 8).astype(np.float32)[:, None]], 1))
    arrays["tables"] = constants()[0]
    arrays["pages"] = np.ascontiguousarray(np.repeat(a["page_table"].T, 8, axis=0))

    nc = bacc.Bacc("TRN2", target_bir_lowering=False, num_devices=1)
    A = {n: nc.dram_tensor(n, x.shape, mybir.dt.from_np(x.dtype), kind="ExternalInput").ap()
         for n, x in arrays.items()}
    for n, shape in OUTS:
        A[n] = nc.dram_tensor(n, shape, mybir.dt.float32, kind="ExternalOutput").ap()
    build(nc, A)
    r = run_bass_kernel_spmd(nc, [arrays], core_ids=[0])
    return tuple(r.results[0][n] for n, _ in OUTS)
```

```python
import concourse.bass as bass
from concourse import mybir
from contextlib import ExitStack
import numpy as np

D, L, NS, T = 1024, 512, 8, 520
HALF = T // 2
KT = D // 128
TT = 4
FM, TM, GA = 2560, 2328, 16
CHUNK = 256
HKV, HD, G = 2, 64, 4
NCMP, NSEL, TOPK = 127, 33, 16
NEG = -1e30
EPS = 1e-6
LEVELS = 7
WINDOWS = (2, 4, 8, 16)
HIST = 15

CV, CQ, CK, CS, CW, CG = 0, 1024, 1536, 1792, 2048, 2304
ZG, ZU, ZQ, ZK = 0, 8, 12, 16


def constants():
    p = np.arange(128)
    parts = {}

    def put(name, a):
        full = np.zeros((128, a.shape[1]), np.float32)
        full[:a.shape[0]] = a
        parts[name] = full

    put("ident", np.eye(128))
    put("ones", np.ones((128, 128)))
    put("causal", np.where(p[None, :] <= p[:, None], 0.0, NEG))
    masks = []
    for lev in range(LEVELS):
        half = 1 << lev
        same = (p[:, None] // (2 * half)) == (p[None, :] // (2 * half))
        masks.append(same & (p[:, None] % (2 * half) < half) & (p[None, :] % (2 * half) >= half))
    masks.append(np.eye(128, dtype=bool))
    put("masks", np.concatenate(masks, 1).astype(np.float32))
    tok = np.arange(L)[:, None]
    c32 = np.arange(32)[None, :]
    pm = ((tok >= 16 * c32) & (tok < 16 * c32 + 32) & (c32 < 31)) / 32.0
    put("pool", pm.reshape(TT, 128, 32).transpose(1, 0, 2).reshape(128, TT * 32))
    c = np.arange(128)[None, :]
    put("shift", np.where((p[:, None] == c) | (p[:, None] == c + 1), 1 / 32.0, 0.0))
    n = np.arange(NSEL)[None, :]
    put("overlap", ((p[:NCMP, None] // 4 == n) | ((p[:NCMP, None] + 1) // 4 == n)).astype(np.float32))
    put("expand", (np.arange(NSEL)[:, None] == p[None, :] // 4).astype(np.float32))
    seen = ((16 * c32 + 31 <= tok) & (c32 < 31)).astype(np.float32)
    seen = seen.reshape(TT, 128, 32).transpose(1, 0, 2).reshape(128, TT * 32)
    put("cmp01", seen)
    put("cmpneg", np.where(seen > 0, 0.0, NEG))
    t16 = np.arange(16)
    put("corr", np.tile(np.concatenate([w / np.minimum(w, t16 + 1.0) for w in WINDOWS]), (128, 1)))
    put("newmask", np.where(np.arange(NS)[:, None] == np.arange(64)[None, :] // 8, 0.0, NEG))
    put("onehot", np.repeat(np.eye(NS), 64, 1))
    bonus = np.zeros((16, NSEL))
    bonus[:, [0, NSEL - 2, NSEL - 1]] = 1000.0
    put("bonus", bonus)
    put("number", np.tile(np.arange(NSEL, dtype=np.float32), (16, 1)))
    put("reset", np.tile((np.arange(L) % 128 != 0).astype(np.float32), (128, 1)))
    off, at = {}, 0
    for k, a in parts.items():
        off[k] = (at, at + a.shape[1])
        at += a.shape[1]
    return np.concatenate(list(parts.values()), 1), off


EVENTS = {
    "pe_event": """la_mm hist_mm tail_mm os_mm ost_mm ckv_mm kct_mm cxs_mm cxt_mm cxp_mm cxo_mm gb_mm imp_mm
           sel_mm bs_mm""".split(),
    "act_event": """lsp lb_e lf_h decs decc ng rq kst_rs cm_e kst_xr cxe""".split(),
    "dve_event": """eps ga_ev idx q_act lb_d fg lf_g qk kdec qdec qm tail oss k_norm q_norm kst ckv kct cm cp
           gd kst_x cx cxs cxm cxp pcg rank selt bs nsa_done""".split(),
}


UNITS_OF = [2] * 10 + [1] + [5] * 10 + [2, 2, 4] * 8 + [2] * 4 + [2] * 32
N_MIX, N_OUT, N_MLP = 21, 45, 49


def units_before(n):
    return sum(UNITS_OF[:n])


SMALL = {}
for _n, _k in (("n1", 8), ("n2", 8), ("bg", 32), ("psc", 4), ("ba", 2), ("lb", 2), ("gn", 1), ("hn", 1),
               ("qg", 64), ("kg", 192), ("r8", 1)):
    SMALL[_n] = (sum(b - a for a, b in SMALL.values()), sum(b - a for a, b in SMALL.values()) + _k)
NSMALL = SMALL["r8"][1]
NCON = constants()[0].shape[1]


def build(nc, A):
    f32, f32r, i32 = mybir.dt.float32, mybir.dt.float32r, mybir.dt.int32
    ACT, ALU, AX = mybir.ActivationFunctionType, mybir.AluOpType, mybir.AxisListType.X
    _, COFF = constants()
    ctx = ExitStack()
    with ctx:
        def sb(name, n, dt=f32):
            return ctx.enter_context(nc.sbuf_tensor(name, [128, n], dt))

        con = sb("con", NCON)
        small = sb("small", NSMALL)
        xT = sb("xT", KT * T)[:].rearrange("p (k t) -> p k t", t=T)
        stat = sb("stat", 400)
        eps = stat[:, 396:397]
        idx = sb("idx", 2 * NS, i32)
        gaT = sb("gaT", T)
        wa2 = sb("wa2", 256)
        tmp = sb("tmp", 3 * T)
        RST, TH = tmp[:, 0:T], [tmp[:, T * i:T * (i + 1)] for i in (1, 2)]
        ZW = 20 * T + 5 * TM
        W0 = ZW + 2 * KT * T

        def place(name, at, n, dt=f32r):
            with ExitStack() as below:
                if at:
                    below.enter_context(nc.sbuf_tensor(name + "_below", [128, at], f32))
                return below.enter_context(nc.sbuf_tensor(name, [128, n], dt))[:]

        def parts(name, at, tiles):
            return place(name, at, tiles * T).rearrange("p (k t) -> p k t", t=T)

        hH, hL = parts("hH", ZW, KT), parts("hL", ZW + KT * T, KT)
        bL = [parts(f"bL{b}", 4 * b * T, 4) for b in range(4)]
        bH = [parts(f"bH{b}", (16 + 4 * b) * T, 4) for b in range(4)]
        mL, mH = parts("mL", 32 * T, KT), parts("mH", 16 * T, KT)
        uH, uL = parts("uH", 0, 16), parts("uL", 16 * T, 16)
        slot = lambda ap: ap.rearrange("p (k n) -> p k n", k=KT)
        WL, WH = [[slot(place(f"{name}{i}", W0 + at + 2048 * i, 2048)) for i in range(2)]
                  for name, at in (("WL", 0), ("WH", 4096))]
        M = sb("M", W0 + 12288)
        WR = [slot(M[:, W0 + 8192 + 2048 * i:W0 + 8192 + 2048 * (i + 1)]) for i in range(2)]
        Z = M[:, 0:ZW]
        zf = Z[:, 0:20 * T].rearrange("p (k t) -> p k t", t=T)
        zt = Z[:, 20 * T:].rearrange("p (i c) -> p i c", c=TM)
        R = M[:, ZW:W0 + 12288]
        PS = ctx.enter_context(nc.psum_tensor("PS", [128, 8, 512], f32))

        def C(name, a=0, b=None, p=128):
            lo, hi = COFF[name]
            return con[0:p, lo + a:(hi if b is None else lo + b)]

        def V(name, a=0, b=None, p=128):
            lo, hi = SMALL[name]
            return small[0:p, lo + a:(hi if b is None else lo + b)]

        ident, ones = C("ident"), C("ones")
        S = {}

        def sem(name):
            if name not in S:
                S[name] = ctx.enter_context(nc.semaphore(name))
            return S[name]

        signalled = {e: 0 for e in EVENTS}

        def once(name):
            e = [e for e in EVENTS if name in EVENTS[e]][0]
            assert EVENTS[e][signalled[e]] == name, name
            signalled[e] += 1
            return sem(e)

        def done(name):
            e = [e for e in EVENTS if name in EVENTS[e]][0]
            return sem(e), EVENTS[e].index(name) + 1

        def steps(eng, name):
            own, n = sem(name), [0]

            def step(ins):
                n[0] += 1
                ins.then_inc(own, 1)
                eng.wait_ge(own, n[0])
            return step

        def pair(bank):
            return PS[:, bank:bank + 2, 0:HALF]

        def halves(ap):
            return ap.rearrange("p (h n) -> p h n", h=2)

        def bc(ap, n):
            return ap.unsqueeze(len(ap.shape)).to_broadcast(list(ap.shape) + [n])


        LF = R[:, 0:4 * T].rearrange("p (k t) -> p k t", t=T)
        KD = R[:, 0:2048].rearrange("p (c k f) -> p c k f", c=4, k=4)
        B = R[:, 2080:4128]
        E0 = R[:, 4160:6208]
        A0 = R[:, 6240:8288]
        A1 = R[:, 12416:14464]
        E1 = R[:, 14464:16512]
        AL, EL = [A0, A1], [E0, E1]
        SIGQ = R[:, 4160:5200].rearrange("p (k t) -> p k t", t=T)
        SIGF = R[:, 5200:6240].rearrange("p (k t) -> p k t", t=T)
        TMPA = R[:, 6240:7280].rearrange("p (k t) -> p k t", t=T)
        SIGG = R[:, 8320:8320 + 8 * T].rearrange("p (k t) -> p k t", t=T)
        SC = R[:, 8320:12416].rearrange("p (g k t) -> p g k t", g=8, k=4)
        ST = R[:, 12416:14464].rearrange("p (c k v) -> p c k v", c=4, k=4)
        OB = R[:, 4160:4160 + 8 * T].rearrange("p (k t) -> p k t", t=T)
        SS = R[:, 8320:12416].rearrange("p (m s k v) -> p m s k v", m=2, s=NS, k=2)
        VB = [R[:, 14464 + 512 * i:14464 + 512 * (i + 1)].rearrange("p (s k v) -> p s k v", s=2, k=2)
              for i in range(2)]
        QM = R[:, 15488:16000]
        OSS = R[0:16, 16000:16512]
        SQ = [zf[:, ZK + i] for i in range(2)]
        RN = [zf[:, ZK + 2 + i] for i in range(2)]
        decS = stat[:, 0:32].rearrange("p (k s) -> p k s", k=4)
        decC = stat[:, 32:48].rearrange("p (k c) -> p k c", k=4)
        lbv = stat[:, 48:60].rearrange("p (k a) -> p k a", k=2)
        gq8 = stat[:, 60:124]

        def flat(ap):
            return ap.rearrange("p a b -> p (a b)")

        def chunks(buf):
            return buf.rearrange("p (k t) -> p k t", k=4)

        def head_cols(k, par):
            h = (k // 2) * 4 + (k % 2) * 2 + par
            return slice(CV + 128 * h, CV + 128 * (h + 1)), h

        w_in = A["w_in"].rearrange("(k p) n -> p k n", p=128)
        w_gate = A["w_gate"].rearrange("o (k p) n -> p (o k) n", p=128)
        w_branch = A["w_branch"].rearrange("o b (c p) n -> p (o b c) n", p=128)
        w_out = A["w_out"].rearrange("o (k p) n -> p (o k) n", p=128)
        w1 = A["mlp_w1"].rearrange("o (k p) n -> p (o k) n", p=128)
        w2 = A["mlp_w2"].rearrange("o (k p) n -> p (o k) n", p=128)
        mixT = M[:, 32 * T:40 * T].rearrange("p (k t) -> p k t", t=T)
        SG = [M[:, 40 * T + T * i:40 * T + T * (i + 1)] for i in range(2)] + [RST, TH[0]]
        GP = TH[1]
        UR = [M[:, 32 * T + T * i:32 * T + T * (i + 1)] for i in range(2)]
        US = TH
        YT = Z[:, 0:5120].rearrange("p (i d) -> p i d", i=5)
        XI = Z[:, 0:5120].rearrange("p (i d) -> p i d", i=5)


        WP = [R[:, a:a + n * (HIST + L)].rearrange("p (g t) -> p g t", g=n)
              for a, n in ((16512, 4), (18624, 3))]
        WIN = [WP[0][:, 0], WP[1][:, 0], WP[0][:, 2], WP[1][:, 2]]
        poolw = zt[:, 0:4, 0:128]
        hist = zt[0:NS * HIST, 0:4, 128:256]
        tail = zt[0:23, 0:4, 256:384]
        PD = zt[:, 0:4, 504:1024]

        TQ = R[:, 0:2560].rearrange("p (i c) -> p i c", i=5)
        QN = R[:, 16512:19072].rearrange("p (i g k d) -> p i g k d", i=5, g=G, k=HKV)
        TK = R[:, 2560:3840].rearrange("p (i c) -> p i c", i=5)
        QT = R[:, 5120:7200].rearrange("p (g t) -> p g t", t=T)
        KTS, KTW = R[:, 7200:7720], R[:, 7720:8240]
        P = [R[:, 8240 + 512 * i:8752 + 512 * i] for i in range(3)]
        PT = [R[:, 9776 + 512 * i:10288 + 512 * i].rearrange("p (k t) -> p k t", k=4) for i in range(3)]
        PTC = R[:, 8240:9264].rearrange("p (i k t) -> p i k t", i=4, k=2)
        CM = R[:, 11312:12336].rearrange("p (i h c) -> p i h c", i=4, h=8)
        CKV = gaT[0:32, 0:256]
        VBK = zf[:, ZK, 0:512].rearrange("p (k c) -> p k c", k=2)
        ON = zt[:, :, 1024:1536]
        ONT = zf[:, ZQ:ZQ + 4]
        rq = stat[:, 128:188].rearrange("p (i h) -> p i h", i=5)
        kcT = stat[:, 188:220]
        nmc = stat[:, 220:252]
        rsc = stat[:, 252:284].rearrange("p (i h) -> p i h", i=4)
        nm = [stat[:, 284 + i:285 + i] for i in range(3)]
        rs = stat[:, 288:352].rearrange("p (i b h) -> p i b h", i=4, b=2)
        kst = stat[0:32, 352:360]

        KTX = zf[:, ZK:ZK + 4].rearrange("p a b -> p (a b)")[:, 0:2048].rearrange("p (i t) -> p i t", i=16)
        KCT = zt[:, 0, 0:8 * NCMP].rearrange("p (s c) -> p s c", s=NS)
        S16 = [zt[:, 3 * (x < 4), 256 * (x % 4):256 * (x % 4) + 256] for x in range(NS)]
        Y = [R[:, 12416 + 4096 * i:12416 + 4096 * (i + 1)] for i in range(2)]
        X = [R[:, 4096 * i:4096 * (i + 1)] for i in range(4)] + [Y[1]]
        SLOT = [3, 2, 1, 0, 4, 3, 2, 1]
        CX = [zt[0:NCMP, 1 + u, 0:1024].rearrange("p (s c) -> p s c", s=4) for u in range(2)]
        SX = zt[:, 3, 0:512].rearrange("p (s i h) -> p s i h", s=4, h=8)
        QB = zt[:, 4, 0:64].rearrange("p (s h) -> p s h", h=8)
        KNEW = zt[:, 4, 64:80].rearrange("p (b s) -> p b s", b=2)
        GB = zt[:, 4, 80:272].rearrange("p (b n) -> p b n", b=3)
        OACC = zt[:, 4, 272:336]
        BS = zt[:, 4, 336:352].rearrange("p (s k) -> p s k", k=2)
        PCR = zt[0:64, 4, 352:479]
        PCT = gaT[0:NCMP, 0:64]
        PCG = gaT[0:NCMP, 64:80]
        SN = [gaT[0:NS, 80 + 64 * b:144 + 64 * b] for b in range(2)]
        M1 = gaT[:, 208:272]
        DG = gaT[0:64, 272:336]
        COEF = gaT[:, 336:400]
        GD = gaT[0:NS, 304:496].rearrange("p (b s h) -> p b s h", b=3, h=8)
        SELT = gaT[0:NSEL, 496:512]
        OT = stat[:, 128:192]
        SO = zt[0:8, 4, 480:1504]
        SCO = stat[0:16, 192:225]
        RANK = stat[0:16, 225:258]
        CMAX = stat[0:64, 258:261]
        KST = stat[0:NCMP, 261:277].rearrange("p (s k) -> p s k", k=2)
        SM = stat[0:64, 277:278]
        SQX = zf[:, ZK:ZK + 4].rearrange("p a b -> p (a b)")[0:NCMP, 0:1024]
        T1 = zf[:, ZK:ZK + 4].rearrange("p a b -> p (a b)")[0:16, 0:NSEL * NSEL].rearrange("p (n m) -> p n m", m=NSEL)
        T2 = zt[0:16, 4, 440:440 + NSEL * NSEL].rearrange("p (n m) -> p n m", m=NSEL)
        T3 = con[0:16, COFF["masks"][0]:COFF["masks"][0] + NSEL * NSEL].rearrange("p (n m) -> p n m", m=NSEL)
        ROUNDS = [(1, 0, 8), (0, 0, 4), (0, 4, 4)]
        SXB = [SX, zt[:, 3, 0:256].rearrange("p (s i h) -> p s i h", s=8, h=8)]
        o_bank = lambda j: (7, 5)[j // 4]

        def xtile(b, s, i):
            if b == 0:
                t = X[SLOT[s]][:, 256 * i:256 * i + 256]
            else:
                t = Y[s // 4][:, 1024 * (s % 4) + 256 * i:1024 * (s % 4) + 256 * i + 256]
            return t[:, 0:128], t[:, 128:256]

        SQN = TH

        block = ctx.enter_context(nc.Block())
        UNITS = [(i, b, h) for i in range(TT) for b in range(2) for h in (7, 6, 5, 4, 0, 1, 2, 3)]

        @block.sync
        def _(sp):
            first = COFF["ones"][1]
            sp.dma_start(con[:, 0:first], A["tables"][:, 0:first]).then_inc(sem("ld_con"), 16)
            for i in range(TT):
                sp.dma_start(XI[:, i], A["x_prompt"][0, 128 * i:128 * (i + 1), :]).then_inc(sem("ld_x"), 16)
            sp.dma_start(XI[0:NS, 4], A["x_sample"].rearrange("s o d -> (s o) d")).then_inc(sem("ld_x"), 16)
            sp.dma_start(small[:], A["vectors"]).then_inc(sem("ld_con"), 16)
            def load(n, src, cols=CHUNK):
                sp.dma_start(WR[n % 2][:, :, 0:cols], src).then_inc(sem(f"raw{n % 2}"), 16)

            def reload(first, i, src):
                sp.wait_ge(sem("w_lo"), i * 2 + first - 1)
                load(first, src)

            load(0, w_in[:, :, 0:CHUNK])
            load(1, w_in[:, :, CHUNK:2 * CHUNK])
            sp.dma_start(con[:, first:], A["tables"][:, first:]).then_inc(sem("ld_tab"), 16)
            sp.dma_start(wa2[0:GA, :], A["gla_wa2"][0]).then_inc(sem("ld_wa2"), 16)
            sp.dma_start(idx[:, 0:NS], A["pages"]).then_inc(sem("ld_idx"), 16)
            with sp.Fori(0, 4) as i:
                for u in range(2):
                    reload(2 + u, i, w_in[:, :, bass.ds(i * 512 + 512 + 256 * u, CHUNK)])
            sp.wait_ge(sem("w_lo"), 9)
            load(10, w_in[:, :, FM:FM + 128], 128)
            sp.wait_ge(sem("w_lo"), 10)
            load(11, w_in[:, :, FM + GA:FM + GA + CHUNK])
            with sp.Fori(0, 4) as i:
                for u in range(2):
                    reload(12 + u, i, w_in[:, :, bass.ds(i * 512 + FM + GA + 256 + 256 * u, CHUNK)])
            sp.wait_ge(sem("w_lo"), 19)
            load(20, w_in[:, :, FM + GA + 9 * CHUNK:FM + GA + TM], 24)
            sp.wait_ge(sem("o_mm"), 8)
            for m, name in enumerate(("state_gla", "state_hgrn")):
                src = A[name].rearrange("o s (k q) f v -> q f (o s) k v", q=2)
                for q in range(2):
                    sp.dma_start(SS[64 * q:64 * q + 64, m], src[q]).then_inc(sem("ld_ss"), 16)
            for g in range(4):
                sp.dma_start(poolw[:, g], A["pool_w"][0, g]).then_inc(sem("ld_pool"), 16)
            sp.dma_start(hist, A["state_pool"].rearrange("o s j (g c) -> (o s j) g c", g=4))\
              .then_inc(sem("ld_pool"), 16)
            sp.dma_start(A["pool_sample"][0, :, 0:HIST - 1], A["state_pool"][0, :, 1:HIST])\
              .then_inc(sem("stored"), 16)
            sp.wait_ge(sem("st"), 4)
            for m, name in enumerate(("gla_prompt", "hgrn_prompt")):
                dst = A[name].rearrange("o b (k q) f v -> q f (o b k) v", q=2)
                for q in range(2):
                    sp.dma_start(dst[q], ST[64 * q:64 * q + 64, 3, 2 * m:2 * m + 2]).then_inc(sem("st_out"), 16)
            sp.wait_ge(sem("ss_done"), 8)
            for m, name in enumerate(("gla_sample", "hgrn_sample")):
                dst = A[name].rearrange("o s (k q) f v -> q f (o s) k v", q=2)
                for q in range(2):
                    sp.dma_start(dst[q], SS[64 * q:64 * q + 64, m]).then_inc(sem("st_out"), 16)
            sp.wait_ge(*done("tail"))
            sp.dma_start(A["pool_prompt"][0, 0].rearrange("j (g c) -> j g c", g=4), tail[0:HIST])\
              .then_inc(sem("stored"), 16)
            sp.dma_start(A["pool_sample"][0, :, HIST - 1].rearrange("s (g c) -> s g c", g=4),
                         tail[HIST:HIST + NS]).then_inc(sem("stored"), 16)
            sp.wait_ge(*done("k_norm"))
            for name, col in (("cmp", CK), ("slc", CS), ("win", CW)):
                sp.dma_start(A[name + "_rows_prompt"].rearrange("o b (i p) a k d -> p (o b i) (a k d)", p=128),
                             zt[:, 0:4, col:col + 256]).then_inc(sem("rows_out"), 16)
                sp.dma_start(A[name + "_rows_sample"].rearrange("o s b a k d -> (o s b) (a k d)"),
                             zt[0:NS, 4, col:col + 256]).then_inc(sem("rows_out"), 16)
            for n in range(2):
                sp.wait_ge(sem("c_red"), 7 + n)
                sp.dma_start(Y[n].rearrange("p (s c) -> p s c", s=4),
                             A["cache_win_kv"].rearrange("o s (p i) a k d -> p (o s) (i a k d)", i=4)
                             [:, 4 * n:4 * n + 4]).then_inc(sem(f"xw{n}"), 16)
            sp.wait_ge(sem("rows_out"), 96)
            sp.wait_ge(sem("sv_mm"), 13)
            with sp.Fori(0, 4) as dq:
                for v in range(6):
                    bp, kind = v // 3, v % 3
                    sp.wait_ge(sem("w_lo"), dq * 6 + N_MIX + v - 1)
                    if kind < 2:
                        src = w_gate[:, :, bass.ds(dq * 256 + 2048 * bp + 1024 * kind, CHUNK)]
                    else:
                        src = w_branch[:, 8 * bp:8 * bp + 8, bass.ds(dq * 256, CHUNK)]
                    load(N_MIX + v, src)
            with sp.Fori(0, 2) as i:
                for u in range(2):
                    reload(N_OUT + u, i, w_out[:, :, bass.ds(i * 512 + 256 * u, CHUNK)])
            with sp.Fori(0, 2) as hf:
                with sp.Fori(0, 4) as i:
                    for u in range(2):
                        reload(N_MLP + u, hf * 8 + i, w1[:, :, bass.ds(hf * 2048 + i * 512 + 256 * u, CHUNK)])
                with sp.Fori(0, 4) as dq:
                    for kq in range(2):
                        reload(N_MLP + 8 + kq, hf * 8 + dq,
                               w2[:, bass.ds(hf * 16 + 8 * kq, 8), bass.ds(dq * 256, CHUNK)])
            for i in range(5):
                sp.wait_ge(sem("y_ev"), 2 * i + 2)
                if i < TT:
                    sp.dma_start(A["y_prompt"][0, 128 * i:128 * i + 128], YT[:, i]).then_inc(sem("stored"), 16)
                else:
                    sp.dma_start(A["y_sample"].rearrange("s o d -> (s o) d"), YT[0:NS, i])\
                      .then_inc(sem("stored"), 16)
            sp.wait_ge(sem("stored"), 16 * 8)
            sp.wait_ge(sem("st_out"), 128)

        @block.tensor
        def _(pe):
            mm, tr = nc.tensor.matmul, nc.tensor.transpose

            def norm_sum(tag, k, bank):
                pe.wait_ge(sem(tag + "_sq"), k + 1)
                for h in range(2):
                    last = mm(PS[:, bank + h, 0:HALF], ones, SQN[k % 2][:, HALF * h:HALF * h + HALF],
                              start=(k == 0), stop=(k == KT - 1))
                last.then_inc(sem(tag + "_mm"), 1)

            def fm_unit(n, j, bank, rhs, k0=0, k1=KT, start=True, stop=True, ready=None):
                for k in range(k0, k1):
                    if ready:
                        pe.wait_ge(sem(ready), k + 1)
                    hi, lo = rhs(k - k0)
                    for w, x in ((WH, hi), (WH, lo), (WL, hi)):
                        for h in range(2):
                            last = mm(PS[:, bank + h, 0:HALF], w[n % 2][:, k, 128 * j:128 * j + 128],
                                      x[:, HALF * h:HALF * h + HALF], start=(start and k == k0 and w is WH and x is hi),
                                      stop=(stop and k == k1 - 1 and w is WL))
                last.then_inc(sem("prod"), 1)

            hk = lambda k: (hH[:, k], hL[:, k])

            def warm(n):
                for _ in range(n):
                    mm(PS[:, 7], ident, con[:, 0:512], start=True, stop=True)

            pe.wait_ge(sem("ld_con"), 16)
            pe.wait_ge(sem("ld_x"), 80)
            for n in range(10):
                i, k4, w = n // 2, 4 * (n % 2), (128 if n < 8 else NS)
                if n >= 8:
                    pe.wait_ge(sem("xt_ev"), n - 7)
                for j in range(4):
                    last = tr(PS[:, n % 8, w * j:w * (j + 1)], XI[0:w, i, 128 * (k4 + j):128 * (k4 + j + 1)],
                              ident[0:w, 0:w])
                last.then_inc(sem("xt"), 1)
            pe.wait_ge(sem("xt_ev"), 10)
            for k in range(KT):
                norm_sum("n1", k, 0)

            with pe.Fori(0, 5) as i:
                for u in range(2):
                    pe.wait_ge(sem("w_lo"), i * 2 + u + 1)
                    for j in range(2):
                        pe.wait_ge(sem("fm_free"), i * 4 + 2 * u + j + 1)
                        fm_unit(u, j, 2 * (2 * u + j), hk, ready="n1_h" if u + j == 0 else None)
            pe.wait_ge(sem("w_lo"), 11)
            pe.wait_ge(sem("fm_free"), 21)
            fm_unit(10, 0, 0, hk)
            pe.wait_ge(sem("fm_free"), 24)
            pe.wait_ge(*done("ga_ev"))

            def tm_unit(n, i, cols):
                m = 128 if i < TT else NS
                t = slice(128 * i, 128 * i + m)
                for k in range(KT):
                    for x, w in ((hH, WH), (hH, WL), (hL, WH)):
                        last = mm(PS[0:m, i, 0:cols], x[:, k, t], w[n % 2][:, k, 0:cols],
                                  start=(k == 0 and x is hH and w is WH), stop=(k == KT - 1 and x is hL))
                last.then_inc(sem("prod"), 1)

            pe.wait_ge(sem("w_lo"), 12)
            for i in range(5):
                pe.wait_ge(sem("tm_free"), i + 1)
                tm_unit(11, i, CHUNK)
            with pe.Fori(0, 4) as c:
                for u in range(2):
                    pe.wait_ge(sem("w_lo"), c * 2 + u + 13)
                    for i in range(5):
                        pe.wait_ge(sem("tm_free"), c * 10 + 5 * u + i + 6)
                        tm_unit(12 + u, i, CHUNK)
            pe.wait_ge(sem("w_lo"), 21)
            for i in range(5):
                pe.wait_ge(sem("tm_free"), 45 + i + 1)
                tm_unit(20, i, 24)

            pe.wait_ge(sem("tm_free"), 55)
            pe.wait_ge(sem("ld_tab"), 16)
            pe.wait_ge(sem("ld_wa2"), 16)
            for k in range(2):
                for h in range(2):
                    last = mm(PS[:, 2 * k + h, 0:HALF], wa2[0:GA, 128 * k:128 * k + 128],
                              gaT[0:GA, HALF * h:HALF * h + HALF], start=True, stop=True)
            last.then_inc(once("la_mm"), 1)
            warm(24)
            pe.wait_ge(sem("la_ev"), 1)
            pe.wait_ge(*done("qk"))
            for step in range(LEVELS + 1):
                if step:
                    pe.wait_ge(sem("a_ready"), 2 * step)
                for g in range(8):
                    c, par = g // 2, g % 2
                    if step:
                        pe.wait_ge(sem("sc_cp"), 8 * (step - 1) + g + 1)
                    for k in range(4):
                        r, t = slice(64 * par, 64 * par + 64), slice(128 * c, 128 * c + 128)
                        if step:
                            a = chunks(AL[(step - 1) % 2])[r, k, t]
                            last = mm(PS[:, g, 128 * k:128 * k + 128], a, a, start=True, stop=True)
                        else:
                            last = mm(PS[:, g, 128 * k:128 * k + 128], zf[r, ZK + k, t], zf[r, ZQ + k, t],
                                      start=True, stop=True)
                    last.then_inc(sem("sc_mm"), 1)
            pe.wait_ge(*done("kdec"))
            pe.wait_ge(sem("sc_cp"), 8 * LEVELS + 8)
            for c in range(4):
                for k in range(4):
                    last = tr(PS[:, c, 128 * k:128 * k + 128], chunks(A0)[:, k, 128 * c:128 * c + 128], ident)
                last.then_inc(sem("kt_mm"), 1)
            for c in range(4):
                pe.wait_ge(sem("kd_ev"), c + 1)
                for par in range(2):
                    for k in range(4):
                        last = mm(PS[64 * par:64 * par + 64, 4 + c, 128 * k:128 * k + 128],
                                  KD[:, c, k, 64 * par:64 * par + 64], zt[:, c, head_cols(k, par)[0]],
                                  start=True, stop=True)
                last.then_inc(sem("ds_mm"), 1)
            pe.wait_ge(sem("st"), 4)
            pe.wait_ge(*done("qdec"))
            for hh in range(8):
                k, par = hh // 2, hh % 2
                r = slice(64 * par, 64 * par + 64)
                for c in range(4):
                    o = PS[:, hh, 128 * c:128 * c + 128]
                    last = mm(o, zt[:, c, head_cols(k, par)[0]], SC[:, 2 * c + par, k], start=True, stop=(c == 0))
                    if c:
                        last = mm(o, ST[r, c - 1, k], chunks(A0)[r, k, 128 * c:128 * c + 128],
                                  start=False, stop=True)
                last.then_inc(sem("o_mm"), 1)
            pe.wait_ge(sem("ob"), 8)
            for g in range(8):
                m = g // 4
                v = zt[0:NS, 4, 512 * m:512 * m + 512].rearrange("p (k q v) -> p k q v", k=2, q=2)
                for par in range(2):
                    for j in range(2):
                        s = 2 * (g % 4) + j
                        last = mm(PS[64 * par:64 * par + 64, g, 256 * j:256 * j + 256],
                                  C("onehot", 64 * s, 64 * s + 64, NS), v[:, :, par, :], start=True, stop=True)
                last.then_inc(sem("vb_mm"), 1)
            pe.wait_ge(sem("ss_done"), 8)
            pe.wait_ge(sem("ld_pool"), 80)
            for g in range(4):
                last = tr(PS[:, 2, 120 * g:120 * g + 120], hist[:, g], ident[0:120, 0:120])
            last.then_inc(once("hist_mm"), 1)
            for g in range(4):
                last = tr(PS[0:23, 3, 128 * g:128 * g + 128], zf[:, ZU + g, 497:520], ident)
            last.then_inc(once("tail_mm"), 1)
            pe.wait_ge(sem("ss_done"), 8)
            pe.wait_ge(*done("qm"))
            for k in range(4):
                for x in range(NS):
                    last = mm(PS[0:16, 0, 128 * k:128 * k + 128], QM[:, 128 * k + 16 * x:128 * k + 16 * x + 16],
                              SS[:, k // 2, x, k % 2], start=(x == 0), stop=(x == NS - 1))
            last.then_inc(once("os_mm"), 1)
            pe.wait_ge(*done("oss"))
            for k in range(4):
                last = tr(PS[:, 1, 16 * k:16 * k + 16], OSS[:, 128 * k:128 * k + 128], ident[0:16, 0:16])
            last.then_inc(once("ost_mm"), 1)
            for g in range(4):
                pe.wait_ge(sem("pd"), 2 * g + 2)
                if g >= 2:
                    pe.wait_ge(sem("pool_ev"), g - 1)
                for h in range(2):
                    last = mm(PS[:, 2 + 2 * (g % 2) + h, 0:HALF], poolw[:, g], PD[:, g, HALF * h:HALF * h + HALF],
                              start=True, stop=True)
                last.then_inc(sem("pool_mm"), 1)

            pe.wait_ge(sem("os_ev"), 2)
            for hh in range(8):
                pe.wait_ge(sem("hn_sq"), hh + 1)
                if hh == 1:
                    pe.wait_ge(sem("pool_ev"), 4)
                if hh >= 4:
                    pe.wait_ge(sem("hn_ln"), hh - 3)
                for h in range(2):
                    last = mm(PS[:, 2 * (hh % 4) + h, 0:HALF], ones, SQ[hh % 2][:, HALF * h:HALF * h + HALF],
                              start=True, stop=True)
                last.then_inc(sem("hn_mm"), 1)

            pe.wait_ge(sem("hn_ln"), 8)
            pe.wait_ge(*done("tail"))
            pe.wait_ge(*done("q_norm"))
            pe.wait_ge(*done("k_norm"))
            for i in range(5):
                w = 128 if i < TT else NS
                for g in range(G):
                    last = tr(PS[:, i, w * g:w * g + w], QN[0:w, i, g].rearrange("p k d -> p (k d)"),
                              ident[0:w, 0:w])
                last.then_inc(sem("qt_mm"), 1)
            for n, col in enumerate((CS, CW)):
                for i in range(TT):
                    last = tr(PS[:, 5 + n, 128 * i:128 * i + 128], zt[:, i, col:col + 128], ident)
                last.then_inc(sem("qt_mm"), 1)
            for n, col in enumerate((CS, CW)):
                last = tr(PS[:, 7, NS * n:NS * n + NS], zt[0:NS, 4, col:col + 128], ident[0:NS, 0:NS])
            last.then_inc(sem("qt_mm"), 1)
            pe.wait_ge(sem("qt_ev"), 8)
            for i in range(TT):
                last = mm(PS[0:32, 0, 0:256], C("pool", 32 * i, 32 * i + 32), zt[:, i, CK:CK + 256],
                          start=(i == 0), stop=(i == TT - 1))
            last.then_inc(once("ckv_mm"), 1)
            pe.wait_ge(*done("ckv"))
            tr(PS[:, 1, 0:32], CKV[:, 0:128], ident[0:32, 0:32]).then_inc(once("kct_mm"), 1)
            pe.wait_ge(*done("kct"))
            for k in range(HKV):
                r = slice(64 * k, 64 * k + 64)
                for i in range(TT):
                    for g in range(G):
                        last = mm(PS[:, 4 * k + i, 32 * g:32 * g + 32], QT[r, g, 128 * i:128 * i + 128],
                                  kcT[r, :], start=True, stop=True)
                    last.then_inc(sem("cs_mm"), 1)
            pe.wait_ge(*done("cp"))
            for i in range(TT + 1):
                if i < TT:
                    for k in range(HKV):
                        last = tr(PS[:, 2 * (i % 2) + k, 0:128],
                                  CM[:, i, 4 * k:4 * k + 4].rearrange("p h c -> p (h c)"), ident)
                    last.then_inc(sem("ct_mm"), 1)
                if i:
                    pe.wait_ge(sem("ct_ev"), i)
                    for k in range(HKV):
                        last = mm(PS[:, 3 + i, 256 * k:256 * k + 256], PTC[:, i - 1, k], VBK[:, k],
                                  start=True, stop=True)
                    last.then_inc(sem("co_mm"), 1)
            pe.wait_ge(sem("co_ev"), 4)
            def compressed_step(u):
                if u in (24, 26, 28, 30):
                    x = u - 24
                    pe.wait_ge(sem("c_red"), x + 2)
                    if x:
                        pe.wait_ge(sem("sh_ev"), x // 2)
                    for y in range(2):
                        last = mm(PS[0:NCMP, 5, 256 * y:256 * y + 256], C("shift", 0, NCMP), S16[x + y],
                                  start=True, stop=True)
                    last.then_inc(sem("sh_mm"), 1)
                elif u in (38, 40):
                    n = (u - 38) // 2
                    pe.wait_ge(*done("cx"))
                    if n:
                        pe.wait_ge(sem("kx_ev"), 1)
                    for x in range(4):
                        last = tr(PS[:, 5, NCMP * x:NCMP * x + NCMP], CX[n][:, x, 0:128], ident[0:NCMP, 0:NCMP])
                    last.then_inc(sem("kx_mm"), 1)
                elif u == 42:
                    pe.wait_ge(sem("kx_ev"), 2)
                    for x in range(NS):
                        last = mm(PS[0:NCMP, 5, 8 * x:8 * x + 8], KCT[:, x], QB[:, x], start=True, stop=True)
                    last.then_inc(once("cxs_mm"), 1)
                elif u == 44:
                    pe.wait_ge(*done("cxs"))
                    tr(PS[0:64, 5, 0:NCMP], PCT, ident[0:NCMP, 0:NCMP]).then_inc(once("cxt_mm"), 1)
                elif u == 48:
                    pe.wait_ge(*done("cxp"))
                    tr(PS[0:NCMP, 5, 0:64], PCR, ident[0:64, 0:64]).then_inc(once("cxp_mm"), 1)
                elif u == 50:
                    pe.wait_ge(*done("pcg"))
                    for x in range(NS):
                        last = mm(PS[:, 5, 8 * x:8 * x + 8], CX[x // 4][:, x % 4, 128:256], PCT[:, 8 * x:8 * x + 8],
                                  start=True, stop=True)
                    last.then_inc(once("cxo_mm"), 1)
                    mm(PS[:, 5, 64:256], ones[0:NS], GD.rearrange("p b s h -> p (b s h)"), start=True, stop=True)\
                        .then_inc(once("gb_mm"), 1)
                    mm(PS[0:16, 5, 256:256 + NSEL], PCG, C("overlap", p=NCMP), start=True, stop=True)\
                        .then_inc(once("imp_mm"), 1)
                elif u == 58:
                    pe.wait_ge(*done("rank"))
                    tr(PS[0:NSEL, 5, 0:16], RANK, ident[0:16, 0:16]).then_inc(once("sel_mm"), 1)
                elif u == 60:
                    pe.wait_ge(*done("selt"))
                    mm(PS[:, 5, 0:16], C("expand", p=NSEL), SELT, start=True, stop=True).then_inc(once("bs_mm"), 1)
                    for b in range(2):
                        mm(PS[0:NS, 5, 64 + 64 * b:128 + 64 * b], KNEW[:, b], QB.rearrange("p s h -> p (s h)"),
                           start=True, stop=True).then_inc(sem("sn_mm"), 1)

            NU = len(UNITS)
            pe.wait_ge(*done("gd"))
            for u in range(NU + 3):
                compressed_step(u)
                if u < NU:
                    i, b, h = UNITS[u]
                    k, g = h // G, h % G
                    r, bank = slice(64 * k, 64 * k + 64), u % 3
                    if u >= 3:
                        pe.wait_ge(sem("ex"), u - 2)
                    mm(PS[:, bank, 0:128 * i + 128], QT[r, g, 128 * i:128 * i + 128],
                       (KTS, KTW)[b][r, 0:128 * i + 128], start=True, stop=True).then_inc(sem("s_mm"), 1)
                if 2 <= u < NU + 2:
                    v = u - 2
                    i = UNITS[v][0]
                    pe.wait_ge(sem("ex"), v + 1)
                    if v >= 2:
                        pe.wait_ge(sem("pt_ev"), v - 1)
                    for j in range(i + 1):
                        last = tr(PS[:, 3 + v % 2, 128 * j:128 * j + 128], P[v % 3][:, 128 * j:128 * j + 128], ident)
                    last.then_inc(sem("t_mm"), 1)
                if u >= 3:
                    v = u - 3
                    i, b, h = UNITS[v]
                    pe.wait_ge(sem("pt_ev"), v + 1)
                    if v % 16 == 0 and i:
                        pe.wait_ge(sem("on"), i)
                    col = (CS, CW)[b] + 128
                    out = slice(64 * h - 64 * (h // G), 64 * h - 64 * (h // G) + (64 if h == 3 else 128))
                    for j in range(i + 1):
                        last = mm(PS[:, 6 + b, out], PT[v % 3][:, j], zt[:, j, col:col + out.stop - out.start],
                                  start=(j == 0), stop=(j == i))
                    last.then_inc(sem("pv_mm"), 1)
            for i in range(TT):
                pe.wait_ge(sem("on"), i + 1)
                if i == 0:
                    pe.wait_ge(sem("on"), TT)
                for c in range(4):
                    last = tr(PS[:, i, 128 * c:128 * c + 128], ON[:, i, 128 * c:128 * c + 128], ident)
                last.then_inc(sem("ont_mm"), 1)
            pe.wait_ge(sem("ont"), 4)
            pe.wait_ge(sem("sn"), 2)
            kt, m0 = 0, 0
            for n, (b, s0, ns) in enumerate(ROUNDS):
                per, w = (4, 1)[b], 8 * ns
                for t0 in range(0, per * ns, 4):
                    for t in range(t0, t0 + 4):
                        x = s0 + t // per
                        if b == 0:
                            pe.wait_ge(sem(f"xs{SLOT[x]}"), 32 if x > 4 else 16)
                        else:
                            pe.wait_ge(sem(f"xw{x // 4}"), 16)
                        if kt + t >= 4:
                            pe.wait_ge(sem("ktx"), kt + t - 3)
                        for i in range(4):
                            last = tr(PS[:, t % 4, 128 * i:128 * i + 128], xtile(b, x, 4 * (t % per) + i)[0], ident)
                        last.then_inc(sem("ktx_mm"), 1)
                    for t in range(t0, t0 + 4):
                        x, m = s0 + t // per, m0 + t // per
                        if t % per == 0 and m >= 2:
                            pe.wait_ge(sem("sx"), m - 1)
                        pe.wait_ge(sem("ktx"), kt + t + 1)
                        for i in range(4):
                            at = 8 * (4 * (t % per) + i)
                            last = mm(PS[:, 4 + m % 2, at:at + 8], KTX[:, 4 * (t % 4) + i], QB[:, x],
                                      start=True, stop=True)
                        last.then_inc(sem("sx_mm"), 1)
                kt, m0 = kt + per * ns, m0 + ns
                new = SN[b][:, 8 * s0:8 * s0 + w]
                pe.wait_ge(sem("m1"), n + 1)
                if n:
                    pe.wait_ge(sem("oacc"), n + 1)
                tr(PS[0:w, 6, 0:128], M1[:, 0:w], ident)
                tr(PS[0:w, 6, 128:136], new, ident[0:NS, 0:NS]).then_inc(sem("mt_mm"), 1)
                pe.wait_ge(sem("dg"), n + 1)
                mm(PS[:, 6, 0:w], ones[0:w], DG[0:w, 0:w], start=True, stop=True).then_inc(sem("mb_mm"), 1)
                pe.wait_ge(sem("r1"), n + 1)
                mm(PS[:, 6, 64:64 + w], ones, M1[:, 0:w], start=True, stop=False)
                mm(PS[:, 6, 64:64 + w], ones[0:NS], new, start=False, stop=True).then_inc(sem("sum_mm"), 1)
                for j in range(ns):
                    x = s0 + j
                    o = PS[0:8, o_bank(j), 128 * (j % 4):128 * (j % 4) + 128]
                    for i in range(4 * per):
                        mm(o, SXB[b][:, j, i], xtile(b, x, i)[1], start=(i == 0), stop=False)
                    col = (CS, CW)[b] + 128
                    mm(o, SN[b][:, 8 * x:8 * x + 8], zt[0:NS, 4, col:col + 128], start=False, stop=True)\
                        .then_inc(sem("sv_mm"), 1)
                pe.wait_ge(sem("so"), n + 1)
                for j in range(ns):
                    last = tr(PS[:, 6, 128 + 8 * j:136 + 8 * j], SO[:, 128 * j:128 * j + 128], ident[0:8, 0:8])
                last.then_inc(sem("so_mm"), 1)

            pe.wait_ge(*done("nsa_done"))
            with pe.Fori(0, 4) as dq:
                for v in range(6):
                    bp, kind = v // 3, v % 3
                    pe.wait_ge(sem("w_lo"), dq * 6 + N_MIX + v + 1)
                    if kind < 2:
                        for j in range(2):
                            q = 2 * kind + j
                            pe.wait_ge(sem("mix_mul"), dq * 8 + 4 * bp + q + 1)
                            fm_unit(N_MIX + v, j, 2 * q, hk, ready="n3_h" if v + q == 0 else None)
                    else:
                        pe.wait_ge(sem("b_lo"), 2 * bp + 2)
                        for q in range(4):
                            pe.wait_ge(sem("sg"), dq * 8 + 4 * bp + q + 1)
                            b = 2 * bp + q // 2
                            fm_unit(N_MIX + v, q % 2, 2 * q, lambda c: (bH[b][:, c], bL[b][:, c]),
                                    k0=4 * (q // 2), k1=4 * (q // 2) + 4)
            pe.wait_ge(sem("mix_mul"), 36)
            for n in range(8):
                if n % 2 == 0:
                    pe.wait_ge(sem("w_lo"), N_OUT + n // 2 + 1)
                if n >= 3:
                    pe.wait_ge(sem("wo_ev"), n - 2)
                fm_unit(N_OUT + n // 2, n % 2, 2 * (n % 3), lambda k: (mH[:, k], mL[:, k]),
                        ready="m_lo" if n == 0 else None)
                if n >= 2:
                    norm_sum("n2", n - 2, 6)
            norm_sum("n2", 6, 6)
            norm_sum("n2", 7, 6)
            pe.wait_ge(sem("wo_ev"), 8)
            with pe.Fori(0, 2) as hf:
                with pe.Fori(0, 4) as i:
                    for u in range(2):
                        pe.wait_ge(sem("y_free"), hf * 8 + 4)
                        pe.wait_ge(sem("w_lo"), hf * 16 + i * 2 + N_MLP + u + 1)
                        for j in range(2):
                            pe.wait_ge(sem("u_free"), hf * 16 + i * 4 + 2 * u + j + 1)
                            fm_unit(N_MLP + u, j, 2 * (2 * u + j), hk, ready="n2_h" if u + j == 0 else None)
                with pe.Fori(0, 2) as e:
                    for f in range(2):
                        for kq in range(2):
                            pe.wait_ge(sem("u_free"), hf * 16 + 20)
                            pe.wait_ge(sem("w_lo"), hf * 16 + e * 4 + N_MLP + 8 + 2 * f + kq + 1)
                            pe.wait_ge(sem("u_lo"), hf * 16 + 8 * kq + 8)
                            for j in range(2):
                                if kq == 0:
                                    pe.wait_ge(sem("y_free"), hf * 8 + e * 4 + 2 * f + j + 1)
                                fm_unit(N_MLP + kq, j, 4 * f + 2 * j,
                                        lambda k: (uH[:, 8 * kq + k], uL[:, 8 * kq + k]),
                                        start=(kq == 0), stop=(kq == 1))
            pe.wait_ge(sem("y_free"), 20)
            for n in range(10):
                i, k4, w = n // 2, 4 * (n % 2), (128 if n < 8 else NS)
                if n >= 8:
                    pe.wait_ge(sem("y_ev"), n - 7)
                for j in range(4):
                    last = tr(PS[0:w, n % 8, 128 * j:128 * j + 128], xT[:, k4 + j, 128 * i:128 * i + w], ident)
                last.then_inc(sem("yt_mm"), 1)

        @block.scalar
        def _(act):
            f = nc.scalar.activation
            step = steps(act, "act_step")

            def norm_square(tag, k):
                if k >= 2:
                    act.wait_ge(sem(tag + "_mm"), k - 1)
                f(SQN[k % 2], xT[:, k], ACT.Square).then_inc(sem(tag + "_sq"), 1)

            def norm_root(tag, bank):
                act.wait_ge(sem(tag + "_mm"), KT)
                step(f(halves(RST), pair(bank), ACT.Ln, bias=eps, scale=1.0 / D))
                f(RST, RST, ACT.Exp, scale=-0.5).then_inc(sem(tag + "_rs"), 1)

            def upper(n, i=0, tiles=None, cols=CHUNK):
                act.wait_ge(sem(f"raw{n % 2}"), i * 16 + 16 * (n // 2) + 16)
                if tiles is not None:
                    act.wait_ge(sem("prod"), tiles)
                nc.scalar.copy(WH[n % 2][:, :, 0:cols], WR[n % 2][:, :, 0:cols]).then_inc(sem("w_hi"), 1)

            def h_upper(tag, chunk=None):
                for k in range(KT):
                    if chunk and k == 2:
                        upper(chunk, 0, units_before(chunk - 1))
                    act.wait_ge(sem(tag + "_raw"), k + 1)
                    nc.scalar.copy(hH[:, k], TH[k % 2]).then_inc(sem(tag + "_hi"), 1)

            act.wait_ge(*done("eps"))
            act.wait_ge(sem("xt_ev"), 10)
            for k in range(KT):
                norm_square("n1", k)
            norm_root("n1", 0)
            upper(0)
            h_upper("n1")
            upper(1)
            with act.Fori(0, 4) as i:
                for u in range(2):
                    upper(2 + u, i, i * 4 + 2 * u + 2)
            for n in (10, 11):
                upper(n, 0, units_before(n - 1), 128 if n == 10 else CHUNK)
            with act.Fori(0, 4) as i:
                for u in range(2):
                    upper(12 + u, i, i * 10 + 5 * u + 21)
            upper(20, 0, units_before(19), 24)

            act.wait_ge(sem("prod"), units_before(N_MIX))
            act.wait_ge(sem("fm_free"), 24)
            f(SIGQ, zf[:, ZQ + 2:ZQ + 4], ACT.Sigmoid).then_inc(sem("sig"), 1)
            f(SIGF, zf[:, ZK + 2:ZK + 4], ACT.Sigmoid).then_inc(sem("sig"), 1)
            f(SIGG, zf[:, ZG:ZG + 8], ACT.Sigmoid).then_inc(sem("sig"), 1)
            act.wait_ge(sem("la_ev"), 2)
            step(f(TMPA, LF[:, 0:2], ACT.Abs))
            step(f(TMPA, TMPA, ACT.Exp, scale=-1.0))
            f(TMPA, TMPA, ACT.Ln, bias=1.0).then_inc(once("lsp"), 1)
            act.wait_ge(*done("lb_d"))
            f(lbv[:, :, 1], lbv[:, :, 0], ACT.Exp).then_inc(once("lb_e"), 1)
            act.wait_ge(*done("fg"))
            f(LF[:, 2:4], LF[:, 2:4], ACT.Ln).then_inc(once("lf_h"), 1)
            act.wait_ge(*done("lf_h"))
            act.wait_ge(*done("lf_g"))
            f(decS, LF[:, :, L:T], ACT.Exp).then_inc(once("decs"), 1)
            for lev in range(LEVELS):
                act.wait_ge(sem("dist"), 2 * lev + 2)
                f(EL[lev % 2], EL[lev % 2], ACT.Exp).then_inc(sem("e_ready"), 1)
            act.wait_ge(sem("a_ready"), 2 * LEVELS)
            f(E1, B, ACT.Exp).then_inc(sem("eb"), 1)
            act.wait_ge(sem("dist"), 2 * LEVELS + 1)
            f(E0, E0, ACT.Exp).then_inc(sem("eb"), 1)
            f(decC, B.rearrange("p (k c t) -> p k c t", k=4, c=4)[:, :, :, 127], ACT.Exp).then_inc(once("decc"), 1)
            act.wait_ge(sem("o_mm"), 8)
            f(zt[:, :, CG:CG + 24], zt[:, :, CG:CG + 24], ACT.Sigmoid).then_inc(once("ng"), 1)
            f(TQ, zt[:, :, CQ:CQ + 512], ACT.Square).then_inc(sem("tq"), 1)
            f(TK[:, :, 0:128], zt[:, :, CS:CS + 128], ACT.Square).then_inc(sem("tq"), 1)
            f(TK[:, :, 128:256], zt[:, :, CW:CW + 128], ACT.Square).then_inc(sem("tq"), 1)
            nc.scalar.preload_act_table_set("natural_log_exp_and_others")
            act.wait_ge(sem("rq_sum"), 2)
            step(f(rq, rq, ACT.Ln, bias=eps, scale=1.0 / HD))
            f(rq, rq, ACT.Exp, scale=-0.5).then_inc(once("rq"), 1)
            act.wait_ge(sem("ob"), 8)
            act.wait_ge(sem("os_ev"), 2)
            for hh in range(9):
                if hh < 8:
                    if hh >= 2:
                        act.wait_ge(sem("hn_mm"), hh - 1)
                    f(SQ[hh % 2], OB[:, hh], ACT.Square).then_inc(sem("hn_sq"), 1)
                if hh:
                    j = hh - 1
                    act.wait_ge(sem("hn_mm"), j + 1)
                    if j >= 2:
                        act.wait_ge(sem("hn"), j - 1)
                    f(halves(RN[j % 2]), pair(2 * (j % 4)), ACT.Ln, bias=eps, scale=1.0 / 128)\
                        .then_inc(sem("hn_ln"), 1)
                    act.wait_ge(sem("hn_ln"), j + 1)
                    f(RN[j % 2], RN[j % 2], ACT.Exp, scale=-0.5).then_inc(sem("hn_rs"), 1)

            act.wait_ge(*done("kst"))
            step(f(kst[:, 0:2], kst[:, 0:2], ACT.Ln, bias=eps[0:32], scale=1.0 / HD))
            f(kst[:, 0:2], kst[:, 0:2], ACT.Exp, scale=-0.5).then_inc(once("kst_rs"), 1)
            act.wait_ge(*done("cm"))
            f(CM, CM, ACT.Exp).then_inc(once("cm_e"), 1)
            for u in range(len(UNITS)):
                if u == 35:
                    act.wait_ge(*done("kst_x"))
                    step(f(KST, KST, ACT.Ln, bias=eps[0:NCMP], scale=1.0 / HD))
                    f(KST, KST, ACT.Exp, scale=-0.5).then_inc(once("kst_xr"), 1)
                if u == 46:
                    act.wait_ge(*done("cxm"))
                    f(PCR, PS[0:64, 5, 0:NCMP], ACT.Exp, bias=CMAX[:, 0:1], accum_out=CMAX[:, 1:2])\
                        .then_inc(once("cxe"), 1)
                i, b, h = UNITS[u]
                act.wait_ge(sem("mx"), u + 1)
                if u >= 3:
                    act.wait_ge(sem("t_mm"), u - 2)
                f(P[u % 3][:, 0:128 * i + 128], PS[:, u % 3, 0:128 * i + 128], ACT.Exp, bias=nm[u % 3],
                  accum_out=rs[:, i, b, h:h + 1]).then_inc(sem("ex"), 1)
            for n, (b, s0, ns) in enumerate(ROUNDS):
                act.wait_ge(sem("sxm"), n + 1)
                f(SXB[b], SXB[b], ACT.Exp).then_inc(sem("sxe"), 1)
                new = SN[b][:, 8 * s0:8 * s0 + 8 * ns]
                f(new, new, ACT.Exp).then_inc(sem("sxe"), 1)

            act.wait_ge(sem("sv_mm"), 15)
            for n in (N_MIX, N_MIX + 1):
                upper(n)
            h_upper("n3")
            act.wait_ge(*done("nsa_done"))
            for b in range(4):
                nc.scalar.copy(bH[b], zf[:, 4 * b:4 * b + 4]).then_inc(sem("b_hi"), 1)
            with act.Fori(0, 4) as dq:
                for v in range(6):
                    bp, kind = v // 3, v % 3
                    first = units_before(N_MIX + v)
                    for j in range(2):
                        if j == 1:
                            n = N_MIX + v + 2
                            act.wait_ge(sem(f"raw{n % 2}"), dq * 48 + 16 * (n // 2) + 16)
                            act.wait_ge(sem("prod"), dq * 16 + units_before(n - 1))
                            nc.scalar.copy(WH[n % 2], WR[n % 2]).then_inc(sem("w_hi"), 1)
                        if kind < 2:
                            q = 2 * kind + j
                            act.wait_ge(sem("prod"), dq * 16 + first + j + 1)
                            act.wait_ge(sem("mix_mul"), dq * 8 + 4 * bp + q + 1)
                            f(halves(SG[q]), pair(2 * q), ACT.Sigmoid,
                              bias=V("bg")[:, bass.ds(dq * 2 + 16 * bp + 8 * kind + j, 1)]).then_inc(sem("sg"), 1)
            act.wait_ge(sem("prod"), units_before(N_OUT - 3))
            for k in range(KT):
                act.wait_ge(sem("mix_add"), 6 * (k // 2 + 1) + 1)
                nc.scalar.copy(mH[:, k], mixT[:, k]).then_inc(sem("m_hi"), 1)
            for k in range(KT):
                if k in (2, 4, 6):
                    upper(N_OUT + 1 + k // 2, 0, units_before(N_OUT + k // 2))
                act.wait_ge(sem("wo_ev"), k + 1)
                norm_square("n2", k)
            norm_root("n2", 6)
            h_upper("n2", N_MLP + 1)
            for hf in range(2):
                with act.Fori(0, 4) as i:
                    for u in range(2):
                        n = N_MLP + u
                        for j in range(2):
                            if j == 1:
                                upper(n + 2, i + hf * 8, i * 4 + hf * 32 + units_before(n + 1))
                            q = 2 * u + j
                            act.wait_ge(sem("prod"), i * 4 + hf * 32 + units_before(n) + j + 1)
                            act.wait_ge(sem("u_sq"), i * 4 + hf * 16 + q + 1)
                            f(halves(UR[j]), pair(2 * q), ACT.Relu).then_inc(sem("u_free"), 1)
                with act.Fori(0, 3) as dq:
                    for kq in range(2):
                        n = N_MLP + 8 + kq
                        upper(n + 2, dq + hf * 8, dq * 4 + hf * 32 + units_before(n + 1))
                if hf == 0:
                    for n in (N_MLP + 14, N_MLP + 15):
                        upper(n + 2, 0, units_before(n + 1))

        @block.vector
        def _(dve):
            v = nc.vector
            step = steps(dve, "dve_step")

            def norm_apply(tag, g):
                for k in range(KT + 1):
                    if k < KT:
                        if k >= 2:
                            dve.wait_ge(sem(tag + "_h"), k - 1)
                        v.scalar_tensor_tensor(TH[k % 2], xT[:, k], V(g, k, k + 1), RST, ALU.mult, ALU.mult)\
                            .then_inc(sem(tag + "_raw"), 1)
                    if k:
                        dve.wait_ge(sem(tag + "_hi"), k)
                        v.tensor_tensor(hL[:, k - 1], TH[(k - 1) % 2], hH[:, k - 1], ALU.subtract)\
                            .then_inc(sem(tag + "_h"), 1)

            dve.sem_inc(sem("fm_free"), 4)
            dve.sem_inc(sem("tm_free"), 5)
            dve.sem_inc(sem("mix_mul"), 4)
            dve.sem_inc(sem("mix_add"), 1)
            dve.sem_inc(sem("y_free"), 4)
            dve.sem_inc(sem("u_sq"), 2)
            dve.sem_inc(sem("u_free"), 4)
            v.memset(eps, EPS).then_inc(once("eps"), 1)
            for n in range(10):
                i, k4, w = n // 2, 4 * (n % 2), (128 if n < 8 else NS)
                dve.wait_ge(sem("xt"), n + 1)
                v.tensor_copy(xT[:, k4:k4 + 4, 128 * i:128 * i + w],
                              PS[:, n % 8, 0:4 * w].rearrange("p (k t) -> p k t", k=4)).then_inc(sem("xt_ev"), 1)
            dve.wait_ge(sem("xt_ev"), 10)
            dve.wait_ge(sem("n1_rs"), 1)
            dve.wait_ge(sem("ld_con"), 32)
            norm_apply("n1", "n1")

            with dve.Fori(0, 5) as i:
                for j in range(4):
                    dve.wait_ge(sem("prod"), i * 4 + j + 1)
                    v.tensor_copy(halves(zf[:, bass.ds(i * 4 + j, 1)].rearrange("p k t -> p (k t)")), pair(2 * j))\
                        .then_inc(sem("fm_free"), 1)
            dve.wait_ge(sem("prod"), 21)
            v.tensor_copy(halves(gaT[0:GA]), PS[0:GA, 0:2, 0:HALF]).then_inc(once("ga_ev"), 1)
            dve.wait_ge(sem("zt_zero"), 1)

            def tm_evac(n, i, c0, cols):
                m = 128 if i < TT else NS
                dve.wait_ge(sem("prod"), n + 22)
                v.tensor_copy(zt[0:m, i, c0], PS[0:m, i, 0:cols]).then_inc(sem("tm_free"), 1)

            for i in range(5):
                tm_evac(i, i, slice(0, CHUNK), CHUNK)
            with dve.Fori(0, 4) as c:
                for u in range(2):
                    for i in range(5):
                        tm_evac(c * 10 + 5 * u + 5 + i, i, bass.ds(c * 512 + 256 * u + 256, CHUNK), CHUNK)
            for i in range(5):
                tm_evac(45 + i, i, slice(9 * CHUNK, TM), 24)

            dve.wait_ge(sem("ld_idx"), 16)
            dve.wait_ge(sem("ld_con"), 32)
            v.tensor_scalar(idx[:, NS:], idx[:, 0:NS], 8.0, V("r8"), ALU.mult, ALU.add).then_inc(once("idx"), 1)
            dve.wait_ge(sem("fm_free"), 24)
            dve.wait_ge(sem("ld_tab"), 16)
            step(v.tensor_scalar(zf[:, ZQ:ZQ + 2], zf[:, ZQ:ZQ + 2], 0.125, None, ALU.mult))
            dve.wait_ge(sem("sig"), 1)
            v.scalar_tensor_tensor(zf[:, ZQ + 2:ZQ + 4], zf[:, ZQ + 2:ZQ + 4], 0.125, SIGQ, ALU.mult, ALU.mult)\
                .then_inc(once("q_act"), 1)
            dve.wait_ge(*done("la_mm"))
            for k in range(2):
                v.tensor_scalar(halves(LF[:, k]), pair(2 * k), V("ba", k, k + 1), None, ALU.add)\
                    .then_inc(sem("la_ev"), 1)
            v.tensor_tensor(lbv[:, :, 0], V("lb"), V("lb"), ALU.subtract).then_inc(once("lb_d"), 1)
            dve.wait_ge(*done("lb_e"))
            step(v.reciprocal(lbv[:, :, 2], lbv[:, :, 1]))
            step(v.tensor_tensor(lbv[:, :, 3], lbv[:, :, 1], lbv[:, :, 2], ALU.mult))
            step(v.tensor_tensor(lbv[:, :, 4], lbv[:, :, 3], lbv[:, :, 3], ALU.subtract))
            step(v.tensor_scalar(lbv[:, :, 5], lbv[:, :, 4], -1.0, 1.0, ALU.mult, ALU.add))
            dve.wait_ge(sem("sig"), 2)
            for k in range(2):
                step(v.tensor_scalar(LF[:, 2 + k], SIGF[:, k], lbv[:, k, 5:6], lbv[:, k, 4:5], ALU.mult, ALU.add))
            step(v.tensor_scalar(zf[:, ZK + 2:ZK + 4], LF[:, 2:4], -1.0, 1.0, ALU.mult, ALU.add))
            v.tensor_scalar(LF[:, 2:4], LF[:, 2:4], 2.0 ** -63, None, ALU.max).then_inc(once("fg"), 1)
            dve.wait_ge(sem("la_ev"), 2)
            dve.wait_ge(*done("lsp"))
            step(v.scalar_tensor_tensor(flat(LF[:, 0:2]), flat(LF[:, 0:2]), 0.0, flat(TMPA), ALU.min, ALU.subtract))
            v.tensor_scalar(LF[:, 0:2], LF[:, 0:2], 1.0 / 16, None, ALU.mult).then_inc(once("lf_g"), 1)
            dve.wait_ge(*done("lf_g"))
            dve.wait_ge(*done("lf_h"))
            for k in range(4):
                v.tensor_tensor_scan(chunks(B)[:, k], C("reset"), LF[:, k, 0:L], 0.0, ALU.mult, ALU.add)\
                    .then_inc(sem("cum"), 1)
            dve.wait_ge(sem("sig"), 3)
            v.tensor_tensor(flat(zf[:, ZG:ZG + 8]), flat(zf[:, ZG:ZG + 8]), flat(SIGG), ALU.mult)\
                .then_inc(once("qk"), 1)

            def score_copy(st):
                for g in range(8):
                    dve.wait_ge(sem("sc_mm"), 8 * st + g + 1)
                    mk = LEVELS if st == 0 else st - 1
                    mask = C("masks", 128 * mk, 128 * mk + 128)
                    ps = PS[:, g].rearrange("p (k t) -> p k t", k=4)
                    if st == 0:
                        v.tensor_tensor(SC[:, g], ps, mask.unsqueeze(1).to_broadcast([128, 4, 128]), ALU.mult)\
                            .then_inc(sem("sc_cp"), 1)
                    else:
                        v.copy_predicated(SC[:, g], mask.bitcast(i32).unsqueeze(1).to_broadcast([128, 4, 128]), ps)\
                            .then_inc(sem("sc_cp"), 1)

            dve.wait_ge(*done("qk"))
            for lev in range(LEVELS):
                half = 1 << lev
                dve.wait_ge(sem("e_ready"), lev + 1)
                if lev >= 2:
                    dve.wait_ge(sem("sc_mm"), 8 * lev)
                if lev == 0:
                    dve.wait_ge(*done("lsp"))
                for side, z0 in ((0, ZK), (1, ZQ)):
                    blk = lambda ap: ap.rearrange("p k (n q h) -> p k n q h", q=2, h=half)[:, :, :, side]
                    a, e = blk(chunks(AL[lev % 2])), blk(chunks(EL[lev % 2]))
                    x = zf[:, z0:z0 + 4, 0:L].rearrange("p k (n q h) -> p k n q h", q=2, h=half)[:, :, :, side]
                    v.tensor_tensor(a, x, e, ALU.mult).then_inc(sem("a_ready"), 1)
                score_copy(lev)
                dve.wait_ge(sem("sc_cp"), 8 * lev + 8)
            score_copy(LEVELS)

            dve.wait_ge(sem("eb"), 2)
            dve.wait_ge(sem("sc_mm"), 8 * LEVELS + 8)
            v.tensor_tensor(chunks(A0), zf[:, ZK:ZK + 4, 0:L], chunks(E0), ALU.mult).then_inc(once("kdec"), 1)
            dve.wait_ge(*done("decs"))
            dve.wait_ge(sem("cum"), 4)
            for c in range(4):
                dve.wait_ge(sem("kt_mm"), c + 1)
                v.tensor_copy(KD[:, c].rearrange("p k f -> p (k f)"), PS[:, c]).then_inc(sem("kd_ev"), 1)
            v.tensor_tensor(chunks(A0), zf[:, ZQ:ZQ + 4, 0:L], chunks(E1), ALU.mult).then_inc(once("qdec"), 1)
            dve.wait_ge(*done("decc"))
            for c in range(4):
                dve.wait_ge(sem("ds_mm"), c + 1)
                ds = PS[:, 4 + c].rearrange("p (k v) -> p k v", k=4)
                if c == 0:
                    v.tensor_copy(ST[:, 0], ds).then_inc(sem("st"), 1)
                else:
                    dve.wait_ge(sem("st"), c)
                    step(v.tensor_tensor(ST[:, c], ST[:, c - 1], bc(decC[:, :, c], 128), ALU.mult))
                    v.tensor_tensor(ST[:, c], ST[:, c], ds, ALU.add).then_inc(sem("st"), 1)
            dve.wait_ge(sem("o_mm"), 8)
            for hh in range(8):
                v.tensor_copy(OB[:, hh, 0:L], PS[:, hh]).then_inc(sem("ob"), 1)
            dve.wait_ge(sem("ld_ss"), 64)
            for m in range(2):
                d = decS[:, 2 * m:2 * m + 2].rearrange("p k s -> p s k")
                step(v.tensor_tensor(SS[:, m], SS[:, m], bc(d, 128), ALU.mult))
            for g in range(8):
                m, s0 = g // 4, 2 * (g % 4)
                dve.wait_ge(sem("vb_mm"), g + 1)
                k = zf[:, ZK + 2 * m:ZK + 2 * m + 2, L + s0:L + s0 + 2].rearrange("p k s -> p s k")
                step(v.tensor_tensor(VB[g % 2], PS[:, g].rearrange("p (s k v) -> p s k v", s=2, k=2), bc(k, 128), ALU.mult))
                v.tensor_tensor(SS[:, m, s0:s0 + 2], SS[:, m, s0:s0 + 2], VB[g % 2], ALU.add)\
                    .then_inc(sem("ss_done"), 1)
            step(v.memset(QM, 0.0))
            for k in range(4):
                for par in range(2):
                    r = slice(64 * par, 64 * par + 64)
                    ins = v.tensor_copy(QM[r, 128 * k + 8 * par:128 * k + 128:17], zf[r, ZQ + k, L:T])
            ins.then_inc(once("qm"), 1)
            dve.wait_ge(*done("hist_mm"))
            dve.wait_ge(sem("o_mm"), 8)
            hs = stat[:, 60:92].rearrange("p (g s) -> p g s", g=4)
            for g, w in enumerate(WINDOWS):
                step(v.tensor_reduce(hs[:, g], PS[:, 2, 120 * g:120 * g + 120].rearrange("p (s j) -> p s j", s=NS)
                                     [:, :, HIST + 1 - w:HIST], AX, ALU.add))
            step(v.tensor_tensor(hs, hs, zf[:, ZU:ZU + 4, L:T], ALU.add))
            dve.wait_ge(*done("tail_mm"))
            v.tensor_copy(tail, PS[0:23, 3].rearrange("p (g c) -> p g c", g=4)).then_inc(once("tail"), 1)
            dve.wait_ge(sem("win"), 1)
            for g, w in enumerate(WINDOWS):
                win = WIN[g][:, HIST:HIST + L]
                v.scalar_tensor_tensor(PD[:, g, 0:L], win, 1.0 / w, zf[:, ZU + g, 0:L], ALU.mult, ALU.subtract)\
                    .then_inc(sem("pd"), 1)
                v.scalar_tensor_tensor(PD[:, g, L:T], hs[:, g], 1.0 / w, zf[:, ZU + g, L:T], ALU.mult, ALU.subtract)\
                    .then_inc(sem("pd"), 1)
            dve.wait_ge(*done("os_mm"))
            v.tensor_copy(OSS, PS[0:16, 0]).then_inc(once("oss"), 1)
            dve.wait_ge(sem("pd"), 8)
            step(v.tensor_scalar(gq8, V("qg"), 0.125, None, ALU.mult))
            dve.wait_ge(sem("tq"), 3)
            v.tensor_reduce(rq[:, :, 0:8], TQ.rearrange("p i (h d) -> p i h d", d=HD), AX, ALU.add)\
                .then_inc(sem("rq_sum"), 1)
            v.tensor_reduce(rq[:, :, 8:12], TK.rearrange("p i (h d) -> p i h d", d=HD), AX, ALU.add)\
                .then_inc(sem("rq_sum"), 1)
            dve.wait_ge(*done("ost_mm"))
            for par in range(2):
                v.tensor_copy(OB[:, par:8:2, L:T], PS[:, 1, 0:64].rearrange("p (k q s) -> p k q s", k=4, q=2)[:, :, par])\
                    .then_inc(sem("os_ev"), 1)
            for g in range(4):
                dve.wait_ge(sem("pool_mm"), g + 1)
                v.tensor_scalar(halves(zf[:, ZU + g]), pair(2 + 2 * (g % 2)), V("psc", g, g + 1), None, ALU.mult)\
                    .then_inc(sem("pool_ev"), 1)

            dve.wait_ge(*done("rq"))
            for n, col in enumerate((CS, CW)):
                kk = zt[:, :, col:col + 128].rearrange("p i (h d) -> p i h d", d=HD)
                step(v.tensor_tensor(kk, kk, bc(rq[:, :, 8 + 2 * n:10 + 2 * n], HD), ALU.mult))
                gain = V("kg", 64 * (n + 1), 64 * (n + 2)).unsqueeze(1).unsqueeze(1).to_broadcast([128, 5, 2, HD])
                ins = v.tensor_tensor(kk, kk, gain, ALU.mult)
                if n == 0:
                    step(ins)
                else:
                    ins.then_inc(once("k_norm"), 1)
            for i in range(5):
                for k in range(HKV):
                    q = zt[:, i, CQ + 256 * k:CQ + 256 * k + 256].rearrange("p (g d) -> p g d", g=G)
                    step(v.tensor_tensor(QN[:, i, :, k], q, bc(rq[:, i, 4 * k:4 * k + 4], HD), ALU.mult))
            qv = R[:, 16512:19072].rearrange("p (n d) -> p n d", d=HD)
            v.tensor_tensor(qv, qv, gq8.unsqueeze(1).to_broadcast([128, 40, HD]), ALU.mult)\
                .then_inc(once("q_norm"), 1)
            dve.wait_ge(sem("os_ev"), 2)
            for hh in range(8):
                dve.wait_ge(sem("hn_rs"), hh + 1)
                gain = V("gn") if hh < 4 else V("hn")
                step(v.scalar_tensor_tensor(OB[:, hh], OB[:, hh], gain, RN[hh % 2], ALU.mult, ALU.mult))
                v.tensor_tensor(zf[:, ZG + hh], zf[:, ZG + hh], OB[:, hh], ALU.mult).then_inc(sem("hn"), 1)

            dve.wait_ge(sem("st_out"), 128)
            dve.wait_ge(sem("hn"), 8)
            for i in range(5):
                w = 128 if i < TT else NS
                dve.wait_ge(sem("qt_mm"), i + 1)
                v.tensor_copy(QT[:, :, 128 * i:128 * i + w], PS[:, i, 0:4 * w].rearrange("p (g t) -> p g t", g=G))\
                    .then_inc(sem("qt_ev"), 1)
            dve.wait_ge(sem("qt_mm"), 8)
            v.tensor_copy(KTS[:, 0:L], PS[:, 5]).then_inc(sem("qt_ev"), 1)
            v.tensor_copy(KTW[:, 0:L], PS[:, 6]).then_inc(sem("qt_ev"), 1)
            new = R[:, 7200:8240].rearrange("p (b t) -> p b t", b=2)[:, :, L:T]
            v.tensor_copy(new, PS[:, 7, 0:16].rearrange("p (b s) -> p b s", b=2)).then_inc(sem("qt_ev"), 1)
            dve.wait_ge(*done("ckv_mm"))
            step(v.tensor_copy(CKV, PS[0:32, 0, 0:256]))
            sq = gaT[0:32, 256:384]
            step(v.tensor_tensor(sq, CKV[:, 0:128], CKV[:, 0:128], ALU.mult))
            v.tensor_reduce(kst[:, 0:2], sq.rearrange("p (k d) -> p k d", d=HD), AX, ALU.add).then_inc(once("kst"), 1)
            dve.wait_ge(sem("hn"), 8)
            step(v.memset(VBK, 0.0))
            for j in range(4):
                step(v.tensor_copy(VBK[32 * j:32 * j + 32, :, 64 * j:64 * j + 64],
                                   CKV[:, 128:256].rearrange("p (k d) -> p k d", d=HD)))
            dve.wait_ge(*done("kst_rs"))
            ck = CKV[:, 0:128].rearrange("p (k d) -> p k d", d=HD)
            step(v.tensor_tensor(ck, ck, bc(kst[:, 0:2], HD), ALU.mult))
            v.tensor_tensor(ck, ck, V("kg", 0, 64, 32).unsqueeze(1).to_broadcast([32, 2, HD]), ALU.mult)\
                .then_inc(once("ckv"), 1)
            dve.wait_ge(*done("kct_mm"))
            v.tensor_copy(kcT, PS[:, 1, 0:32]).then_inc(once("kct"), 1)
            for k in range(HKV):
                for i in range(TT):
                    dve.wait_ge(sem("cs_mm"), 4 * k + i + 1)
                    neg = C("cmpneg", 32 * i, 32 * i + 32).unsqueeze(1).to_broadcast([128, 4, 32])
                    v.tensor_tensor(CM[:, i, 4 * k:4 * k + 4], PS[:, 4 * k + i, 0:128].rearrange("p (h c) -> p h c", h=4),
                                    neg, ALU.add).then_inc(sem("cs_ev"), 1)
            dve.wait_ge(sem("cs_ev"), 8)
            cm = CM.rearrange("p i h c -> p (i h) c")
            step(v.tensor_reduce(nmc, cm, AX, ALU.max, negate=True))
            v.tensor_tensor(cm, cm, bc(nmc, 32), ALU.add).then_inc(once("cm"), 1)
            dve.wait_ge(*done("cm_e"))
            step(v.tensor_reduce(rsc.rearrange("p i h -> p (i h)"), cm, AX, ALU.add))
            v.tensor_tensor(CM, CM, C("cmp01").rearrange("p (i c) -> p i c", i=4).unsqueeze(2)
                            .to_broadcast([128, 4, 8, 32]), ALU.mult).then_inc(once("cp"), 1)
            step(v.reciprocal(rsc, rsc))
            dve.wait_ge(*done("ng"))
            gate = zt[:, :, CG:CG + 24].rearrange("p i (h b) -> p i h b", b=3)
            step(v.tensor_tensor(rsc, rsc, gate[:, 0:4, :, 0], ALU.mult))
            for i in range(TT + 1):
                if i < TT:
                    dve.wait_ge(sem("ct_mm"), i + 1)
                    v.tensor_copy(PTC[:, i], PS[:, 2 * (i % 2):2 * (i % 2) + 2, 0:128]).then_inc(sem("ct_ev"), 1)
                if i:
                    dve.wait_ge(sem("co_mm"), i)
                    v.tensor_tensor(ON[:, i - 1].rearrange("p (h d) -> p h d", d=HD),
                                    PS[:, 3 + i].rearrange("p (h d) -> p h d", d=HD), bc(rsc[:, i - 1], HD), ALU.mult)\
                        .then_inc(sem("co_ev"), 1)
            dve.wait_ge(sem("rows_out"), 96)
            dve.wait_ge(sem("stored"), 48)
            step(v.memset(QB, 0.0))
            for k in range(HKV):
                r = slice(64 * k, 64 * k + 64)
                step(v.tensor_copy(QB[r, :, 4 * k:4 * k + 4], QT[r, :, L:T].rearrange("p g s -> p s g")))
            step(v.tensor_copy(KNEW, new))
            g8 = zt[0:NS, 4, CG:CG + 24].rearrange("p (h b) -> p b h", b=3)
            one = C("onehot", p=NS).rearrange("p (s c) -> p s c", s=NS)[:, :, 0:8]
            for b in range(3):
                ins = v.tensor_tensor(GD[:, b], g8[:, b].unsqueeze(1).to_broadcast([NS, NS, 8]), one, ALU.mult)
                if b < 2:
                    step(ins)
                else:
                    ins.then_inc(once("gd"), 1)

            sq3 = [16, NSEL, NSEL]
            by_m = lambda a: a.unsqueeze(1).to_broadcast(sq3)
            num = C("number", p=16)

            def compressed_step(u):
                if u in (25, 27, 29, 31):
                    x = u - 25
                    dve.wait_ge(sem("sh_mm"), x // 2 + 1)
                    v.tensor_copy(CX[x // 4][:, x % 4:x % 4 + 2].rearrange("p s c -> p (s c)"), PS[0:NCMP, 5])\
                        .then_inc(sem("sh_ev"), 1)
                elif u in (32, 33):
                    if u == 32:
                        dve.wait_ge(sem("sh_ev"), 4)
                    sq = SQX[:, 512 * (u - 32):512 * (u - 32) + 512].rearrange("p (s c) -> p s c", s=4)
                    step(v.tensor_tensor(sq, CX[u - 32][:, :, 0:128], CX[u - 32][:, :, 0:128], ALU.mult))
                elif u == 34:
                    v.tensor_reduce(KST, SQX.rearrange("p (s k d) -> p s k d", s=NS, k=2), AX, ALU.add)\
                        .then_inc(once("kst_x"), 1)
                elif u in (36, 37):
                    n = u - 36
                    dve.wait_ge(*done("kst_xr"))
                    ck = CX[n][:, :, 0:128].rearrange("p s (k d) -> p s k d", d=HD)
                    step(v.tensor_tensor(ck, ck, bc(KST[:, 4 * n:4 * n + 4], HD), ALU.mult))
                    gain = V("kg", 0, 64, NCMP).unsqueeze(1).unsqueeze(1).to_broadcast([NCMP, 4, 2, HD])
                    ins = v.tensor_tensor(ck, ck, gain, ALU.mult)
                    if n == 0:
                        step(ins)
                    else:
                        ins.then_inc(once("cx"), 1)
                elif u in (39, 41):
                    n = (u - 39) // 2
                    dve.wait_ge(sem("kx_mm"), n + 1)
                    v.tensor_copy(KCT[:, 4 * n:4 * n + 4].rearrange("p s c -> p (s c)"), PS[:, 5, 0:4 * NCMP])\
                        .then_inc(sem("kx_ev"), 1)
                elif u == 43:
                    dve.wait_ge(*done("cxs_mm"))
                    v.tensor_copy(PCT, PS[0:NCMP, 5, 0:64]).then_inc(once("cxs"), 1)
                elif u == 45:
                    dve.wait_ge(*done("cxt_mm"))
                    v.tensor_reduce(CMAX[:, 0:1], PS[0:64, 5, 0:NCMP], AX, ALU.max, negate=True)\
                        .then_inc(once("cxm"), 1)
                elif u == 47:
                    dve.wait_ge(*done("cxe"))
                    step(v.reciprocal(CMAX[:, 2:3], CMAX[:, 1:2]))
                    v.tensor_scalar(PCR, PCR, CMAX[:, 2:3], None, ALU.mult).then_inc(once("cxp"), 1)
                elif u == 49:
                    dve.wait_ge(*done("cxp_mm"))
                    step(v.tensor_copy(PCT, PS[0:NCMP, 5, 0:64]))
                    v.tensor_reduce(PCG, PCT.rearrange("p (n g) -> p n g", g=G), AX, ALU.add).then_inc(once("pcg"), 1)
                elif u == 51:
                    dve.wait_ge(*done("gb_mm"))
                    step(v.tensor_copy(GB.rearrange("p b n -> p (b n)"), PS[:, 5, 64:256]))
                    v.tensor_tensor(OACC, PS[:, 5, 0:64], GB[:, 0], ALU.mult).then_inc(sem("oacc"), 1)
                    dve.wait_ge(*done("imp_mm"))
                    step(v.tensor_tensor(SCO, PS[0:16, 5, 256:256 + NSEL], C("bonus", p=16), ALU.add))
                elif u == 52:
                    step(v.tensor_tensor(T1, by_m(SCO), bc(SCO, NSEL), ALU.is_gt))
                elif u == 53:
                    step(v.tensor_tensor(T2, by_m(SCO), bc(SCO, NSEL), ALU.is_equal))
                elif u == 54:
                    step(v.tensor_tensor(T3, by_m(num), bc(num, NSEL), ALU.is_lt))
                elif u == 55:
                    step(v.tensor_tensor(T2, T2, T3, ALU.mult))
                elif u == 56:
                    step(v.tensor_tensor(T1, T1, T2, ALU.add))
                elif u == 57:
                    step(v.tensor_reduce(RANK, T1, AX, ALU.add))
                    v.tensor_scalar(RANK, RANK, float(TOPK), None, ALU.is_lt).then_inc(once("rank"), 1)
                elif u == 59:
                    dve.wait_ge(*done("sel_mm"))
                    v.tensor_copy(SELT, PS[0:NSEL, 5, 0:16]).then_inc(once("selt"), 1)
                elif u == 61:
                    dve.wait_ge(*done("bs_mm"))
                    v.tensor_scalar(BS.rearrange("p s k -> p (s k)"), PS[:, 5, 0:16], -1.0, -NEG, ALU.add, ALU.mult)\
                        .then_inc(once("bs"), 1)
                    for b in range(2):
                        dve.wait_ge(sem("sn_mm"), b + 1)
                        v.tensor_tensor(SN[b], PS[0:NS, 5, 64 + 64 * b:128 + 64 * b], C("newmask", p=NS), ALU.add)\
                            .then_inc(sem("sn"), 1)

            NU = len(UNITS)
            for u in range(NU + 2):
                compressed_step(u)
                if u < NU:
                    i = UNITS[u][0]
                    dve.wait_ge(sem("s_mm"), u + 1)
                    if u >= 3:
                        dve.wait_ge(sem("ex"), u - 2)
                    diagonal = PS[:, u % 3, 128 * i:128 * i + 128]
                    step(v.tensor_tensor(diagonal, diagonal, C("causal"), ALU.add))
                    v.tensor_reduce(nm[u % 3], PS[:, u % 3, 0:128 * i + 128], AX, ALU.max, negate=True)\
                        .then_inc(sem("mx"), 1)
                if u >= 2:
                    w = u - 2
                    i = UNITS[w][0]
                    dve.wait_ge(sem("t_mm"), w + 1)
                    if w >= 3:
                        dve.wait_ge(sem("pv_mm"), w - 2)
                    v.tensor_copy(PT[w % 3][:, 0:i + 1].rearrange("p k t -> p (k t)"),
                                  PS[:, 3 + w % 2, 0:128 * i + 128]).then_inc(sem("pt_ev"), 1)
                if u % 16 == 1 and u > 1:
                    i = u // 16 - 1
                    step(v.reciprocal(rs[:, i], rs[:, i]))
                    step(v.tensor_tensor(rs[:, i].rearrange("p b h -> p h b"),
                                         rs[:, i].rearrange("p b h -> p h b"), gate[:, i, :, 1:3], ALU.mult))
                    dve.wait_ge(sem("pv_mm"), 16 * i + 16)
                    dve.wait_ge(sem("co_ev"), 4)
                    on = ON[:, i].rearrange("p (h d) -> p h d", d=HD)
                    for b in range(2):
                        t = TQ[:, b].rearrange("p (h d) -> p h d", d=HD)
                        step(v.tensor_tensor(t, PS[:, 6 + b].rearrange("p (h d) -> p h d", d=HD),
                                             bc(rs[:, i, b], HD), ALU.mult))
                        ins = v.tensor_tensor(on, on, t, ALU.add)
                        if b == 0:
                            step(ins)
                        else:
                            ins.then_inc(sem("on"), 1)
            for i in range(TT):
                dve.wait_ge(sem("ont_mm"), i + 1)
                v.tensor_copy(ONT[:, :, 128 * i:128 * i + 128], PS[:, i].rearrange("p (c t) -> p c t", c=4))\
                    .then_inc(sem("ont"), 1)
            dve.wait_ge(sem("sn"), 2)
            dve.wait_ge(*done("bs"))
            kt, m0 = 0, 0
            for n, (b, s0, ns) in enumerate(ROUNDS):
                per, w, SXn = (4, 1)[b], 8 * ns, SXB[b]
                ni = 4 * per
                if n:
                    dve.wait_ge(sem("sv_mm"), m0)
                for t0 in range(0, per * ns, 4):
                    for t in range(t0, t0 + 4):
                        dve.wait_ge(sem("ktx_mm"), kt + t + 1)
                        if kt + t >= 4:
                            dve.wait_ge(sem("sx_mm"), kt + t - 3)
                        v.tensor_copy(KTX[:, 4 * (t % 4):4 * (t % 4) + 4].rearrange("p i t -> p (i t)"), PS[:, t % 4])\
                            .then_inc(sem("ktx"), 1)
                    for t in range(t0 + per - 1, t0 + 4, per):
                        j = t // per
                        x, m = s0 + j, m0 + j
                        dve.wait_ge(sem("sx_mm"), kt + t + 1)
                        ps = PS[:, 4 + m % 2, 0:8 * ni]
                        if b == 0:
                            bias = BS[:, x].unsqueeze(1).unsqueeze(3).to_broadcast([128, 16, 2, 4])
                            v.tensor_tensor(SX[:, j].rearrange("p i (k g) -> p i k g", k=2),
                                            ps.rearrange("p (i k g) -> p i k g", k=2, g=4), bias, ALU.add)\
                                .then_inc(sem("sx"), 1)
                        else:
                            v.tensor_copy(SXn[:, j].rearrange("p i h -> p (i h)"), ps).then_inc(sem("sx"), 1)
                kt, m0 = kt + per * ns, m0 + ns
                dve.wait_ge(sem("sx"), m0)
                m1 = M1[:, 0:w].rearrange("p (s h) -> p s h", s=ns)
                v.tensor_reduce(m1, SXn.rearrange("p s i h -> p s h i"), AX, ALU.max).then_inc(sem("m1"), 1)
                dve.wait_ge(sem("mt_mm"), n + 1)
                step(v.tensor_reduce(SM[0:w], PS[0:w, 6, 0:136], AX, ALU.max))
                v.tensor_scalar(DG[0:w, 0:w], ident[0:w, 0:w], SM[0:w], None, ALU.mult).then_inc(sem("dg"), 1)
                dve.wait_ge(sem("mb_mm"), n + 1)
                mb = PS[:, 6, 0:w]
                v.tensor_tensor(SXn, SXn, mb.rearrange("p (s h) -> p s h", s=ns).unsqueeze(2)
                                .to_broadcast([128, ns, ni, 8]), ALU.subtract).then_inc(sem("sxs"), 1)
                mine = slice(8 * s0, 8 * s0 + w)
                v.tensor_tensor(SN[b][:, mine], SN[b][:, mine], mb[0:NS], ALU.subtract).then_inc(sem("sxm"), 1)
                dve.wait_ge(sem("sxe"), 2 * n + 2)
                v.tensor_reduce(m1, SXn.rearrange("p s i h -> p s h i"), AX, ALU.add).then_inc(sem("r1"), 1)
                dve.wait_ge(sem("sum_mm"), n + 1)
                step(v.reciprocal(COEF[:, 0:w], PS[:, 6, 64:64 + w]))
                step(v.tensor_tensor(COEF[:, 0:w], COEF[:, 0:w], GB[:, 1 + b, mine], ALU.mult))
                dve.wait_ge(sem("sv_mm"), m0)
                for j in range(ns // 4):
                    ins = v.tensor_copy(SO[:, 512 * j:512 * j + 512], PS[0:8, o_bank(4 * j)])
                ins.then_inc(sem("so"), 1)
                dve.wait_ge(sem("so_mm"), n + 1)
                step(v.tensor_tensor(OT[:, 0:w], PS[:, 6, 128:128 + w], COEF[:, 0:w], ALU.mult))
                v.tensor_tensor(OACC[:, mine], OACC[:, mine], OT[:, 0:w], ALU.add).then_inc(sem("oacc"), 1)
            dve.wait_ge(sem("oacc"), 4)
            oa = OACC.rearrange("p (s k j q) -> p k q j s", k=2, j=2, q=2)
            for k in range(2):
                for q in range(2):
                    ins = v.tensor_copy(ONT[64 * q:64 * q + 64, 2 * k:2 * k + 2, L:T], oa[64 * k:64 * k + 64, k, q])
                    if k + q < 2:
                        step(ins)
                    else:
                        ins.then_inc(once("nsa_done"), 1)


            norm_apply("n3", "n1")
            for b in range(4):
                dve.wait_ge(sem("b_hi"), b + 1)
                v.tensor_tensor(bL[b], zf[:, 4 * b:4 * b + 4], bH[b], ALU.subtract).then_inc(sem("b_lo"), 1)
            with dve.Fori(0, 4) as dq:
                adds = 0
                for bp in range(2):
                    for q in range(4):
                        dve.wait_ge(sem("sg"), dq * 8 + 4 * bp + q + 1)
                        dve.wait_ge(sem("prod"), dq * 16 + units_before(N_MIX + 3 * bp + 2) + q + 1)
                        m = mixT[:, bass.ds(dq * 2 + q % 2, 1)].rearrange("p k t -> p (k t)")
                        if bp == 0 and q < 2:
                            v.tensor_tensor(halves(m), pair(2 * q), halves(SG[q]), ALU.mult)\
                                .then_inc(sem("mix_mul"), 1)
                            continue
                        dve.wait_ge(sem("mix_add"), dq * 6 + adds + 1)
                        v.tensor_tensor(halves(GP), pair(2 * q), halves(SG[q]), ALU.mult).then_inc(sem("mix_mul"), 1)
                        dve.wait_ge(sem("mix_mul"), dq * 8 + 4 * bp + q + 5)
                        v.tensor_tensor(m, m, GP, ALU.add).then_inc(sem("mix_add"), 1)
                        adds += 1
            for k in range(KT):
                dve.wait_ge(sem("m_hi"), k + 1)
                v.tensor_tensor(mL[:, k], mixT[:, k], mH[:, k], ALU.subtract).then_inc(sem("m_lo"), 1)
            for n in range(8):
                dve.wait_ge(sem("prod"), units_before(N_OUT) + n + 1)
                v.tensor_tensor(halves(xT[:, n]), halves(xT[:, n]), pair(2 * (n % 3)), ALU.add)\
                    .then_inc(sem("wo_ev"), 1)
            dve.wait_ge(sem("wo_ev"), 8)
            dve.wait_ge(sem("n2_rs"), 1)
            norm_apply("n2", "n2")
            with dve.Fori(0, 2) as hf:
                with dve.Fori(0, 4) as i:
                    for q in range(4):
                        n = hf * 16 + i * 4 + q
                        tile = lambda part: part[:, bass.ds(i * 4 + q, 1)].rearrange("p k t -> p (k t)")
                        dve.wait_ge(sem("u_free"), n + 5)
                        v.tensor_tensor(US[q % 2], UR[q % 2], UR[q % 2], ALU.mult).then_inc(sem("u_sq"), 1)
                        dve.wait_ge(sem("u_sq"), n + 3)
                        v.tensor_copy(tile(uH), US[q % 2]).then_inc(sem("u_hi"), 1)
                        dve.wait_ge(sem("u_hi"), n + 1)
                        v.tensor_tensor(tile(uL), US[q % 2], tile(uH), ALU.subtract).then_inc(sem("u_lo"), 1)
                        dve.wait_ge(sem("u_lo"), n + 1)
                with dve.Fori(0, 2) as e:
                    for f in range(2):
                        for j in range(2):
                            dve.wait_ge(sem("prod"), hf * 32 + e * 8 + units_before(N_MLP + 8) + 4 * f + j + 3)
                            x = halves(xT[:, bass.ds(e * 4 + 2 * f + j, 1)].rearrange("p k t -> p (k t)"))
                            v.tensor_tensor(x, x, pair(4 * f + 2 * j), ALU.add).then_inc(sem("y_free"), 1)
            for n in range(10):
                w = 128 if n < 8 else NS
                dve.wait_ge(sem("yt_mm"), n + 1)
                v.tensor_copy(YT[0:w, n // 2, 512 * (n % 2):512 * (n % 2) + 512], PS[0:w, n % 8])\
                    .then_inc(sem("y_ev"), 1)

        @block.gpsimd
        def _(gp):
            p = nc.gpsimd
            step = steps(gp, "pool_step")
            p.memset(zt[:, 4, :], 0.0).then_inc(sem("zt_zero"), 1)

            def lower(n, i=0, cols=CHUNK):
                gp.wait_ge(sem("w_hi"), i + n + 1)
                c = slice(0, cols)
                p.tensor_tensor(WL[n % 2][:, :, c], WR[n % 2][:, :, c], WH[n % 2][:, :, c], ALU.subtract)\
                    .then_inc(sem("w_lo"), 1)

            with gp.Fori(0, 5) as i:
                for u in range(2):
                    lower(u, i * 2)
            lower(10, cols=128)
            lower(11)
            with gp.Fori(0, 4) as i:
                for u in range(2):
                    lower(12 + u, i * 2)
            lower(20, cols=24)
            gp.wait_ge(sem("cum"), 4)
            gp.wait_ge(*done("q_act"))
            gp.wait_ge(*done("fg"))
            for lev in range(LEVELS):
                half = 1 << lev
                if lev >= 2:
                    gp.wait_ge(sem("a_ready"), 2 * lev - 2)
                blk = lambda ap: ap.rearrange("p (n q h) -> p n q h", q=2, h=half)
                b, e = blk(B), blk(EL[lev % 2])
                mid = b[:, :, 0, half - 1:half].to_broadcast([128, 2048 // (2 * half), half])
                p.tensor_tensor(e[:, :, 0], mid, b[:, :, 0], ALU.subtract).then_inc(sem("dist"), 1)
                p.tensor_tensor(e[:, :, 1], b[:, :, 1], mid, ALU.subtract).then_inc(sem("dist"), 1)
            gp.wait_ge(sem("a_ready"), 2 * LEVELS)
            b = B.rearrange("p (n t) -> p n t", t=128)
            p.tensor_tensor(E0.rearrange("p (n t) -> p n t", t=128), b[:, :, 127:128].to_broadcast([128, 16, 128]),
                            b, ALU.subtract).then_inc(sem("dist"), 1)

            gp.wait_ge(sem("prod"), units_before(N_MIX))
            gp.wait_ge(sem("ld_tab"), 16)
            for w in WP:
                step(p.memset(w[:, :, 0:HIST], 0.0))
            u = zf[:, ZU:ZU + 4]
            step(p.tensor_copy(WP[0][:, :, HIST:HIST + 1], u[:, :, 0:1]))
            step(p.tensor_tensor(WP[0][:, :, HIST + 1:], u[:, :, 1:L], u[:, :, 0:L - 1], ALU.add))
            for n in (1, 2, 3):
                sh = 1 << n
                src, dst = WP[(n - 1) % 2], WP[n % 2]
                a, b = (n - (n - 1) % 2, n - n % 2)
                step(p.tensor_tensor(dst[:, b:, HIST:], src[:, a:, HIST:], src[:, a:, HIST - sh:HIST + L - sh], ALU.add))
            for g in range(4):
                first = WIN[g][:, HIST:HIST + 16]
                ins = p.tensor_tensor(first, first, C("corr", 16 * g, 16 * g + 16), ALU.mult)
                if g < 3:
                    step(ins)
                else:
                    ins.then_inc(sem("win"), 1)
            row = lambda name: A[name].rearrange("o n (r t) a k d -> (o n r) (t a k d)", t=16)
            gather = lambda slot, x, name: p.indirect_dma_start(
                slot, None, row(name), bass.IndirectOffsetOnAxis(idx[:, NS + x:NS + x + 1], 0))
            gp.wait_ge(*done("idx"))
            gp.wait_ge(sem("pd"), 8)
            gp.wait_ge(sem("os_ev"), 2)
            gp.wait_ge(sem("st_out"), 128)
            for x in range(NS + 1):
                if x < NS:
                    if x == 1:
                        gp.wait_ge(sem("qt_mm"), 5)
                    if x >= 2:
                        gp.wait_ge(sem("c_red"), x - 1)
                    gather(Y[x % 2], x, "cache_cmp_kv").then_inc(sem(f"xc{x % 2}"), 16)
                if x:
                    y = x - 1
                    gp.wait_ge(sem(f"xc{y % 2}"), 16 * (y // 2 + 1))
                    if y == 0:
                        gp.wait_ge(sem("pool_mm"), 4)
                        gp.wait_ge(sem("stored"), 48)
                    t = Y[y % 2].rearrange("p (t c) -> p t c", t=16)
                    for n in (8, 4, 2):
                        step(p.tensor_tensor(t[:, 0:n], t[:, 0:n], t[:, n:2 * n], ALU.add))
                    p.tensor_tensor(S16[y], t[:, 0], t[:, 1], ALU.add).then_inc(sem("c_red"), 1)
            gp.wait_ge(sem("on"), 4)
            for x in (1, 2, 3, 0, 4, 5, 6, 7):
                if x == 0:
                    gp.wait_ge(sem("sv_mm"), 4)
                if x == 4:
                    gp.wait_ge(sem("sv_mm"), 8)
                if x > 4:
                    gp.wait_ge(sem("sv_mm"), 8 + x - 4)
                gather(X[SLOT[x]], x, "cache_slc_kv").then_inc(sem(f"xs{SLOT[x]}"), 16)
            gp.wait_ge(sem("sv_mm"), 15)
            with gp.Fori(0, 30) as i:
                for u in range(2):
                    lower(N_MIX + u, i * 2)


NAMES = ["x_prompt", "x_sample", "state_gla", "state_hgrn", "state_pool", "cache_cmp_kv", "cache_slc_kv",
         "cache_win_kv", "gla_wa2", "pool_w", "w_branch", "w_gate", "w_out", "mlp_w1", "mlp_w2"]
OUTS = [("y_prompt", (1, 512, 1024)), ("y_sample", (8, 1, 1024)), ("gla_prompt", (1, 1, 4, 64, 128)),
        ("gla_sample", (1, 8, 4, 64, 128)), ("hgrn_prompt", (1, 1, 4, 64, 128)), ("hgrn_sample", (1, 8, 4, 64, 128)),
        ("pool_prompt", (1, 1, 15, 512)), ("pool_sample", (1, 8, 15, 512)),
        ("cmp_rows_prompt", (1, 1, 512, 2, 2, 64)), ("cmp_rows_sample", (1, 8, 1, 2, 2, 64)),
        ("slc_rows_prompt", (1, 1, 512, 2, 2, 64)), ("slc_rows_sample", (1, 8, 1, 2, 2, 64)),
        ("win_rows_prompt", (1, 1, 512, 2, 2, 64)), ("win_rows_sample", (1, 8, 1, 2, 2, 64))]


def kernel(**inputs):
    import concourse.bacc as bacc
    from concourse.bass_utils import run_bass_kernel_spmd

    a = {k: np.asarray(v) for k, v in inputs.items()}
    arrays = {n: np.ascontiguousarray(a[n]) for n in NAMES}
    w = a["w_in"][0]
    sizes = (256, 256, 512, 512, 16, 256, 256, 512, 512, 512, 512, 128, 128, 128, 128, 128, 128, 24)
    at = np.cumsum((0,) + sizes)
    gq, gk, gv, gr, ga, hq, hf, hi, hg, pu, nq, ck, cv, sk, sv, wk, wv, ng = (
        slice(at[i], at[i + 1]) for i in range(len(sizes)))
    order = (gr, hg, pu, gq, hq, gk, hf, ga, gv, hi, nq, ck, cv, sk, sv, wk, wv, ng)
    arrays["w_in"] = np.ascontiguousarray(np.concatenate([w[:, o] for o in order], 1))
    cols = lambda v, k: v.reshape(k, 128).T
    rows = lambda v: np.broadcast_to(v.reshape(1, -1), (128, v.size))
    arrays["vectors"] = np.ascontiguousarray(np.concatenate([
        cols(a["norm1_g"][0], 8), cols(a["norm2_g"][0], 8), cols(a["b_gate"][0], 32), cols(a["pool_scale"][0], 4),
        cols(a["gla_ba"][0], 2), cols(a["hgrn_lb_param"][0], 2), cols(a["gla_norm_g"][0], 1),
        cols(a["hgrn_norm_g"][0], 1), rows(a["nsa_q_norm_g"][0]), rows(a["nsa_k_norm_g"][0]),
        (np.arange(128) % 8).astype(np.float32)[:, None]], 1))
    arrays["tables"] = constants()[0]
    arrays["pages"] = np.ascontiguousarray(np.repeat(a["page_table"].T, 8, axis=0))

    nc = bacc.Bacc("TRN2", target_bir_lowering=False, num_devices=1)
    A = {n: nc.dram_tensor(n, x.shape, mybir.dt.from_np(x.dtype), kind="ExternalInput").ap()
         for n, x in arrays.items()}
    for n, shape in OUTS:
        A[n] = nc.dram_tensor(n, shape, mybir.dt.float32, kind="ExternalOutput").ap()
    build(nc, A)
    r = run_bass_kernel_spmd(nc, [arrays], core_ids=[0])
    return tuple(r.results[0][n] for n, _ in OUTS)
```
